# Optimizing a Trainium2 kernel written in Bass

```python
import jax, jax.numpy as jnp
from jax import lax
import numpy as np

D_MODEL = 1024
BATCH = 1
SEQ = 512
DEPTH = 1

N_MIXERS = 2
D_RNN = 1280
LRU_BLOCKS = 16
LRU_BLOCK_W = D_RNN // LRU_BLOCKS
CONV_W = 4
LRU_C = 8.0
N_HEADS = 16
N_KV_HEADS = 4
HEAD_DIM = 64
GROUP = N_HEADS // N_KV_HEADS
WINDOW = 128
ATT_BLOCK = WINDOW
Q_DIM = N_HEADS * HEAD_DIM
KV_DIM = N_KV_HEADS * HEAD_DIM
QKV_DIM = Q_DIM + 2 * KV_DIM
N_GROUPS = 4
EXPERTS_PER_GROUP = 8
N_EXPERTS = N_GROUPS * EXPERTS_PER_GROUP
TOP_K = 2
D_EXPERT = 512
MOE_BLOCK = 128
ALPHA = (2 * DEPTH) ** 0.25
BETA = (8 * DEPTH) ** -0.25
LN_EPS = 1e-5
N_REC_LAYERS = (DEPTH + N_MIXERS - 1) // N_MIXERS
N_ATT_LAYERS = DEPTH // N_MIXERS


def layer_norm(x, g, b):
    xf = x.astype(jnp.float32)
    mu = jnp.mean(xf, axis=-1, keepdims=True)
    xc = xf - mu
    var = jnp.mean(xc * xc, axis=-1, keepdims=True)
    y = xc * lax.rsqrt(var + LN_EPS) * g.astype(jnp.float32) + b.astype(jnp.float32)
    return y.astype(x.dtype)

def _linear_recurrence_combine(c1, c2):
    a1, b1 = c1
    a2, b2 = c2
    return a1 * a2, a2 * b1 + b2

def rglru_block(x, w_in, conv_w, conv_b, w_r, b_r, w_i, b_i, lam, w_out):
    B, S, _ = x.shape
    gate, xr = jnp.split(x @ w_in, 2, axis=-1)
    xp = jnp.pad(xr, ((0, 0), (CONV_W - 1, 0), (0, 0)))
    xc = conv_b + sum(xp[:, k:k + S] * conv_w[k] for k in range(CONV_W))
    xb = xc.reshape(B, S, LRU_BLOCKS, LRU_BLOCK_W)
    r = jax.nn.sigmoid(jnp.einsum('bsnk,nkj->bsnj', xb, w_r).reshape(B, S, D_RNN) + b_r)
    i = jax.nn.sigmoid(jnp.einsum('bsnk,nkj->bsnj', xb, w_i).reshape(B, S, D_RNN) + b_i)
    log_a = -LRU_C * r.astype(jnp.float32) * jax.nn.softplus(-lam.astype(jnp.float32))
    a = jnp.exp(log_a)
    u = jnp.sqrt(-jnp.expm1(2.0 * log_a)) * (i * xc).astype(jnp.float32)
    _, h = lax.associative_scan(_linear_recurrence_combine, (a, u), axis=1)
    y = h.astype(x.dtype) * jax.nn.gelu(gate)
    return y @ w_out

def alibi_slopes():
    return 2.0 ** (-8.0 * jnp.arange(1, N_HEADS + 1, dtype=jnp.float32) / N_HEADS)

def _with_prev_block(t):
    prev = jnp.concatenate([jnp.zeros_like(t[:, :1]), t[:, :-1]], axis=1)
    return jnp.concatenate([prev, t], axis=2)

def swa_sink_alibi(x, w_qkv, sinks, w_o):
    B, S, _ = x.shape
    NB = S // ATT_BLOCK
    qkv = x @ w_qkv
    q = qkv[..., :Q_DIM].reshape(B, NB, ATT_BLOCK, N_KV_HEADS, GROUP, HEAD_DIM) * (HEAD_DIM ** -0.5)
    k = qkv[..., Q_DIM:Q_DIM + KV_DIM].reshape(B, NB, ATT_BLOCK, N_KV_HEADS, HEAD_DIM)
    v = qkv[..., Q_DIM + KV_DIM:].reshape(B, NB, ATT_BLOCK, N_KV_HEADS, HEAD_DIM)
    kk = _with_prev_block(k)
    vv = _with_prev_block(v)
    s = jnp.einsum('bnqkgd,bnskd->bnkgqs', q, kk).astype(jnp.float32)
    qi = jnp.arange(ATT_BLOCK)[:, None]
    sj = jnp.arange(2 * ATT_BLOCK)[None, :]
    dist = qi - sj + ATT_BLOCK
    valid = (dist >= 0) & (dist < WINDOW)
    not_before_start = (jnp.arange(NB)[:, None, None] > 0) | (sj[None] >= ATT_BLOCK)
    mask = valid[None] & not_before_start
    slopes = alibi_slopes().reshape(N_KV_HEADS, GROUP)
    s = s - slopes[:, :, None, None] * dist.astype(jnp.float32)
    s = jnp.where(mask[None, :, None, None], s, -jnp.inf)
    sink = sinks.astype(jnp.float32).reshape(N_KV_HEADS, GROUP)[None, None, :, :, None, None]
    m = jnp.maximum(jnp.max(s, axis=-1, keepdims=True), sink)
    p = jnp.exp(s - m)
    denom = jnp.sum(p, axis=-1, keepdims=True) + jnp.exp(sink - m)
    o = jnp.einsum('bnkgqs,bnskd->bnqkgd', (p / denom).astype(x.dtype), vv)
    return o.reshape(B, S, Q_DIM) @ w_o

def hier_moe(x, w_rg, b_rg, w_re, b_re, w1, w3, w2):
    B, S, D = x.shape
    T = B * S
    TK = T * TOP_K
    xf = x.reshape(T, D)
    g_logits = (xf @ w_rg + b_rg).astype(jnp.float32)
    g_idx = jnp.argmax(g_logits, axis=-1)
    g_gate = jnp.take_along_axis(jax.nn.softmax(g_logits, axis=-1), g_idx[:, None], axis=1)
    e_logits = (xf @ w_re + b_re).astype(jnp.float32).reshape(T, N_GROUPS, EXPERTS_PER_GROUP)
    e_in_group = jnp.take_along_axis(e_logits, g_idx[:, None, None], axis=1)[:, 0]
    top_v, top_i = lax.top_k(e_in_group, TOP_K)
    gates = jax.nn.softmax(top_v, axis=-1) * g_gate
    expert = g_idx[:, None] * EXPERTS_PER_GROUP + top_i
    flat_e = expert.reshape(TK)
    order = jnp.argsort(flat_e)
    sorted_e = flat_e[order]
    counts = jnp.bincount(flat_e, length=N_EXPERTS)
    padded = ((counts + MOE_BLOCK - 1) // MOE_BLOCK) * MOE_BLOCK
    starts = jnp.cumsum(counts) - counts
    pends = jnp.cumsum(padded)
    pstarts = pends - padded
    dest = pstarts[sorted_e] + (jnp.arange(TK) - starts[sorted_e])
    slot_dest = jnp.zeros_like(dest).at[order].set(dest)
    n_blocks = -(-(TK + N_EXPERTS * (MOE_BLOCK - 1)) // MOE_BLOCK)
    n_rows = n_blocks * MOE_BLOCK
    xbuf = jnp.zeros((n_rows, D), x.dtype).at[slot_dest].set(jnp.repeat(xf, TOP_K, axis=0))
    block_start = jnp.arange(n_blocks) * MOE_BLOCK
    block_e = jnp.minimum(jnp.sum(block_start[:, None] >= pends[None, :], axis=1), N_EXPERTS - 1)

    def expert_block(args):
        xb, e = args
        hdn = jax.nn.silu(xb @ w1[e]) * (xb @ w3[e])
        return hdn @ w2[e]

    ybuf = lax.map(expert_block, (xbuf.reshape(n_blocks, MOE_BLOCK, D), block_e)).reshape(n_rows, D)
    y_slots = ybuf[slot_dest].reshape(T, TOP_K, D)
    out = jnp.einsum('tk,tkd->td', gates.astype(x.dtype), y_slots)
    return out.reshape(B, S, D)

def first_inputs(seed: int = 0) -> dict:
    key = jax.random.key(seed)
    ks = jax.random.split(key, 24)

    def nrm(k, shape, scale):
        return jax.random.normal(k, shape, jnp.float32) * scale

    x = nrm(ks[0], (BATCH, SEQ, D_MODEL), 1.0)
    rec_w_in = nrm(ks[1], (N_REC_LAYERS, D_MODEL, 2 * D_RNN), D_MODEL ** -0.5)
    rec_conv_w = nrm(ks[2], (N_REC_LAYERS, CONV_W, D_RNN), CONV_W ** -0.5)
    rec_conv_b = nrm(ks[3], (N_REC_LAYERS, D_RNN), 0.01)
    rec_w_r = nrm(ks[4], (N_REC_LAYERS, LRU_BLOCKS, LRU_BLOCK_W, LRU_BLOCK_W), LRU_BLOCK_W ** -0.5)
    rec_b_r = nrm(ks[5], (N_REC_LAYERS, D_RNN), 0.01)
    rec_w_i = nrm(ks[6], (N_REC_LAYERS, LRU_BLOCKS, LRU_BLOCK_W, LRU_BLOCK_W), LRU_BLOCK_W ** -0.5)
    rec_b_i = nrm(ks[7], (N_REC_LAYERS, D_RNN), 0.01)
    a_c = jax.random.uniform(ks[8], (N_REC_LAYERS, D_RNN), jnp.float32, minval=0.9, maxval=0.999)
    a0 = a_c ** (1.0 / LRU_C)
    rec_lambda = jnp.log(a0) - jnp.log1p(-a0)
    rec_w_out = nrm(ks[9], (N_REC_LAYERS, D_RNN, D_MODEL), BETA * D_RNN ** -0.5)
    col_scale = jnp.concatenate([jnp.ones((Q_DIM + KV_DIM,), jnp.float32), jnp.full((KV_DIM,), BETA, jnp.float32)])
    att_w_qkv = nrm(ks[10], (N_ATT_LAYERS, D_MODEL, QKV_DIM), D_MODEL ** -0.5) * col_scale
    att_sinks = nrm(ks[11], (N_ATT_LAYERS, N_HEADS), 0.5)
    att_w_o = nrm(ks[12], (N_ATT_LAYERS, Q_DIM, D_MODEL), BETA * Q_DIM ** -0.5)
    moe_w_group = nrm(ks[13], (DEPTH, D_MODEL, N_GROUPS), D_MODEL ** -0.5)
    moe_b_group = nrm(ks[14], (DEPTH, N_GROUPS), 0.01)
    moe_w_expert = nrm(ks[15], (DEPTH, D_MODEL, N_EXPERTS), D_MODEL ** -0.5)
    moe_b_expert = nrm(ks[16], (DEPTH, N_EXPERTS), 0.01)
    moe_w1 = nrm(ks[17], (DEPTH, N_EXPERTS, D_MODEL, D_EXPERT), D_MODEL ** -0.5)
    moe_w3 = nrm(ks[18], (DEPTH, N_EXPERTS, D_MODEL, D_EXPERT), D_MODEL ** -0.5)
    moe_w2 = nrm(ks[19], (DEPTH, N_EXPERTS, D_EXPERT, D_MODEL), BETA * D_EXPERT ** -0.5)
    ln_g = 1.0 + nrm(ks[20], (DEPTH, 2, D_MODEL), 0.02)
    ln_b = nrm(ks[21], (DEPTH, 2, D_MODEL), 0.02)
    return {'x': x, 'rec_w_in': rec_w_in, 'rec_conv_w': rec_conv_w, 'rec_conv_b': rec_conv_b,
            'rec_w_r': rec_w_r, 'rec_b_r': rec_b_r, 'rec_w_i': rec_w_i, 'rec_b_i': rec_b_i,
            'rec_lambda': rec_lambda, 'rec_w_out': rec_w_out, 'att_w_qkv': att_w_qkv,
            'att_sinks': att_sinks, 'att_w_o': att_w_o, 'moe_w_group': moe_w_group,
            'moe_b_group': moe_b_group, 'moe_w_expert': moe_w_expert, 'moe_b_expert': moe_b_expert,
            'moe_w1': moe_w1, 'moe_w3': moe_w3, 'moe_w2': moe_w2, 'ln_g': ln_g, 'ln_b': ln_b}

def first_block(x, rec_w_in, rec_conv_w, rec_conv_b, rec_w_r, rec_b_r, rec_w_i, rec_b_i, rec_lambda,
              rec_w_out, att_w_qkv, att_sinks, att_w_o, moe_w_group, moe_b_group, moe_w_expert,
              moe_b_expert, moe_w1, moe_w3, moe_w2, ln_g, ln_b):
    for layer in range(DEPTH):
        j = layer // N_MIXERS
        if layer % N_MIXERS == 0:
            h = rglru_block(x, rec_w_in[j], rec_conv_w[j], rec_conv_b[j], rec_w_r[j], rec_b_r[j],
                            rec_w_i[j], rec_b_i[j], rec_lambda[j], rec_w_out[j])
        else:
            h = swa_sink_alibi(x, att_w_qkv[j], att_sinks[j], att_w_o[j])
        x = layer_norm(ALPHA * x + h, ln_g[layer, 0], ln_b[layer, 0])
        f = hier_moe(x, moe_w_group[layer], moe_b_group[layer], moe_w_expert[layer], moe_b_expert[layer],
                     moe_w1[layer], moe_w3[layer], moe_w2[layer])
        x = layer_norm(ALPHA * x + f, ln_g[layer, 1], ln_b[layer, 1])
    return x


DEPTH_2 = 2

FOURIER_WIDTH = 512
FOURIER_GROUP = FOURIER_WIDTH // N_GROUPS
CONV_WIDTH = 512
CONV_K = 3
POOL_WIDTH = 512
POOL_GROUP = POOL_WIDTH // N_GROUPS
POOL_WINDOWS = (2, 4, 8, 16)
OUT_GROUP = D_MODEL // N_GROUPS
N_BRANCHES = 3
D_FF = 2816
EPS = 1e-6

OFF_F = 0
OFF_B = OFF_F + FOURIER_WIDTH
OFF_C = OFF_B + CONV_WIDTH
OFF_V = OFF_C + CONV_WIDTH
OFF_P = OFF_V + CONV_WIDTH
OFF_G = OFF_P + POOL_WIDTH
IN_WIDTH = OFF_G + N_BRANCHES * D_MODEL


def rmsnorm(x, g):
    xf = x.astype(jnp.float32)
    y = xf * lax.rsqrt(jnp.mean(xf * xf, axis=-1, keepdims=True) + EPS)
    return (y * g.astype(jnp.float32)).astype(x.dtype)

def swiglu(h, w1, w3, w2):
    return (jax.nn.silu(h @ w1) * (h @ w3)) @ w2

def fourier_mix(u, w_map):
    b, s, _ = u.shape
    ug = u.reshape(b, s, N_GROUPS, FOURIER_GROUP).astype(jnp.float32)
    f = jnp.fft.fftn(ug, axes=(1, 3), norm="ortho").real.astype(u.dtype)
    y = jnp.einsum("bsgc,gcd->bsgd", f, w_map)
    return y.reshape(b, s, D_MODEL)

def short_conv(bg, cg, v, w_conv, w_out):
    z = cg * v
    zp = jnp.pad(z, ((0, 0), (1, 1), (0, 0)))
    conv = w_conv[0] * zp[:, :-2] + w_conv[1] * zp[:, 1:-1] + w_conv[2] * zp[:, 2:]
    return (bg * conv) @ w_out

def pool_mix(u, w_map, scale):
    s = u.shape[1]
    t = jnp.arange(s, dtype=jnp.float32)
    outs = []
    for i, w in enumerate(POOL_WINDOWS):
        half = w // 2
        ug = u[..., i * POOL_GROUP:(i + 1) * POOL_GROUP].astype(jnp.float32)
        cs = jnp.pad(jnp.cumsum(ug, axis=1), ((0, 0), (1, 0), (0, 0)))
        padded = jnp.pad(cs, ((0, 0), (half, half), (0, 0)), mode="edge")
        win = padded[:, w:w + s] - padded[:, :s]
        count = jnp.minimum(t + half, float(s)) - jnp.maximum(t - half, 0.0)
        pooled = win / count[None, :, None] - ug
        outs.append(pooled.astype(u.dtype) @ w_map[i])
    return jnp.concatenate(outs, axis=-1) * scale

def second_inputs(seed: int = 0) -> dict:
    key = jax.random.key(seed)
    ks = jax.random.split(key, 20)
    f32 = jnp.float32

    def nrm(k, shape, fan_in):
        return jax.random.normal(k, shape, f32) * (fan_in ** -0.5)

    def gain(k, shape):
        return 1.0 + 0.02 * jax.random.normal(k, shape, f32)

    L, D = DEPTH_2, D_MODEL
    return {
        "x": jax.random.normal(ks[0], (BATCH, SEQ, D), f32),
        "g_ffn1": gain(ks[1], (L, D)),
        "w1_a": nrm(ks[2], (L, D, D_FF), D),
        "w3_a": nrm(ks[3], (L, D, D_FF), D),
        "w2_a": nrm(ks[4], (L, D_FF, D), D_FF),
        "g_mix": gain(ks[5], (L, D)),
        "w_in": nrm(ks[6], (L, D, IN_WIDTH), D),
        "w_fourier": nrm(ks[7], (L, N_GROUPS, FOURIER_GROUP, OUT_GROUP), FOURIER_GROUP),
        "w_conv": nrm(ks[8], (L, CONV_K, CONV_WIDTH), CONV_K),
        "w_conv_out": nrm(ks[9], (L, CONV_WIDTH, D), CONV_WIDTH),
        "w_pool": nrm(ks[10], (L, N_GROUPS, POOL_GROUP, OUT_GROUP), POOL_GROUP),
        "pool_scale": gain(ks[11], (L, D)),
        "w_o": nrm(ks[12], (L, D, D), D),
        "g_ffn2": gain(ks[13], (L, D)),
        "w1_b": nrm(ks[14], (L, D, D_FF), D),
        "w3_b": nrm(ks[15], (L, D, D_FF), D),
        "w2_b": nrm(ks[16], (L, D_FF, D), D_FF),
        "g_final": gain(ks[17], (D,)),
    }

def second_block(x, g_ffn1, w1_a, w3_a, w2_a, g_mix, w_in, w_fourier, w_conv, w_conv_out,
              w_pool, pool_scale, w_o, g_ffn2, w1_b, w3_b, w2_b, g_final):
    b, s, d = x.shape
    for l in range(DEPTH_2):
        h = rmsnorm(x, g_ffn1[l])
        x = x + 0.5 * swiglu(h, w1_a[l], w3_a[l], w2_a[l])

        h = rmsnorm(x, g_mix[l])
        p = h @ w_in[l]
        gates = jax.nn.sigmoid(p[..., OFF_G:].astype(jnp.float32)).astype(x.dtype)
        gates = gates.reshape(b, s, N_BRANCHES, d)
        y_f = fourier_mix(p[..., OFF_F:OFF_B], w_fourier[l])
        y_c = short_conv(p[..., OFF_B:OFF_C], p[..., OFF_C:OFF_V], p[..., OFF_V:OFF_P],
                         w_conv[l], w_conv_out[l])
        y_p = pool_mix(p[..., OFF_P:OFF_G], w_pool[l], pool_scale[l])
        merged = gates[:, :, 0] * y_f + gates[:, :, 1] * y_c + gates[:, :, 2] * y_p
        x = x + merged @ w_o[l]

        h = rmsnorm(x, g_ffn2[l])
        x = x + 0.5 * swiglu(h, w1_b[l], w3_b[l], w2_b[l])
    return rmsnorm(x, g_final)


def setup_inputs(seed=0):
    out = dict(first_inputs(seed))
    for name, value in second_inputs(seed + 1).items():
        if name != "x":
            out[name + "_2"] = value
    return out


def reference(
    x, rec_w_in, rec_conv_w, rec_conv_b, rec_w_r, rec_b_r, rec_w_i, rec_b_i, rec_lambda,
    rec_w_out, att_w_qkv, att_sinks, att_w_o, moe_w_group, moe_b_group, moe_w_expert,
    moe_b_expert, moe_w1, moe_w3, moe_w2, ln_g, ln_b, g_ffn1_2, w1_a_2, w3_a_2, w2_a_2, g_mix_2,
    w_in_2, w_fourier_2, w_conv_2, w_conv_out_2, w_pool_2, pool_scale_2, w_o_2, g_ffn2_2,
    w1_b_2, w3_b_2, w2_b_2, g_final_2,
):
    x = first_block(
        x, rec_w_in, rec_conv_w, rec_conv_b, rec_w_r, rec_b_r, rec_w_i, rec_b_i, rec_lambda,
        rec_w_out, att_w_qkv, att_sinks, att_w_o, moe_w_group, moe_b_group, moe_w_expert,
        moe_b_expert, moe_w1, moe_w3, moe_w2, ln_g, ln_b,
    )
    return second_block(
        x, g_ffn1_2, w1_a_2, w3_a_2, w2_a_2, g_mix_2, w_in_2, w_fourier_2, w_conv_2,
        w_conv_out_2, w_pool_2, pool_scale_2, w_o_2, g_ffn2_2, w1_b_2, w3_b_2, w2_b_2,
        g_final_2,
    )


_drawn_inputs = setup_inputs


def setup_inputs(seed=0):
    import zlib

    import numpy as np

    out = dict(_drawn_inputs(seed))
    spreads = {}
    factors = {'rec_b_r': 25.311,
     'rec_b_i': 22.874,
     'moe_b_group': 5.355,
     'moe_b_expert': 4.321,
     'g_ffn1_2': 4.136,
     'pool_scale_2': 22.042,
     'g_ffn2_2': 34.131,
     'g_final_2': 22.911,
     'g_mix_2': 3.591}
    for name, (base, spread) in spreads.items():
        noise = np.random.default_rng([zlib.crc32(name.encode()), seed]).standard_normal(out[name].shape)
        drawn = base * np.exp(spread * noise) if base else spread * noise
        out[name] = __import__('jax').numpy.asarray(drawn.astype(out[name].dtype))
    for name, factor in factors.items():
        out[name] = (out[name] * factor).astype(out[name].dtype)
    return out
```

```python
from contextlib import ExitStack

import concourse.bass as bass
from concourse import mybir

F32 = mybir.dt.float32
F32R = mybir.dt.float32r
U32 = mybir.dt.uint32
ALU = mybir.AluOpType
ACT = mybir.ActivationFunctionType
AX_X = mybir.AxisListType.X

P = 128
T = 512
D = 1024
TT = T // P
DT = D // P
R = 1280
RT = R // P
LRU_BLOCKS = 16
LRU_W = R // LRU_BLOCKS
CONV_W = 4
NG = 4
EPG = 8
NE = NG * EPG
FE = 512
FET = FE // P
FF = 2816
FFT = FF // P
LAYERS = 2
ALPHA = 2.0 ** 0.25
LN_EPS = 1e-5
RMS_EPS = 1e-6
W = 1024
EXTRA = (2 * T - NE) // P
NBLK = NE + EXTRA
BIG = 1e30

IN_F, IN_B, IN_C, IN_V, IN_P, IN_G = 0, 4, 8, 12, 16, 20
IN_TILES = 44

BD_PAIRS = [(i, j) for j in range(RT) for i in range(RT)
            if any(n * LRU_W < (i + 1) * P and (n + 1) * LRU_W > i * P
                   and n * LRU_W < (j + 1) * P and (n + 1) * LRU_W > j * P for n in range(LRU_BLOCKS))]

PARAM_GROUPS = [("conv_w", CONV_W * RT), ("conv_b", RT), ("b_r", RT), ("b_i", RT), ("lam", RT),
                ("g_ffn1", LAYERS * DT), ("g_mix", LAYERS * DT), ("g_ffn2", LAYERS * DT),
                ("pool_scale", LAYERS * DT), ("g_final", DT), ("w_conv", LAYERS * 3 * 4)]
PCOL = {}
NPAR = 0
for _name, _n in PARAM_GROUPS:
    PCOL[_name] = NPAR
    NPAR += _n

C_IDENT = 0
C_UPPER = C_IDENT + P
C_IOTA = C_UPPER + P
C_GRANK = C_IOTA + P
C_ERANK = C_GRANK + TT * NG
C_EIDX = C_ERANK + TT * NE
C_SLOT = C_EIDX + TT * NE
C_ROW4 = C_SLOT + 2 * TT
NCONST = C_ROW4 + 1


class Queue:

    def __init__(self, sem, eng=None):
        self.sem = sem
        self.eng = eng
        self.done = 0
        self.seen = {}

    def wait(self, *tokens):
        for token in tokens:
            if token is not None and self.eng is not None:
                sem, value = token
                if self.seen.get(id(sem), 0) < value:
                    self.eng.wait_ge(sem, value)
                    self.seen[id(sem)] = value

    def run(self, fn, *tokens):
        self.wait(*tokens)
        if self.eng is not None:
            fn(self.eng).then_inc(self.sem, 1)
        self.done += 1
        return (self.sem, self.done)

    def issue(self, fn, *tokens):
        self.wait(*tokens)
        if self.eng is not None:
            fn(self.eng)

    def here(self):
        return (self.sem, self.done) if self.done else None


def build(nc, io):
    with ExitStack() as ctx:
        def sb(name, shape, dt=F32, into=None):
            return (into or ctx).enter_context(nc.sbuf_tensor(name, shape, dt))

        def sem(name):
            return ctx.enter_context(nc.semaphore(name))

        s_pe, s_act, s_dve, s_pool = (sem(n) for n in ("s_pe", "s_act", "s_dve", "s_pool"))
        o_pe, o_act, o_dve, o_pool = (sem(n) for n in ("o_pe", "o_act", "o_dve", "o_pool"))
        NRAW, NSPLIT = 5, 3
        s_raw = [sem(f"s_raw{i}") for i in range(NRAW)]
        s_par, s_x, s_bd, s_xt, s_router, s_x1, s_out = (
            sem(n) for n in ("s_par", "s_x", "s_bd", "s_xt", "s_router", "s_x1", "s_out"))
        s_gb = [sem(f"s_gb{i}") for i in range(4)]
        s_gather = [sem(f"s_gather{i}") for i in range(3)]
        s_scatter = [sem(f"s_scatter{i}") for i in range(3)]
        s_ys = [sem(f"s_ys{i}") for i in range(4)]
        o_weight, o_rows, o_store = sem("o_weight"), sem("o_rows"), sem("o_store")

        bank = [ctx.enter_context(nc.psum_tensor(f"bank{i}", [P, 512], F32)) for i in range(8)]
        raw = sb("raw", [P, NRAW, W])
        w_hi = sb("w_hi", [P, NSPLIT, W], F32R)
        w_lo = sb("w_lo", [P, NSPLIT, W], F32R)
        params = sb("params", [P, NPAR])
        consts = sb("consts", [P, NCONST])
        ones = sb("ones", [P, P])

        with ExitStack() as first:
            x_tok = sb("x_tok", [P, TT, D], into=first)
            with ExitStack() as rec:
                x_hi = sb("x_hi", [P, RT, T], F32R, rec)
                x_lo = sb("x_lo", [P, RT, T], F32R, rec)
                gate = sb("gate", [P, 2, T], into=rec)
                xc = sb("xc", [P, RT, T], into=rec)
                hs = sb("hs", [P, RT, T], into=rec)
                bd = sb("bd", [P, 2 * len(BD_PAIRS), P], into=rec)
                xrp = sb("xrp", [P, 2, T + CONV_W - 1], into=rec)
                rg = sb("rg", [P, 2, T], into=rec)
                ig = sb("ig", [P, 2, T], into=rec)
                th = sb("th", [P, 2, T], into=rec)
                av = sb("av", [P, 2, T], into=rec)
                mv = sb("mv", [P, 2, T], into=rec)
                lamw = sb("lamw", [P, 8, RT], into=rec)
            with ExitStack() as moe:
                lnz = sb("lnz", [P, 2, D], into=moe)
                gb = sb("gb", [P, 4, D], into=moe)
                st = sb("st", [P, TT, 24], into=moe)
                x1T = sb("x1T", [P, DT, T], into=moe)
                wr = sb("wr", [P, DT, NG + NE], into=moe)
                br = sb("br", [1, NG + NE], into=moe)
                lg = sb("lg", [P, TT, NG + NE], into=moe)
                rt = sb("rt", [P, 16, TT, NE], into=moe)
                sm = sb("sm", [P, 32, TT], into=moe)
                oneh = sb("oneh", [P, 2 * TT, P], into=moe)
                blkh = sb("blkh", [P, 2 * TT, NBLK], into=moe)
                tabs = sb("tabs", [P, 4, NBLK], into=moe)
                gidx = sb("gidx", [P, NBLK], U32, moe)
                sidx = sb("sidx", [P, NBLK], U32, moe)
                wix = sb("wix", [P, EXTRA, 4], into=moe)
                widx = sb("widx", [P, EXTRA, 4], U32, moe)
                cnt = sb("cnt", [P, 1], U32, moe)
                xe = sb("xe", [P, 3, D], into=moe)
                xeT_hi = sb("xeT_hi", [P, 2, D], F32R, moe)
                xeT_lo = sb("xeT_lo", [P, 2, D], F32R, moe)
                sil = sb("sil", [P, 2, FE], into=moe)
                hd = sb("hd", [P, 2, FE], into=moe)
                hT_hi = sb("hT_hi", [P, 2, FE], F32R, moe)
                hT_lo = sb("hT_lo", [P, 2, FE], F32R, moe)
                ye = sb("ye", [P, 3, D], into=moe)
                o_raw = sb("o_raw", [P, W], into=moe)
                o_hi = sb("o_hi", [P, W], F32R, moe)
                o_lo = sb("o_lo", [P, W], F32R, moe)
                ysl = x1T[:, :, :].rearrange("p a t -> p (a t)").rearrange("p (s d) -> p s d", d=D)
        g_hi = sb("g_hi", [P, FFT, T], F32R)
        g_lo = sb("g_lo", [P, FFT, T], F32R)
        xT = sb("xT", [P, DT, T])
        xg_hi = sb("xg_hi", [P, DT, T], F32R)
        xg_lo = sb("xg_lo", [P, DT, T], F32R)
        tmp = sb("tmp", [P, 8, T])
        rsq = sb("rsq", [P, T])
        zc = sb("zc", [P, 2, T + 16])

        x1_dram = nc.dram_tensor("x1_rows", (T, D), F32, kind="Internal").ap()
        ys_dram = nc.dram_tensor("y_rows", (2 * T, D), F32, kind="Internal").ap()

        ident = consts[:, C_IDENT:C_IDENT + P]
        upper = consts[:, C_UPPER:C_UPPER + P]
        iota = consts[:, C_IOTA:C_IOTA + P]

        def par(name, k=0):
            c = PCOL[name] + k
            return params[:, c:c + 1]

        def program(known, walk=None, eng=None):
            chunks = []
            PE, AC, VE, PO, SP = (Queue(q, eng if walk == n else None) for n, q in
                                  (("pe", s_pe), ("act", s_act), ("dve", s_dve), ("pool", s_pool), ("sp", None)))

            split = []
            used = []
            landed = [0] * NRAW
            LOOK = NSPLIT - 1

            def load(c):
                parts = known[c]
                if c >= NRAW:
                    SP.wait(split[c - NRAW])
                for col, src, width in parts:
                    SP.issue(lambda e, c=c, col=col, src=src, width=width:
                             e.dma_start(raw[:, c % NRAW, col:col + width], src).then_inc(s_raw[c % NRAW], 16))

            def convert(c):
                if c < NRAW:
                    load(c)
                parts = known[c]
                n = parts[-1][0] + parts[-1][2]
                landed[c % NRAW] += 16 * len(parts)
                free = used[c - NSPLIT] if c >= NSPLIT else None
                hi = w_hi[:, c % NSPLIT, 0:n]
                lo = w_lo[:, c % NSPLIT, 0:n]
                src = raw[:, c % NRAW, 0:n]
                high = AC.run(lambda e: e.activation(hi, src, ACT.Copy),
                              (s_raw[c % NRAW], landed[c % NRAW]), free)
                on = PO if c % POOL_EVERY == POOL_EVERY - 1 else VE
                split.append(on.run(lambda e: e.tensor_tensor(lo, src, hi.bitcast(F32), ALU.subtract), high, free))
                if c + NRAW < len(known):
                    load(c + NRAW)

            def take(*parts):
                c = len(chunks)
                chunks.append(parts)
                if known is not None:
                    while len(split) < min(c + LOOK + 1, len(known)):
                        convert(len(split))
                    PE.wait(split[c])
                return c, w_hi[:, c % NSPLIT, :], w_lo[:, c % NSPLIT, :]

            def release(c, token):
                used.append(token)

            RING = 7
            bank_free = [None] * 8
            turn = [0]

            def get_bank():
                b = turn[0] % RING
                turn[0] += 1
                PE.wait(bank_free[b])
                return b

            def mm3(out, a_hi, a_lo, b_hi, b_lo, start, stop):
                PE.issue(lambda e: e.matmul(out, a_lo, b_hi, start=start, stop=False))
                PE.issue(lambda e: e.matmul(out, a_hi, b_lo, start=False, stop=False))
                last = lambda e: e.matmul(out, a_hi, b_hi, start=False, stop=stop)
                return last

            later = []

            def run_later():
                todo, later[:] = list(later), []
                for fn in todo:
                    fn()

            SP.issue(lambda e: e.dma_start(hs[:, 0:DT, :], io["xT"]).then_inc(s_xt, 16))
            AC.issue(lambda e: e.dma_start(params[:, :], io["params"]).then_inc(s_par, 16))
            AC.issue(lambda e: e.dma_start(consts[:, :], io["consts"]).then_inc(s_par, 16))
            AC.issue(lambda e: e.dma_start(bd[:, :, :], io["bd"]).then_inc(s_bd, 16))
            AC.issue(lambda e: e.dma_start(x_tok[:, :, :], io["x"]).then_inc(s_x, 16))
            par_in, bd_in, x_in, xt_in = (s_par, 32), (s_bd, 16), (s_x, 16), (s_xt, 16)
            pad_ready = VE.run(lambda e: e.memset(xrp[:, :, 0:CONV_W - 1], 0.0))
            ones_ready = VE.run(lambda e: e.memset(ones[:, :], 1.0))

            x_split = []
            for k in range(DT):
                a = AC.run(lambda e, k=k: e.activation(x_hi[:, k, :], hs[:, k, :], ACT.Copy), xt_in)
                x_split.append(VE.run(lambda e, k=k: e.tensor_tensor(
                    x_lo[:, k, :], hs[:, k, :], x_hi[:, k, :].bitcast(F32), ALU.subtract), a, xt_in))

            lam = params[:, PCOL["lam"]:PCOL["lam"] + RT]
            L = [lamw[:, i, :] for i in range(8)]
            t = AC.run(lambda e: e.activation(L[0], lam, ACT.Abs), par_in)
            t = AC.run(lambda e: e.activation(L[1], L[0], ACT.Exp, scale=-1.0), t)
            t = VE.run(lambda e: e.tensor_scalar(L[2], L[1], 2.0, None, ALU.add), t)
            t = VE.run(lambda e: e.reciprocal(L[3], L[2]), t)
            t = VE.run(lambda e: e.tensor_tensor(L[2], L[1], L[3], ALU.mult), t)
            t = VE.run(lambda e: e.tensor_tensor(L[3], L[2], L[2], ALU.mult), t)
            t = VE.run(lambda e: e.tensor_scalar(L[4], L[3], 1.0 / 17, 1.0 / 15, ALU.mult, ALU.add), t)
            for n in (13, 11, 9, 7, 5, 3, 1):
                t = VE.run(lambda e: e.tensor_tensor(L[5], L[4], L[3], ALU.mult), t)
                t = VE.run(lambda e, n=n: e.tensor_scalar(L[4], L[5], 1.0 / n, None, ALU.add), t)
            t = VE.run(lambda e: e.tensor_tensor(L[5], L[4], L[2], ALU.mult), t)
            t = VE.run(lambda e: e.tensor_scalar(L[6], lam, -1.0, 0.0, ALU.mult, ALU.max), t, par_in)
            t = VE.run(lambda e: e.tensor_scalar(L[6], L[6], 4.0, None, ALU.mult), t)
            c4_ready = VE.run(lambda e: e.scalar_tensor_tensor(L[7], L[5], 8.0, L[6], ALU.mult, ALU.add), t)
            c4 = L[7]

            def in_tile(j):
                c, hi, lo = take((0, io["rec_in"][j], W))
                b = get_bank()
                for k in range(DT):
                    if j == 0:
                        PE.wait(x_split[k])
                    f = mm3(bank[b][:, :], hi[:, k * P:(k + 1) * P], lo[:, k * P:(k + 1) * P],
                            x_hi[:, k, :], x_lo[:, k, :], k == 0, k == DT - 1)
                    if k < DT - 1:
                        PE.issue(f)
                token = PE.run(f)
                release(c, token)
                return b, token

            xc_ready = [None] * RT
            gates_read = [None] * RT

            def conv(j, b, token):
                copied = AC.run(lambda e: e.activation(xrp[:, j % 2, CONV_W - 1:], bank[b][:, :], ACT.Copy),
                                token, pad_ready, xc_ready[j - 2] if j >= 2 else None)
                bank_free[b] = copied
                t = VE.run(lambda e: e.tensor_scalar(xc[:, j, :], xrp[:, j % 2, 0:T], par("conv_w", j),
                                                     par("conv_b", j), ALU.mult, ALU.add), copied, par_in)
                for k in range(1, CONV_W):
                    t = VE.run(lambda e, k=k: e.scalar_tensor_tensor(
                        xc[:, j, :], xrp[:, j % 2, k:k + T], par("conv_w", k * RT + j), xc[:, j, :],
                        ALU.mult, ALU.add), t)
                xc_ready[j] = t

            h_ready = [None] * RT
            rg_read, ig_read, th_read, av_read, mv_read = ([None] * RT for _ in range(5))

            def recur(j):
                s = j % 2
                old = j - 2 if j >= 2 else None
                past = lambda lst: lst[old] if old is not None else None
                PE.wait(bd_in)
                banks = []
                for m in range(2):
                    b = get_bank()
                    pairs = [n for n, (_, jj) in enumerate(BD_PAIRS) if jj == j]
                    for n in pairs:
                        i = BD_PAIRS[n][0]
                        PE.wait(xc_ready[i])
                        f = lambda e, n=n, i=i, b=b, m=m, pairs=pairs: e.matmul(
                            bank[b][:, :], bd[:, m * len(BD_PAIRS) + n, :], xc[:, i, :],
                            start=n == pairs[0], stop=n == pairs[-1])
                        if n != pairs[-1]:
                            PE.issue(f)
                    banks.append((b, PE.run(f)))
                (b_r, r_done), (b_i, i_done) = banks
                r_ok = AC.run(lambda e: e.activation(rg[:, s, :], bank[b_r][:, :], ACT.Sigmoid,
                                                     bias=par("b_r", j)), r_done, par_in, past(rg_read))
                bank_free[b_r] = r_ok
                i_ok = AC.run(lambda e: e.activation(ig[:, s, :], bank[b_i][:, :], ACT.Sigmoid,
                                                     bias=par("b_i", j)), i_done, past(ig_read))
                bank_free[b_i] = i_ok
                th_ok = AC.run(lambda e: e.activation(th[:, s, :], rg[:, s, :], ACT.Tanh,
                                                      scale=c4[:, j:j + 1]), r_ok, c4_ready, past(th_read))
                rg_read[j] = th_ok
                ix = PO.run(lambda e: e.tensor_tensor(ig[:, s, :], ig[:, s, :], xc[:, j, :], ALU.mult),
                            i_ok, xc_ready[j])
                t = VE.run(lambda e: e.tensor_scalar(av[:, s, :], th[:, s, :], 1.0, None, ALU.add), th_ok)
                t = VE.run(lambda e: e.reciprocal(mv[:, s, :], av[:, s, :]), t, past(mv_read))
                q = VE.run(lambda e: e.tensor_tensor(th[:, s, :], th[:, s, :], mv[:, s, :], ALU.mult), t)
                a_ok = VE.run(lambda e: e.tensor_scalar(av[:, s, :], th[:, s, :], -2.0, 1.0,
                                                        ALU.mult, ALU.add), q)
                t = VE.run(lambda e: e.scalar_tensor_tensor(mv[:, s, :], th[:, s, :], 1.0, th[:, s, :],
                                                            ALU.subtract, ALU.mult), a_ok)
                th_read[j] = t
                root = AC.run(lambda e: e.activation(mv[:, s, :], mv[:, s, :], ACT.Sqrt, scale=-4.0), t)

                def scan():
                    u = VE.run(lambda e: e.tensor_tensor(ig[:, s, :], mv[:, s, :], ig[:, s, :], ALU.mult),
                               root, ix)
                    mv_read[j] = u
                    h_ready[j] = VE.run(lambda e: e.tensor_tensor_scan(
                        hs[:, j, :], av[:, s, :], ig[:, s, :], 0.0, ALU.mult, ALU.add), u)
                    ig_read[j] = av_read[j] = h_ready[j]
                return scan

            pend = []
            for j in range(RT):
                b, token = in_tile(j)
                conv(j, b, token)
                if j >= 2:
                    pend.append(recur(j - 2))
                    if len(pend) > 1:
                        pend.pop(0)()
            rest = list(range(RT - 2, RT))
            y_ready = [None] * RT
            for j in range(RT):
                b, token = in_tile(RT + j)
                if rest:
                    pend.append(recur(rest.pop(0)))
                if pend:
                    pend.pop(0)()
                g_ok = AC.run(lambda e, j=j, b=b: e.activation(gate[:, j % 2, :], bank[b][:, :],
                                                               ACT.Gelu_apprx_tanh),
                              token, y_ready[j - 2] if j >= 2 else None)
                bank_free[b] = g_ok
                if j >= 3:
                    pass
                while h_ready[j] is None:
                    pend.pop(0)()
                y_ready[j] = VE.run(lambda e, j=j: e.tensor_tensor(hs[:, j, :], hs[:, j, :], gate[:, j % 2, :],
                                                                   ALU.mult), g_ok)
            x_free = token
            y_split = []
            for j in range(RT):
                a = AC.run(lambda e, j=j: e.activation(x_hi[:, j, :], hs[:, j, :], ACT.Copy), y_ready[j], x_free)
                y_split.append(VE.run(lambda e, j=j: e.tensor_tensor(
                    x_lo[:, j, :], hs[:, j, :], x_hi[:, j, :].bitcast(F32), ALU.subtract), a))

            out_banks = [(get_bank() if n < RING else 7) for n in range(8)]
            for k in range(RT):
                c, hi, lo = take((0, io["rec_out"][k], W))
                PE.wait(y_split[k])
                done = []
                for tt in range(TT):
                    for half in range(2):
                        f = mm3(bank[out_banks[2 * tt + half]][:, :], x_hi[:, k, tt * P:(tt + 1) * P],
                                x_lo[:, k, tt * P:(tt + 1) * P], hi[:, half * T:(half + 1) * T],
                                lo[:, half * T:(half + 1) * T], k == 0, k == RT - 1)
                        done.append(PE.run(f))
                release(c, done[-1])
            rec_done = done[-1]

            for n in range(4):
                PO.issue(lambda e, n=n: e.dma_start(gb[:, n, :], io["ln"][n:n + 1, :].partition_broadcast(P))
                         .then_inc(s_gb[n], 16), rec_done, VE.here(), AC.here())

            def norm(tt, which, z_ok):
                x = x_tok[:, tt, :]
                for h in range(2):
                    t = VE.run(lambda e, h=h: e.bn_stats(st[:, tt, h * 6:h * 6 + 6], x[:, h * T:(h + 1) * T]), z_ok)
                t = VE.run(lambda e: e.bn_aggr(st[:, tt, 12:14], st[:, tt, 0:12]), t)
                t = VE.run(lambda e: e.tensor_scalar(st[:, tt, 14:15], st[:, tt, 13:14], LN_EPS, None, ALU.add), t)
                t = AC.run(lambda e: e.activation(st[:, tt, 15:16], st[:, tt, 14:15], ACT.Sqrt), t)
                t = VE.run(lambda e: e.reciprocal(st[:, tt, 16:17], st[:, tt, 15:16]), t)
                t = VE.run(lambda e: e.tensor_scalar(x, x, st[:, tt, 12:13], st[:, tt, 16:17],
                                                     ALU.subtract, ALU.mult), t)
                t = VE.run(lambda e: e.tensor_tensor(x, x, gb[:, 2 * which, :], ALU.mult), t, (s_gb[2 * which], 16))
                return PO.run(lambda e: e.tensor_tensor(x, x, gb[:, 2 * which + 1, :], ALU.add),
                              t, (s_gb[2 * which + 1], 16))

            x1_ok = []
            for tt in range(TT):
                for half in range(2):
                    b = out_banks[2 * tt + half]
                    x = x_tok[:, tt, half * T:(half + 1) * T]
                    t = VE.run(lambda e, x=x, b=b: e.scalar_tensor_tensor(
                        x, x, ALPHA, bank[b][:, :], ALU.mult, ALU.add), done[2 * tt + half], x_in)
                    bank_free[b] = t
                x1_ok.append(norm(tt, 0, t))
                PO.issue(lambda e, tt=tt: e.dma_start(x1_dram[tt * P:(tt + 1) * P, :], x_tok[:, tt, :])
                         .then_inc(s_x1, 16), x1_ok[tt])

            def transpose4(src, b, ok):
                PE.wait(ok, par_in)
                for n in range(4):
                    f = lambda e, n=n: e.transpose(bank[b][:, n * P:(n + 1) * P], src(n), ident)
                    if n < 3:
                        PE.issue(f)
                return PE.run(f)

            SP_or_act = AC
            AC.issue(lambda e: e.dma_start(wr[:, :, :], io["wr"]).then_inc(s_router, 16))
            AC.issue(lambda e: e.dma_start(br[:, :], io["br"]).then_inc(s_router, 16))
            x1T_ok = []
            for tt in range(TT):
                for half in range(2):
                    b = get_bank()
                    t = transpose4(lambda n, tt=tt, half=half: x_tok[:, tt, (4 * half + n) * P:(4 * half + n + 1) * P],
                                   b, x1_ok[tt])
                    t = AC.run(lambda e, b=b, tt=tt, half=half: e.activation(
                        x1T[:, 4 * half:4 * half + 4, tt * P:(tt + 1) * P],
                        bank[b][:, :].rearrange("p (n q) -> p n q", n=4), ACT.Copy), t)
                    bank_free[b] = t
                x1T_ok.append(t)
            lg_bank = get_bank()
            PE.wait((s_router, 32), ones_ready)
            for tt in range(TT):
                o = bank[lg_bank][:, tt * (NG + NE):(tt + 1) * (NG + NE)]
                PE.wait(x1T_ok[tt])
                for k in range(DT):
                    PE.issue(lambda e, o=o, k=k, tt=tt: e.matmul(o, x1T[:, k, tt * P:(tt + 1) * P], wr[:, k, :],
                                                                 start=k == 0, stop=False))
                t = PE.run(lambda e, o=o: e.matmul(o, ones[0:1, :], br[0:1, :], start=False, stop=True))
            t = VE.run(lambda e: e.tensor_copy(lg[:, :, :], bank[lg_bank][:, 0:TT * (NG + NE)]
                                               .rearrange("p (a n) -> p a n", a=TT)), t)
            bank_free[lg_bank] = t

            S = lambda n: sm[:, n, :]
            Rt = lambda n: rt[:, n, :, :]
            wide = lambda ap: ap.unsqueeze(2).to_broadcast([P, TT, NE])
            V = lambda fn, *w: VE.run(fn, *w)

            def tt_(o, a, b, op, *w):
                return V(lambda e: e.tensor_tensor(o, a, b, op), *w)

            def ts_(o, a, s1, s2, op0, op1=None, *w):
                if op1 is None:
                    return V(lambda e: e.tensor_scalar(o, a, s1, None, op0), *w)
                return V(lambda e: e.tensor_scalar(o, a, s1, s2, op0, op1), *w)

            grank = consts[:, C_GRANK:C_GRANK + TT * NG].rearrange("p (a n) -> p a n", a=TT)
            erank = consts[:, C_ERANK:C_ERANK + TT * NE].rearrange("p (a n) -> p a n", a=TT)
            eidx = consts[:, C_EIDX:C_EIDX + TT * NE].rearrange("p (a n) -> p a n", a=TT)
            gl = lg[:, :, 0:NG]
            el = lg[:, :, NG:NG + NE]
            G = lambda n: rt[:, n, :, 0:NG]
            gwide = lambda ap: ap.unsqueeze(2).to_broadcast([P, TT, NG])

            t = V(lambda e: e.tensor_reduce(S(0), gl, AX_X, ALU.max), t)
            t = tt_(G(0), gl, gwide(S(0)), ALU.is_equal, t)
            t = tt_(G(1), G(0), grank, ALU.mult, t)
            t = V(lambda e: e.tensor_reduce(S(1), G(1), AX_X, ALU.max), t)
            t = tt_(G(2), G(1), gwide(S(1)), ALU.is_equal, t)
            t2 = tt_(G(3), gl, gwide(S(0)), ALU.subtract, t)
            t2 = AC.run(lambda e: e.activation(G(4), G(3), ACT.Exp), t2)
            t2 = V(lambda e: e.tensor_reduce(S(2), G(4), AX_X, ALU.add), t2)
            t2 = V(lambda e: e.reciprocal(S(3), S(2)), t2)
            t = ts_(G(5), G(2), 1.0, BIG, ALU.subtract, ALU.mult, t2)
            em = Rt(6)
            for g in range(NG):
                sl = slice(g * EPG, (g + 1) * EPG)
                t = tt_(em[:, :, sl], el[:, :, sl], G(5)[:, :, g:g + 1].to_broadcast([P, TT, EPG]), ALU.add, t)

            def largest(vals, value, onehot, scratch, t):
                t = V(lambda e: e.tensor_reduce(value, vals, AX_X, ALU.max), t)
                t = tt_(scratch, vals, wide(value), ALU.is_equal, t)
                t = tt_(scratch, scratch, erank, ALU.mult, t)
                t = V(lambda e: e.tensor_reduce(S(4), scratch, AX_X, ALU.max), t)
                return tt_(onehot, scratch, wide(S(4)), ALU.is_equal, t)

            t = largest(em, S(5), Rt(7), Rt(0), t)
            t = V(lambda e: e.scalar_tensor_tensor(
                rt[:, 8, :, :].rearrange("p a n -> p (a n)"), rt[:, 7, :, :].rearrange("p a n -> p (a n)"),
                -4.0 * BIG, rt[:, 6, :, :].rearrange("p a n -> p (a n)"), ALU.mult, ALU.add), t)
            t = largest(Rt(8), S(6), Rt(9), Rt(0), t)
            t = tt_(S(7), S(6), S(5), ALU.subtract, t)
            t = AC.run(lambda e: e.activation(S(8), S(7), ACT.Exp), t)
            t = ts_(S(9), S(8), 1.0, None, ALU.add, None, t)
            t = V(lambda e: e.reciprocal(S(10), S(9)), t)
            t = tt_(S(11), S(10), S(3), ALU.mult, t)
            t = tt_(S(12), S(11), S(8), ALU.mult, t)
            sel_ok = tt_(Rt(10), Rt(7), Rt(9), ALU.add, t)

            rk_bank = get_bank()
            PE.wait(sel_ok)
            for tt in range(TT + 1):
                o = bank[rk_bank][:, tt * NE:(tt + 1) * NE]
                terms = [(ones[:, :], a) for a in range(min(tt, TT))] + ([(upper, tt)] if tt < TT else [])
                for n, (m, a) in enumerate(terms):
                    f = lambda e, o=o, m=m, a=a, n=n, k=len(terms): e.matmul(
                        o, m, rt[:, 10, a, :], start=n == 0, stop=n == k - 1)
                    if not (tt == TT and n == len(terms) - 1):
                        PE.issue(f)
            t = PE.run(f)
            t = V(lambda e: e.tensor_copy(Rt(11), bank[rk_bank][:, 0:TT * NE]
                                          .rearrange("p (a n) -> p a n", a=TT)), t)
            C = lambda n: rt[:, 12, n, :]
            t = V(lambda e: e.tensor_copy(C(0), bank[rk_bank][:, TT * NE:(TT + 1) * NE]), t)
            bank_free[rk_bank] = t
            t = ts_(C(1), C(0), float(P), None, ALU.is_gt, None, t)
            for m in (2, 3):
                t = V(lambda e, m=m: e.scalar_tensor_tensor(C(2), C(0), float(m * P), C(1), ALU.is_gt, ALU.add), t)
                t = V(lambda e: e.tensor_copy(C(1), C(2)), t)
            D_ = lambda n: rt[:, 13, n, :]
            t = V(lambda e: e.memset(D_(0), 1.0), t)
            t = V(lambda e: e.tensor_tensor_scan(C(3), D_(0), C(1), 0.0, ALU.mult, ALU.add), t)
            t = tt_(D_(1), C(3), C(1), ALU.subtract, t)
            t = V(lambda e: e.tensor_copy(cnt[:, :], C(3)[:, NE - 1:NE]), t)
            cnt_ok = t
            for j in range(EXTRA):
                t = V(lambda e, j=j: e.tensor_scalar(D_(2), C(3), float(j) + 0.5, None, ALU.is_lt), t)
                t = V(lambda e, j=j: e.tensor_reduce(sm[:, 30, 0:1], D_(2), AX_X, ALU.add), t)
                t = V(lambda e: e.tensor_scalar(sm[:, 31, 0:1], sm[:, 30, 0:1], float(4 * P),
                                                consts[:, C_ROW4:C_ROW4 + 1], ALU.mult, ALU.add), t)
                for q in range(4):
                    t = V(lambda e, j=j, q=q: e.tensor_scalar(wix[:, j, q:q + 1], sm[:, 31, 0:1], float(q), None,
                                                              ALU.add), t)
            widx_ok = V(lambda e: e.tensor_copy(widx[:, :, :], wix[:, :, :]), t)
            oneh_ok = []
            for k in range(2):
                oh = Rt(7 if k == 0 else 9)
                o = 13 + 6 * k
                t = tt_(Rt(0), oh, Rt(11), ALU.mult, t)
                t = V(lambda e, o=o: e.tensor_reduce(S(o), Rt(0), AX_X, ALU.add), t)
                t = tt_(Rt(0), oh, eidx, ALU.mult, t)
                t = V(lambda e, o=o: e.tensor_reduce(S(o + 1), Rt(0), AX_X, ALU.add), t)
                for a in range(TT):
                    t = tt_(rt[:, 0, a, :], oh[:, a, :], D_(1), ALU.mult, t)
                t = V(lambda e, o=o: e.tensor_reduce(S(o + 2), Rt(0), AX_X, ALU.add), t)
                t = ts_(S(o + 3), S(o), float(P) - 0.5, None, ALU.is_gt, None, t)
                for m in (2, 3):
                    t = V(lambda e, m=m, o=o: e.scalar_tensor_tensor(
                        S(o + 4), S(o), float(m * P) - 0.5, S(o + 3), ALU.is_gt, ALU.add), t)
                    t = V(lambda e, o=o: e.tensor_copy(S(o + 3), S(o + 4)), t)
                t = V(lambda e, o=o: e.scalar_tensor_tensor(S(o), S(o + 3), -float(P), S(o), ALU.mult, ALU.add), t)
                t = tt_(S(o + 2), S(o + 2), S(o + 3), ALU.add, t)
                t = ts_(S(o + 2), S(o + 2), float(NE - 1), None, ALU.add, None, t)
                t = tt_(S(o + 2), S(o + 2), S(o + 1), ALU.subtract, t)
                t = ts_(S(o + 4), S(o + 3), 0.5, None, ALU.is_gt, None, t)
                t = tt_(S(o + 2), S(o + 2), S(o + 4), ALU.mult, t)
                t = tt_(S(o + 1), S(o + 1), S(o + 2), ALU.add, t)
                for a in range(TT):
                    n = k * TT + a
                    t = V(lambda e, n=n, o=o, a=a: e.tensor_scalar(oneh[:, n, :], iota, sm[:, o, a:a + 1], None,
                                                                   ALU.is_equal), t)
                    t = V(lambda e, n=n, o=o, a=a: e.tensor_scalar(
                        blkh[:, n, :], iota[:, 0:NBLK], sm[:, o + 1, a:a + 1],
                        consts[:, C_SLOT + n:C_SLOT + n + 1], ALU.is_equal, ALU.mult), t)
                    oneh_ok.append(t)
            tb_bank = get_bank()
            for n in range(2 * TT):
                PE.wait(oneh_ok[n])
                f = lambda e, n=n: e.matmul(bank[tb_bank][:, 0:NBLK], oneh[:, n, :], blkh[:, n, :],
                                            start=n == 0, stop=n == 2 * TT - 1)
                if n < 2 * TT - 1:
                    PE.issue(f)
            t = PE.run(f)
            Tb = lambda n: tabs[:, n, :]
            t = V(lambda e: e.tensor_scalar(Tb(0), bank[tb_bank][:, 0:NBLK], 1.0, None, ALU.subtract), t)
            bank_free[tb_bank] = t
            t = ts_(Tb(1), Tb(0), 0.0, float(8 * T), ALU.is_lt, ALU.mult, t)
            t = tt_(Tb(2), Tb(0), Tb(1), ALU.add, t)
            t = V(lambda e: e.tensor_copy(sidx[:, :], Tb(2)), t)
            t = ts_(Tb(1), Tb(2), float(T) - 0.5, -float(T), ALU.is_gt, ALU.mult, t)
            t = tt_(Tb(3), Tb(2), Tb(1), ALU.add, t)
            idx_ok = V(lambda e: e.tensor_copy(gidx[:, :], Tb(3)), t)
            xe_clear = PO.run(lambda e: e.memset(xe[:, :, :], 0.0), rec_done)

            gathers = [0, 0, 0]
            scatters = [0, 0, 0]
            xe_read = {}

            def gather(n):
                s = n % 3
                gathers[s] += 16
                PO.issue(lambda e: e.indirect_dma_start(
                    xe[:, s, :], None, x1_dram, bass.IndirectOffsetOnAxis(ap=gidx[:, n:n + 1], axis=0),
                    bounds_check=T - 1, oob_is_err=False).then_inc(s_gather[s], 16),
                    idx_ok, xe_clear, (s_x1, 16 * TT), xe_read.get(n - 3))

            xeT_ok, xeT_read, hd_ok, hT_ok, sil_read, hd_read, hT_read = {}, {}, {}, {}, {}, {}, {}

            def x_turn(n):
                s = n % 2
                oks = []
                for half in range(2):
                    b = get_bank()
                    t = transpose4(lambda q, half=half: xe[:, n % 3, (4 * half + q) * P:(4 * half + q + 1) * P],
                                   b, (s_gather[n % 3], 16 * (n // 3 + 1)))
                    xe_read[n] = t
                    o = slice(half * T, (half + 1) * T)
                    hi = AC.run(lambda e, o=o, b=b: e.activation(xeT_hi[:, s, o], bank[b][:, :], ACT.Copy),
                                t, xeT_read.get(n - 2))
                    lo = VE.run(lambda e, o=o, b=b: e.tensor_tensor(xeT_lo[:, s, o], bank[b][:, :],
                                                                    xeT_hi[:, s, o].bitcast(F32), ALU.subtract),
                                hi, xeT_read.get(n - 2))
                    bank_free[b] = lo
                xeT_ok[n] = lo

            def up(n):
                s = n % 2
                toks = []
                for m, name in enumerate(("moe1", "moe3")):
                    b = get_bank()
                    for q in range(4):
                        c, hi, lo = take((0, io[name][n, q], W))
                        PE.wait(xeT_ok.get(n))
                        for kk in range(2):
                            k = 2 * q + kk
                            f = mm3(bank[b][:, :], xeT_hi[:, s, k * P:(k + 1) * P], xeT_lo[:, s, k * P:(k + 1) * P],
                                    hi[:, kk * FE:(kk + 1) * FE], lo[:, kk * FE:(kk + 1) * FE], k == 0, k == DT - 1)
                            if kk == 0:
                                PE.issue(f)
                        t = PE.run(f)
                        release(c, t)
                        if m == 1 and q == 1 and n + 1 < NE:
                            x_turn(n + 1)
                    if m == 0:
                        sil_ok = AC.run(lambda e, b=b: e.activation(sil[:, s, :], bank[b][:, :], ACT.Silu),
                                        t, sil_read.get(n - 2))
                        bank_free[b] = sil_ok
                    else:
                        hd_ok[n] = VE.run(lambda e, b=b: e.tensor_tensor(hd[:, s, :], sil[:, s, :], bank[b][:, :],
                                                                         ALU.mult), t, sil_ok, hd_read.get(n - 2))
                        sil_read[n] = bank_free[b] = hd_ok[n]
                xeT_read[n] = t

            def h_turn(n):
                s = n % 2
                b = get_bank()
                t = transpose4(lambda q: hd[:, s, q * P:(q + 1) * P], b, hd_ok[n])
                hd_read[n] = t
                hi = AC.run(lambda e: e.activation(hT_hi[:, s, :], bank[b][:, :], ACT.Copy), t, hT_read.get(n - 2))
                hT_ok[n] = VE.run(lambda e: e.tensor_tensor(hT_lo[:, s, :], bank[b][:, :],
                                                            hT_hi[:, s, :].bitcast(F32), ALU.subtract), hi)
                bank_free[b] = hT_ok[n]

            def down(n):
                s = n % 2
                bs = [get_bank(), get_bank()]
                for q in range(FET):
                    c, hi, lo = take((0, io["moe2"][n, q], W))
                    PE.wait(hT_ok[n])
                    toks = []
                    for half in range(2):
                        f = mm3(bank[bs[half]][:, :], hT_hi[:, s, q * P:(q + 1) * P], hT_lo[:, s, q * P:(q + 1) * P],
                                hi[:, half * T:(half + 1) * T], lo[:, half * T:(half + 1) * T], q == 0, q == FET - 1)
                        toks.append(PE.run(f))
                    release(c, toks[-1])
                hT_read[n] = toks[-1]
                y = n % 3
                gone = (s_scatter[y], scatters[y]) if scatters[y] else None
                a = AC.run(lambda e: e.activation(ye[:, y, 0:T], bank[bs[0]][:, :], ACT.Copy), toks[0], gone)
                v = VE.run(lambda e: e.tensor_copy(ye[:, y, T:D], bank[bs[1]][:, :]), toks[1], gone)
                bank_free[bs[0]], bank_free[bs[1]] = a, v
                scatters[y] += 16
                PO.issue(lambda e: e.indirect_dma_start(
                    ys_dram, bass.IndirectOffsetOnAxis(ap=sidx[:, n:n + 1], axis=0), ye[:, y, :], None,
                    bounds_check=2 * T - 1, oob_is_err=False).then_inc(s_scatter[y], 16), a, v)

            gather(0)
            gather(1)
            x_turn(0)
            for n in range(NE + 1):
                if n + 2 < NE:
                    gather(n + 2)
                if n < NE:
                    up(n)
                if n >= 1:
                    down(n - 1)
                if n < NE:
                    h_turn(n)

            outer = [PE.here(), AC.here(), VE.here(), PO.here(), cnt_ok] + [(s_scatter[i], scatters[i]) for i in range(3)]
            saved = [(q, q.done, q.sem, q.seen) for q in (PE, AC, VE, PO)]
            branch = ExitStack()
            for q, o in ((PE, o_pe), (AC, o_act), (VE, o_dve), (PO, o_pool)):
                q.wait(cnt_ok)
                if q.eng is not None:
                    more = q.eng.value_load(cnt[0:1, 0:1], min_val=0, max_val=EXTRA)
                    branch.enter_context(q.eng.If(more != 0))
                q.sem, q.done, q.seen = o, 0, dict(q.seen)
                q.wait(*outer)
            o_w, o_r, o_s = [0], [0], [0]
            w_free = None
            for x in range(EXTRA):
                n = NE + x
                o_r[0] += 16
                PO.issue(lambda e, n=n: e.indirect_dma_start(
                    xe[:, 0, :], None, x1_dram, bass.IndirectOffsetOnAxis(ap=gidx[:, n:n + 1], axis=0),
                    bounds_check=T - 1, oob_is_err=False).then_inc(o_rows, 16), PE.here())
                for half in range(2):
                    t = transpose4(lambda q, half=half: xe[:, 0, (4 * half + q) * P:(4 * half + q + 1) * P],
                                   half, (o_rows, o_r[0]))
                    o = slice(half * T, (half + 1) * T)
                    hi = AC.run(lambda e, o=o, half=half: e.activation(xeT_hi[:, 0, o], bank[half][:, :], ACT.Copy), t)
                    lo = VE.run(lambda e, o=o, half=half: e.tensor_tensor(
                        xeT_lo[:, 0, o], bank[half][:, :], xeT_hi[:, 0, o].bitcast(F32), ALU.subtract), hi)

                def weights(name, x, q):
                    o_w[0] += 16
                    PO.issue(lambda e: e.indirect_dma_start(
                        o_raw[:, :], None, io[name + "_rows"], bass.IndirectOffsetOnAxis(ap=widx[:, x, q:q + 1], axis=0),
                        bounds_check=NE * P * 4 - 1, oob_is_err=False).then_inc(o_weight, 16), VE.here())
                    hi = AC.run(lambda e: e.activation(o_hi[:, :], o_raw[:, :], ACT.Copy), (o_weight, o_w[0]), PE.here())
                    PE.wait(VE.run(lambda e: e.tensor_tensor(o_lo[:, :], o_raw[:, :], o_hi[:, :].bitcast(F32),
                                                             ALU.subtract), hi))

                if x == 0:
                    o_clear = PO.run(lambda e: e.memset(o_raw[:, :], 0.0))
                    VE.wait(o_clear)
                    PO.wait(o_clear)
                PE.wait(lo)
                for m, name in enumerate(("moe1", "moe3")):
                    for q in range(4):
                        weights(name, x, q)
                        for kk in range(2):
                            k = 2 * q + kk
                            t = PE.run(mm3(bank[2 + m][:, :], xeT_hi[:, 0, k * P:(k + 1) * P],
                                           xeT_lo[:, 0, k * P:(k + 1) * P], o_hi[:, kk * FE:(kk + 1) * FE],
                                           o_lo[:, kk * FE:(kk + 1) * FE], k == 0, k == DT - 1))
                t = AC.run(lambda e: e.activation(sil[:, 0, :], bank[2][:, :], ACT.Silu), t)
                t = VE.run(lambda e: e.tensor_tensor(hd[:, 0, :], sil[:, 0, :], bank[3][:, :], ALU.mult), t)
                t = transpose4(lambda q: hd[:, 0, q * P:(q + 1) * P], 4, t)
                t = AC.run(lambda e: e.activation(hT_hi[:, 0, :], bank[4][:, :], ACT.Copy), t)
                t = VE.run(lambda e: e.tensor_tensor(hT_lo[:, 0, :], bank[4][:, :], hT_hi[:, 0, :].bitcast(F32),
                                                     ALU.subtract), t)
                PE.wait(t)
                for q in range(FET):
                    weights("moe2", x, q)
                    for half in range(2):
                        t = PE.run(mm3(bank[5 + half][:, :], hT_hi[:, 0, q * P:(q + 1) * P],
                                       hT_lo[:, 0, q * P:(q + 1) * P], o_hi[:, half * T:(half + 1) * T],
                                       o_lo[:, half * T:(half + 1) * T], q == 0, q == FET - 1))
                t = VE.run(lambda e: e.tensor_copy(ye[:, 0, 0:T], bank[5][:, :]), t,
                           (o_store, o_s[0]) if o_s[0] else None)
                t = VE.run(lambda e: e.tensor_copy(ye[:, 0, T:D], bank[6][:, :]), t)
                o_s[0] += 16
                PO.issue(lambda e, n=n: e.indirect_dma_start(
                    ys_dram, bass.IndirectOffsetOnAxis(ap=sidx[:, n:n + 1], axis=0), ye[:, 0, :], None,
                    bounds_check=2 * T - 1, oob_is_err=False).then_inc(o_store, 16), t)
            ends = [q.here() for q in (PE, AC, VE, PO)] + [(o_store, o_s[0])]
            for q, done_, s_, seen_ in saved:
                q.wait(*ends)
                q.sem, q.done, q.seen = s_, done_, seen_
            branch.close()

            over = PO.run(lambda e: e.memset(sm[:, 29, 0:1], 0.0), *outer)
            ys_read = [None, None]
            last_tok = []
            for tt in range(TT):
                h = tt % 2
                for k in range(2):
                    PO.issue(lambda e, tt=tt, k=k, h=h: e.dma_start(
                        ysl[:, 2 * h + k, :], ys_dram[k * T + tt * P:k * T + (tt + 1) * P, :])
                        .then_inc(s_ys[2 * h + k], 16), ys_read[h])
                x = x_tok[:, tt, :]
                t = VE.run(lambda e, x=x: e.tensor_scalar(x, x, ALPHA, None, ALU.mult), over)
                for k in range(2):
                    t = VE.run(lambda e, x=x, k=k, h=h, tt=tt: e.scalar_tensor_tensor(
                        x, ysl[:, 2 * h + k, :], sm[:, 11 + k, tt:tt + 1], x, ALU.mult, ALU.add),
                        t, (s_ys[2 * h + k], 16 * (tt // 2 + 1)))
                ys_read[h] = t
                last_tok.append(norm(tt, 1, t))

            FREE = {}
            stat = {"bank_free": VE.here(), "n": 0}
            xg_count = [0]
            xg_ok = [None] * DT
            rs_state = {}

            def finish(j, x_ok, gain):
                s = xg_count[0] % 2
                xg_count[0] += 1
                t = VE.run(lambda e: e.tensor_scalar(tmp[:, 4 + s, :], xT[:, j, :], gain, None, ALU.mult),
                           x_ok, FREE.get(("xg", s)))
                hi = AC.run(lambda e: e.activation(xg_hi[:, j, :], tmp[:, 4 + s, :], ACT.Copy), t)
                xg_ok[j] = VE.run(lambda e: e.tensor_tensor(xg_lo[:, j, :], tmp[:, 4 + s, :],
                                                            xg_hi[:, j, :].bitcast(F32), ALU.subtract), hi)
                FREE["xg", s] = xg_ok[j]
                sq = AC.run(lambda e: e.activation(tmp[:, 6 + s, :], xT[:, j, :], ACT.Square),
                            x_ok, FREE.get(("sq", s)))

                def add():
                    if j == 0:
                        PE.wait(stat["bank_free"])
                    t = PE.run(lambda e: e.matmul(bank[7][:, :], ones[:, :], tmp[:, 6 + s, :],
                                                  start=j == 0, stop=j == DT - 1), sq)
                    FREE["sq", s] = t
                    if j == DT - 1:
                        t = VE.run(lambda e: e.tensor_scalar(rsq[:, :], bank[7][:, :], 1.0 / D, RMS_EPS,
                                                             ALU.mult, ALU.add), t)
                        stat["bank_free"] = t
                        t = AC.run(lambda e: e.activation(rsq[:, :], rsq[:, :], ACT.Sqrt), t)
                        rs_state["ok"] = VE.run(lambda e: e.reciprocal(rsq[:, :], rsq[:, :]), t)
                later.append(add)

            for half in range(2):
                toks = [None] * 4
                for q in range(4):
                    j = 4 * half + q
                    b = get_bank()
                    for tt in range(TT):
                        PE.wait(last_tok[tt])
                        f = lambda e, b=b, j=j, tt=tt: e.transpose(bank[b][:, tt * P:(tt + 1) * P],
                                                                   x_tok[:, tt, j * P:(j + 1) * P], ident)
                        if tt < TT - 1:
                            PE.issue(f)
                    t = PE.run(f)
                    x_ok = VE.run(lambda e, j=j, b=b: e.tensor_copy(xT[:, j, :], bank[b][:, :]), t, *last_tok)
                    bank_free[b] = x_ok
                    run_later()
                    finish(j, x_ok, par("g_ffn1", j))
            tok_gone = t

            def product(b, tiles, rhs_hi, rhs_lo, oks):
                for n, (a_hi, a_lo, k, start, stop) in enumerate(tiles):
                    PE.wait(oks(k))
                    f = mm3(bank[b][:, :], a_hi, a_lo, rhs_hi(k), rhs_lo(k), start, stop)
                    if n < len(tiles) - 1:
                        PE.issue(f)
                return PE.run(f)

            def from_xg(src):
                c, hi, lo = take((0, src, W))
                b = get_bank()
                t = product(b, [(hi[:, k * P:(k + 1) * P], lo[:, k * P:(k + 1) * P], k, k == 0, k == DT - 1)
                                for k in range(DT)], lambda k: xg_hi[:, k, :], lambda k: xg_lo[:, k, :],
                            lambda k: xg_ok[k])
                release(c, t)
                run_later()
                return b, t

            def split_to(g, src_ap, ok, *more):
                hi = AC.run(lambda e: e.activation(g_hi[:, g, :], src_ap, ACT.Copy), ok, *more)
                return VE.run(lambda e: e.tensor_tensor(g_lo[:, g, :], src_ap, g_hi[:, g, :].bitcast(F32),
                                                        ALU.subtract), hi, ok, *more)

            def residual(j, b, t, coef, gain):
                x_ok = VE.run(lambda e: e.scalar_tensor_tensor(xT[:, j, :], bank[b][:, :], coef, xT[:, j, :],
                                                               ALU.mult, ALU.add), t)
                bank_free[b] = x_ok
                finish(j, x_ok, gain)

            def swiglu(l, names, gain):
                g_ok = [None] * FFT
                for j in range(FFT):
                    s = j % 2
                    b1, t1 = from_xg(io[names[0]][l, j])
                    b3, t3 = from_xg(io[names[1]][l, j])
                    u = VE.run(lambda e: e.tensor_tensor(tmp[:, s, :], bank[b1][:, :], rsq[:, :], ALU.mult),
                               t1, rs_state["ok"], FREE.get(("u", s)), tok_gone)
                    bank_free[b1] = u
                    u = AC.run(lambda e: e.activation(tmp[:, s, :], tmp[:, s, :], ACT.Silu), u)
                    v = VE.run(lambda e: e.tensor_tensor(tmp[:, 2 + s, :], bank[b3][:, :], rsq[:, :], ALU.mult), t3,
                               FREE.get(("v", s)))
                    bank_free[b3] = v
                    m = PO.run(lambda e: e.tensor_tensor(tmp[:, 2 + s, :], tmp[:, 2 + s, :], tmp[:, s, :], ALU.mult),
                               u, v)
                    FREE["u", s] = m
                    g_ok[j] = split_to(j, tmp[:, 2 + s, :], m)
                    FREE["v", s] = g_ok[j]
                for j in range(DT):
                    b = get_bank()
                    for q in range(3):
                        k0, k1 = 8 * q, min(8 * q + 8, FFT)
                        c, hi, lo = take((0, io[names[2]][l, j][:, k0 * P:k1 * P], (k1 - k0) * P))
                        t = product(b, [(hi[:, (k - k0) * P:(k - k0 + 1) * P], lo[:, (k - k0) * P:(k - k0 + 1) * P], k,
                                         k == 0, k == FFT - 1) for k in range(k0, k1)],
                                    lambda k: g_hi[:, k, :], lambda k: g_lo[:, k, :], lambda k: g_ok[k])
                        release(c, t)
                    run_later()
                    residual(j, b, t, 0.5, gain(j))

            PAIR_F, PAIR_A, PAIR_M, PAIR_C, PAIR_P = 0, 4, 4, 12, 16

            def mixers(l, gain):
                def column(i):
                    return from_xg(io["w_in"][l, i])

                ok = {}
                for i in range(4):
                    b, t = column(IN_F + i)
                    s = i % 2
                    u = VE.run(lambda e: e.tensor_tensor(tmp[:, s, :], bank[b][:, :], rsq[:, :], ALU.mult),
                               t, rs_state["ok"], FREE.get(("u", s)))
                    bank_free[b] = u
                    ok["u", i] = FREE["u", s] = split_to(PAIR_F + i, tmp[:, s, :], u)

                def conv_branch(i):
                    s = i % 2
                    b, t = column(IN_C + i)
                    cg = VE.run(lambda e: e.tensor_tensor(tmp[:, s, :], bank[b][:, :], rsq[:, :], ALU.mult),
                                t, rs_state["ok"], FREE.get(("u", s)))
                    bank_free[b] = cg
                    b2, t = column(IN_V + i)
                    v = VE.run(lambda e: e.tensor_tensor(tmp[:, 2 + s, :], bank[b2][:, :], rsq[:, :], ALU.mult), t,
                               FREE.get(("v", s)))
                    bank_free[b2] = v
                    z = zc[:, s, :]
                    pad = PO.run(lambda e: e.memset(z, 0.0), FREE.get(("z", s)))
                    t = PO.run(lambda e: e.tensor_tensor(z[:, 1:T + 1], tmp[:, s, :], tmp[:, 2 + s, :], ALU.mult),
                               cg, v, pad)
                    w = lambda k: par("w_conv", (l * 3 + k) * 4 + i)
                    t = VE.run(lambda e: e.tensor_scalar(tmp[:, s, :], z[:, 0:T], w(0), None, ALU.mult), t)
                    for k in (1, 2):
                        t = VE.run(lambda e, k=k: e.scalar_tensor_tensor(tmp[:, s, :], z[:, k:k + T], w(k), tmp[:, s, :],
                                                                         ALU.mult, ALU.add), t)
                    FREE["z", s] = t
                    cv = PO.run(lambda e: e.tensor_tensor(tmp[:, s, :], tmp[:, s, :], rsq[:, :], ALU.mult), t)
                    b3, t = column(IN_B + i)
                    m = VE.run(lambda e: e.tensor_tensor(tmp[:, s, :], tmp[:, s, :], bank[b3][:, :], ALU.mult), t, cv)
                    bank_free[b3] = m
                    ok["c", i] = split_to(PAIR_C + i, tmp[:, s, :], m)
                    FREE["u", s] = FREE["v", s] = ok["c", i]

                def token_spectra():
                    c, hi, lo = take((0, io["dft_c"], 2 * P))
                    for g in range(4):
                        for tt in range(TT):
                            if tt % 2 == 0:
                                b = get_bank()
                            f = mm3(bank[b][:, (tt % 2) * 256:(tt % 2) * 256 + 256],
                                    g_hi[:, PAIR_F + g, tt * P:(tt + 1) * P], g_lo[:, PAIR_F + g, tt * P:(tt + 1) * P],
                                    hi[:, 0:256], lo[:, 0:256], True, True)
                            PE.wait(ok["u", g])
                            t = PE.run(f)
                            if tt % 2 == 1:
                                pr = PAIR_A + 2 * g + tt // 2
                                hi_t = AC.run(lambda e, pr=pr, b=b: e.activation(g_hi[:, pr, :], bank[b][:, :], ACT.Copy), t)
                                ok["a", g, tt // 2] = VE.run(lambda e, pr=pr, b=b: e.tensor_tensor(
                                    g_lo[:, pr, :], bank[b][:, :], g_hi[:, pr, :].bitcast(F32), ALU.subtract), hi_t)
                                bank_free[b] = ok["a", g, tt // 2]
                    release(c, t)
                    ok["u_read"] = t

                def time_spectra():
                    bs = [get_bank() for _ in range(4)]
                    for n in range(4):
                        c, hi, lo = take((0, io["dft_s"][n], W))
                        for g in range(4):
                            for kk in range(2):
                                pr = PAIR_A + 2 * g + n % 2
                                PE.wait(ok["a", g, n % 2])
                                o = kk * 256 + (n // 2) * P
                                f = mm3(bank[bs[g]][:, :], g_hi[:, pr, o:o + P], g_lo[:, pr, o:o + P],
                                        hi[:, kk * T:(kk + 1) * T], lo[:, kk * T:(kk + 1) * T],
                                        n == 0 and kk == 0, n == 3 and kk == 1)
                                t = PE.run(f)
                            if n == 3:
                                hi_t = AC.run(lambda e, g=g: e.activation(g_hi[:, PAIR_F + g, :], bank[bs[g]][:, :],
                                                                          ACT.Copy), t, ok["u_read"])
                                ok["f", g] = VE.run(lambda e, g=g: e.tensor_tensor(
                                    g_lo[:, PAIR_F + g, :], bank[bs[g]][:, :], g_hi[:, PAIR_F + g, :].bitcast(F32),
                                    ALU.subtract), hi_t)
                                bank_free[bs[g]] = ok["f", g]
                        release(c, t)
                    ok["a_read"] = t

                conv_branch(0)
                token_spectra()
                conv_branch(1)
                conv_branch(2)
                time_spectra()
                conv_branch(3)

                for i in range(4):
                    s = i % 2
                    w, half = 2 << i, 1 << i
                    b, t = column(IN_P + i)
                    u0 = VE.run(lambda e: e.tensor_tensor(tmp[:, s, :], bank[b][:, :], rsq[:, :], ALU.mult), t,
                                FREE.get(("u", s)))
                    bank_free[b] = u0
                    pad = PO.run(lambda e: e.memset(zc[:, :, :], 0.0), FREE.get(("z", 0)), FREE.get(("z", 1)))
                    t = PO.run(lambda e: e.tensor_copy(zc[:, 0, half:half + T], tmp[:, s, :]), u0, pad)
                    a, n = 0, 1
                    while n < w:
                        width = T + w - 2 * n
                        last = 2 * n == w
                        dst = tmp[:, 2 + s, 0:width] if last else zc[:, 1 - a, 0:width]
                        t = VE.run(lambda e, a=a, n=n, width=width, dst=dst: e.tensor_tensor(
                            dst, zc[:, a, 0:width], zc[:, a, n:n + width], ALU.add), t, FREE.get(("v", s)))
                        a, n = 1 - a, 2 * n
                    FREE["z", 0] = FREE["z", 1] = t
                    t = VE.run(lambda e: e.tensor_scalar(tmp[:, 2 + s, :], tmp[:, 2 + s, :], 1.0 / w, None, ALU.mult), t)
                    for tm in list(range(half)) + list(range(T - half + 1, T)):
                        count = min(tm + half, T) - max(tm - half, 0)
                        if count != w:
                            t = VE.run(lambda e, tm=tm, count=count: e.tensor_scalar(
                                tmp[:, 2 + s, tm:tm + 1], tmp[:, 2 + s, tm:tm + 1], float(w) / count, None, ALU.mult), t)
                    t = VE.run(lambda e: e.tensor_tensor(tmp[:, 2 + s, :], tmp[:, 2 + s, :], tmp[:, s, :], ALU.subtract), t)
                    FREE["u", s] = t
                    ok["p", i] = FREE["v", s] = split_to(PAIR_P + i, tmp[:, 2 + s, :], t)

                for j in range(DT):
                    s = j % 2
                    c, hi, lo = take((0, io["mix_small"][l, j], 6 * P))
                    g = j // 2
                    outs = []
                    for kind in range(3):
                        b = get_bank()
                        if kind == 0:
                            tiles = [(hi[:, 0:P], lo[:, 0:P], PAIR_F + g, True, True)]
                            oks = lambda k: ok["f", k - PAIR_F]
                        elif kind == 2:
                            tiles = [(hi[:, P:2 * P], lo[:, P:2 * P], PAIR_P + g, True, True)]
                            oks = lambda k: ok["p", k - PAIR_P]
                        else:
                            tiles = [(hi[:, (2 + i) * P:(3 + i) * P], lo[:, (2 + i) * P:(3 + i) * P], PAIR_C + i,
                                      i == 0, i == 3) for i in range(4)]
                            oks = lambda k: ok["c", k - PAIR_C]
                        t = product(b, tiles, lambda k: g_hi[:, k, :], lambda k: g_lo[:, k, :], oks)
                        outs.append((b, t))
                    release(c, t)
                    acc = None
                    for kind in range(3):
                        b, t = column(IN_G + kind * DT + j)
                        q = (3 * j + kind) % 2
                        m = VE.run(lambda e: e.tensor_tensor(tmp[:, q, :], bank[b][:, :], rsq[:, :], ALU.mult), t,
                                   FREE.get(("u", q)))
                        bank_free[b] = m
                        m = AC.run(lambda e: e.activation(tmp[:, q, :], tmp[:, q, :], ACT.Sigmoid), m)
                        by, ty = outs[kind]
                        dst = tmp[:, 2 + s, :] if kind == 0 else tmp[:, q, :]
                        free = FREE.get(("v", s)) if kind == 0 else None
                        if kind == 2:
                            m = VE.run(lambda e: e.scalar_tensor_tensor(dst, bank[by][:, :], par("pool_scale", l * DT + j),
                                                                        tmp[:, q, :], ALU.mult, ALU.mult), m, ty)
                        else:
                            m = VE.run(lambda e: e.tensor_tensor(dst, bank[by][:, :], tmp[:, q, :], ALU.mult), m, ty, free)
                        bank_free[by] = m
                        if kind == 0:
                            acc = m
                        else:
                            acc = PO.run(lambda e: e.tensor_tensor(tmp[:, 2 + s, :], tmp[:, 2 + s, :], tmp[:, q, :],
                                                                   ALU.add), m, acc)
                        FREE["u", q] = acc
                    ok["m", j] = FREE["v", s] = split_to(PAIR_M + j, tmp[:, 2 + s, :], acc, ok["a_read"])
                for j in range(DT):
                    c, hi, lo = take((0, io["w_o"][l, j], W))
                    b = get_bank()
                    t = product(b, [(hi[:, k * P:(k + 1) * P], lo[:, k * P:(k + 1) * P], k, k == 0, k == DT - 1)
                                    for k in range(DT)], lambda k: g_hi[:, PAIR_M + k, :],
                                lambda k: g_lo[:, PAIR_M + k, :], lambda k: ok["m", k])
                    release(c, t)
                    run_later()
                    residual(j, b, t, 1.0, gain(j))

            for l in range(LAYERS):
                swiglu(l, ("w1_a", "w3_a", "w2_a"), lambda j, l=l: par("g_mix", l * DT + j))
                mixers(l, lambda j, l=l: par("g_ffn2", l * DT + j))
                swiglu(l, ("w1_b", "w3_b", "w2_b"),
                       lambda j, l=l: par("g_ffn1", (l + 1) * DT + j) if l + 1 < LAYERS else par("g_final", j))
            run_later()
            for j in range(DT):
                t = VE.run(lambda e, j=j: e.scalar_tensor_tensor(xT[:, j, :], xT[:, j, :], par("g_final", j),
                                                                 rsq[:, :], ALU.mult, ALU.mult), rs_state["ok"])
                SP.issue(lambda e, j=j: e.dma_start(io["out"][:, j, :], xT[:, j, :]).then_inc(s_out, 16), t)
            SP.wait((s_out, 16 * DT))
            return chunks

        chunks = program(None)
        block = ctx.enter_context(nc.Block())

        @block.sync
        def _(eng):
            program(chunks, "sp", eng)

        @block.scalar
        def _(eng):
            program(chunks, "act", eng)

        @block.vector
        def _(eng):
            program(chunks, "dve", eng)

        @block.gpsimd
        def _(eng):
            program(chunks, "pool", eng)

        @block.tensor
        def _(eng):
            program(chunks, "pe", eng)


POOL_EVERY = 10 ** 9


def dram_views(args):
    io = dict(args)
    for n in ("moe1", "moe3", "moe2"):
        io[n] = args[n].rearrange("(e p c) n -> e c p n", p=P, c=4)
        io[n + "_rows"] = args[n]
    return io


def lay_out(inp):
    import numpy as np

    def tiles(w):
        *lead, K, N = w.shape
        n = len(lead)
        w = w.reshape(*lead, K // P, P, N // P, P)
        w = w.transpose(*range(n), n + 2, n + 1, n, n + 3)
        return np.ascontiguousarray(w).reshape(*lead, N // P, P, K)

    def columns(v):
        return np.ascontiguousarray(v.reshape(-1, P).T)

    f = {k: np.asarray(v) for k, v in inp.items()}
    a = {}
    x = f["x"][0]
    a["x"] = np.ascontiguousarray(x.reshape(TT, P, D).transpose(1, 0, 2))
    a["xT"] = np.ascontiguousarray(x.T.reshape(DT, P, T).transpose(1, 0, 2))
    w_in = tiles(f["rec_w_in"][0])
    a["rec_in"] = np.concatenate([w_in[RT:], w_in[:RT]])
    a["rec_out"] = f["rec_w_out"][0].reshape(RT, P, D)
    bd = np.zeros((2, R, R), np.float32)
    for m, name in enumerate(("rec_w_r", "rec_w_i")):
        for n in range(LRU_BLOCKS):
            s = slice(n * LRU_W, (n + 1) * LRU_W)
            bd[m, s, s] = f[name][0, n]
    a["bd"] = np.stack([bd[m, i * P:(i + 1) * P, j * P:(j + 1) * P] for m in range(2) for i, j in BD_PAIRS], axis=1)
    groups = {"conv_w": f["rec_conv_w"][0], "conv_b": f["rec_conv_b"], "b_r": f["rec_b_r"], "b_i": f["rec_b_i"],
              "lam": f["rec_lambda"], "g_ffn1": f["g_ffn1_2"], "g_mix": f["g_mix_2"], "g_ffn2": f["g_ffn2_2"],
              "pool_scale": f["pool_scale_2"], "g_final": f["g_final_2"], "w_conv": f["w_conv_2"]}
    a["params"] = np.concatenate([columns(groups[n]) for n, _ in PARAM_GROUPS], axis=1)
    a["ln"] = np.stack([f["ln_g"][0, 0], f["ln_b"][0, 0], f["ln_g"][0, 1], f["ln_b"][0, 1]])
    a["wr"] = np.concatenate([f["moe_w_group"][0], f["moe_w_expert"][0]], axis=1) \
        .reshape(DT, P, NG + NE).transpose(1, 0, 2).copy()
    a["br"] = np.concatenate([f["moe_b_group"], f["moe_b_expert"]], axis=1)
    for name, src, kt in (("moe1", "moe_w1", DT), ("moe3", "moe_w3", DT), ("moe2", "moe_w2", FET)):
        w = f[src][0]
        a[name] = np.ascontiguousarray(w.reshape(NE, kt, P, -1).transpose(0, 2, 1, 3)).reshape(NE * P * 4, W)
    for s in ("a", "b"):
        for w in ("w1", "w3", "w2"):
            a[f"{w}_{s}"] = tiles(f[f"{w}_{s}_2"])
    a["w_in"] = tiles(f["w_in_2"])
    a["w_o"] = tiles(f["w_o_2"])
    wf, wp = ([f[n][:, j // 2, :, (j % 2) * P:(j % 2 + 1) * P] for j in range(DT)]
              for n in ("w_fourier_2", "w_pool_2"))
    small = [np.concatenate([wf[j], wp[j], tiles(f["w_conv_out_2"])[:, j]], axis=2) for j in range(DT)]
    a["mix_small"] = np.stack(small, axis=1)

    c = np.zeros((P, NCONST), np.float32)
    c[:, C_IDENT:C_IDENT + P] = np.eye(P)
    c[:, C_UPPER:C_UPPER + P] = np.triu(np.ones((P, P)), 1)
    c[:, C_IOTA:C_IOTA + P] = np.arange(P)
    c[:, C_GRANK:C_GRANK + TT * NG] = np.tile(NG - np.arange(NG), TT)
    c[:, C_ERANK:C_ERANK + TT * NE] = np.tile(NE - np.arange(NE), TT)
    c[:, C_EIDX:C_EIDX + TT * NE] = np.tile(np.arange(NE), TT)
    for k in range(2):
        for tt in range(TT):
            c[:, C_SLOT + k * TT + tt] = k * T + tt * P + np.arange(P) + 1
    c[:, C_ROW4] = 4 * np.arange(P)
    a["consts"] = c
    ang = 2 * np.pi / P * np.outer(np.arange(P), np.arange(P))
    a["dft_c"] = (np.concatenate([np.cos(ang), np.sin(ang)], axis=1) / 256.0).astype(np.float32)
    ang = 2 * np.pi / T * (np.outer(np.arange(T), np.arange(T)) % T)
    full = np.stack([np.cos(ang), -np.sin(ang)]).astype(np.float32)
    a["dft_s"] = full.reshape(2, 2, 2, P, T).transpose(0, 1, 3, 2, 4).reshape(4, P, W).copy()
    return a


def kernel(**inputs):
    import numpy as np
    import concourse.bacc as bacc
    from concourse.bass_utils import run_bass_kernel_spmd

    nc = bacc.Bacc("TRN2", target_bir_lowering=False, num_devices=1)
    arrays, args = {}, {}
    for name, a in lay_out(inputs).items():
        arrays[f"in_{name}"] = a
        args[name] = nc.dram_tensor(f"in_{name}", a.shape, mybir.dt.from_np(a.dtype), kind="ExternalInput").ap()
    args["out"] = nc.dram_tensor("out_0", (P, DT, T), F32, kind="ExternalOutput").ap()
    build(nc, dram_views(args))
    r = run_bass_kernel_spmd(nc, [arrays], core_ids=[0])
    got = r.results[0]["out_0"]
    return got.transpose(2, 1, 0).reshape(1, T, D)
```

```python
from contextlib import ExitStack

import concourse.bass as bass
from concourse import mybir

F32 = mybir.dt.float32
F32R = mybir.dt.float32r
U32 = mybir.dt.uint32
ALU = mybir.AluOpType
ACT = mybir.ActivationFunctionType
AX_X = mybir.AxisListType.X

P = 128
T = 512
D = 1024
TT = T // P
DT = D // P
R = 1280
RT = R // P
LRU_BLOCKS = 16
LRU_W = R // LRU_BLOCKS
CONV_W = 4
NG = 4
EPG = 8
NE = NG * EPG
FE = 512
FET = FE // P
FF = 2816
FFT = FF // P
LAYERS = 2
ALPHA = 2.0 ** 0.25
LN_EPS = 1e-5
RMS_EPS = 1e-6
W = 1024
EXTRA = (2 * T - NE) // P
NBLK = NE + EXTRA
BIG = 1e30

IN_F, IN_B, IN_C, IN_V, IN_P, IN_G = 0, 4, 8, 12, 16, 20
IN_TILES = 44

BD_PAIRS = [(i, j) for j in range(RT) for i in range(RT)
            if any(n * LRU_W < (i + 1) * P and (n + 1) * LRU_W > i * P
                   and n * LRU_W < (j + 1) * P and (n + 1) * LRU_W > j * P for n in range(LRU_BLOCKS))]

PARAM_GROUPS = [("conv_w", CONV_W * RT), ("conv_b", RT), ("b_r", RT), ("b_i", RT), ("lam", RT),
                ("g_ffn1", LAYERS * DT), ("g_mix", LAYERS * DT), ("g_ffn2", LAYERS * DT),
                ("pool_scale", LAYERS * DT), ("g_final", DT), ("w_conv", LAYERS * 3 * 4)]
PCOL = {}
NPAR = 0
for _name, _n in PARAM_GROUPS:
    PCOL[_name] = NPAR
    NPAR += _n

C_IDENT = 0
C_UPPER = C_IDENT + P
C_IOTA = C_UPPER + P
C_GRANK = C_IOTA + P
C_ERANK = C_GRANK + TT * NG
C_EIDX = C_ERANK + TT * NE
C_SLOT = C_EIDX + TT * NE
C_ROW4 = C_SLOT + 2 * TT
NCONST = C_ROW4 + 1


class Queue:

    def __init__(self, sem, eng=None):
        self.sem = sem
        self.eng = eng
        self.done = 0
        self.seen = {}

    def wait(self, *tokens):
        for token in tokens:
            if token is not None and self.eng is not None:
                sem, value = token
                if self.seen.get(id(sem), 0) < value:
                    self.eng.wait_ge(sem, value)
                    self.seen[id(sem)] = value

    def run(self, fn, *tokens):
        self.wait(*tokens)
        if self.eng is not None:
            fn(self.eng).then_inc(self.sem, 1)
        self.done += 1
        return (self.sem, self.done)

    def issue(self, fn, *tokens):
        self.wait(*tokens)
        if self.eng is not None:
            fn(self.eng)

    def here(self):
        return (self.sem, self.done) if self.done else None


def build(nc, io):
    with ExitStack() as ctx:
        def sb(name, shape, dt=F32, into=None):
            return (into or ctx).enter_context(nc.sbuf_tensor(name, shape, dt))

        def sem(name):
            return ctx.enter_context(nc.semaphore(name))

        s_pe, s_act, s_dve, s_pool = (sem(n) for n in ("s_pe", "s_act", "s_dve", "s_pool"))
        o_pe, o_act, o_dve, o_pool = (sem(n) for n in ("o_pe", "o_act", "o_dve", "o_pool"))
        NRAW, NMORE, NSPLIT = 5, 11, 3
        s_raw = [sem(f"s_raw{i}") for i in range(NRAW + NMORE)]
        s_par, s_x, s_bd, s_router, s_x1, s_out = (
            sem(n) for n in ("s_par", "s_x", "s_bd", "s_router", "s_x1", "s_out"))
        s_xt = [sem(f"s_xt{i}") for i in range(4)]
        s_gb = [sem(f"s_gb{i}") for i in range(4)]
        s_gather = [sem(f"s_gather{i}") for i in range(3)]
        s_scatter = [sem(f"s_scatter{i}") for i in range(3)]
        s_ys = [sem(f"s_ys{i}") for i in range(4)]
        o_weight, o_rows, o_store = sem("o_weight"), sem("o_rows"), sem("o_store")

        bank = [ctx.enter_context(nc.psum_tensor(f"bank{i}", [P, 512], F32)) for i in range(8)]
        raw = sb("raw", [P, NRAW, W])
        w_hi = sb("w_hi", [P, NSPLIT, W], F32R)
        w_lo = sb("w_lo", [P, NSPLIT, W], F32R)
        params = sb("params", [P, NPAR])
        consts = sb("consts", [P, NCONST])
        ones = sb("ones", [P, P])

        with ExitStack() as first:
            x_tok = sb("x_tok", [P, TT, D], into=first)
            with ExitStack() as rec:
                xc = sb("xc", [P, RT, T], into=rec)
                bd = sb("bd", [P, 2 * len(BD_PAIRS), P], into=rec)
                x_hi = sb("x_hi", [P, RT, T], F32R, rec)
                x_lo = sb("x_lo", [P, RT, T], F32R, rec)
                gate = sb("gate", [P, 2, T], into=rec)
                hs = sb("hs", [P, RT, T], into=rec)
                xrp = sb("xrp", [P, 2, T + CONV_W - 1], into=rec)
                rg = sb("rg", [P, 2, T], into=rec)
                ig = sb("ig", [P, 2, T], into=rec)
                th = sb("th", [P, 2, T], into=rec)
                av = sb("av", [P, 2, T], into=rec)
                mv = sb("mv", [P, 2, T], into=rec)
                lamw = sb("lamw", [P, 8, RT], into=rec)
            with ExitStack() as moe:
                raw_more = sb("raw_more", [P, NMORE, W], into=moe)
                gb = sb("gb", [P, 2, D], into=moe)
                st = sb("st", [P, TT, 20], into=moe)
                wr = sb("wr", [P, DT, NG + NE], into=moe)
                br = sb("br", [1, NG + NE], into=moe)
                lg = sb("lg", [P, TT, NG + NE], into=moe)
                rt = sb("rt", [P, 16, TT, NE], into=moe)
                sm = sb("sm", [P, 32, TT], into=moe)
                place = sb("place", [P, 8, 2 * TT], into=moe)
                oneh = sb("oneh", [P, 2 * TT, P], into=moe)
                blkh = sb("blkh", [P, 2 * TT, NBLK], into=moe)
                tabs = sb("tabs", [P, 4, NBLK], into=moe)
                gidx = sb("gidx", [P, NBLK], U32, moe)
                sidx = sb("sidx", [P, NBLK], U32, moe)
                wix = sb("wix", [P, EXTRA, 4], into=moe)
                widx = sb("widx", [P, EXTRA, 4], U32, moe)
                cnt = sb("cnt", [P, 1], U32, moe)
                sil = sb("sil", [P, 2, FE], into=moe)
                hd = sb("hd", [P, 2, FE], into=moe)
                hT_hi = sb("hT_hi", [P, 2, FE], F32R, moe)
                hT_lo = sb("hT_lo", [P, 2, FE], F32R, moe)
                with ExitStack() as experts:
                    with ExitStack() as router:
                        x1T = sb("x1T", [P, DT, T], into=router)
                    with ExitStack() as branch_only:
                        o_raw = sb("o_raw", [P, W], into=branch_only)
                        o_hi = sb("o_hi", [P, W], F32R, branch_only)
                        o_lo = sb("o_lo", [P, W], F32R, branch_only)
                        sb("o_pad", [P, W], into=branch_only)
                        xe = sb("xe", [P, 3, D], into=branch_only)
                        ye = sb("ye", [P, 3, D], into=branch_only)
                        xeT_hi = sb("xeT_hi", [P, 2, D], F32R, branch_only)
                        xeT_lo = sb("xeT_lo", [P, 2, D], F32R, branch_only)
                with ExitStack() as combine:
                    ysl = sb("ysl", [P, 2 * TT, D], into=combine)
        g_hi = sb("g_hi", [P, FFT, T], F32R)
        g_lo = sb("g_lo", [P, FFT, T], F32R)
        xT = sb("xT", [P, DT, T])
        xg_hi = sb("xg_hi", [P, DT, T], F32R)
        xg_lo = sb("xg_lo", [P, DT, T], F32R)
        tmp = sb("tmp", [P, 8, T])
        rsq = sb("rsq", [P, T])
        zc = sb("zc", [P, 2, T + 16])

        x1_dram = nc.dram_tensor("x1_rows", (T, D), F32, kind="Internal").ap()
        ys_dram = nc.dram_tensor("y_rows", (2 * T, D), F32, kind="Internal").ap()

        ident = consts[:, C_IDENT:C_IDENT + P]
        upper = consts[:, C_UPPER:C_UPPER + P]
        iota = consts[:, C_IOTA:C_IOTA + P]

        def par(name, k=0):
            c = PCOL[name] + k
            return params[:, c:c + 1]

        def program(known, walk=None, eng=None):
            chunks = []
            PE, AC, VE, PO, SP = (Queue(q, eng if walk == n else None) for n, q in
                                  (("pe", s_pe), ("act", s_act), ("dve", s_dve), ("pool", s_pool), ("sp", None)))

            split = []
            used = []
            slots = []
            owner = {}
            landed = [0] * (NRAW + NMORE)
            LOOK = NSPLIT - 1
            more_free = []

            def raw_slot(i, n):
                return raw[:, i, 0:n] if i < NRAW else raw_more[:, i - NRAW, 0:n]

            def load_ready():
                while len(slots) < len(known):
                    c = len(slots)
                    far = known[c][0] == "expert"
                    if far and not more_free:
                        return
                    i = min(range(NRAW + NMORE if far else NRAW), key=lambda i: owner.get(i, -1))
                    if i in owner:
                        if owner[i] >= len(split):
                            return
                        SP.wait(split[owner[i]])
                    elif i >= NRAW:
                        SP.wait(*more_free)
                    owner[i] = c
                    slots.append((i, landed[i] + 16 * (len(known[c]) - 1)))
                    landed[i] = slots[c][1]
                    for col, src, width in known[c][1:]:
                        SP.issue(lambda e: e.dma_start(raw_slot(i, W)[:, col:col + width], src)
                                 .then_inc(s_raw[i], 16))

            def convert(c):
                load_ready()
                i, value = slots[c]
                _, *parts = known[c]
                n = parts[-1][0] + parts[-1][2]
                free = used[c - NSPLIT] if c >= NSPLIT else None
                hi = w_hi[:, c % NSPLIT, 0:n]
                lo = w_lo[:, c % NSPLIT, 0:n]
                src = raw_slot(i, n)
                high = AC.run(lambda e: e.activation(hi, src, ACT.Copy), (s_raw[i], value), free)
                on = PO if known[c][0] == "recurrent" and c % 3 == 2 else VE
                split.append(on.run(lambda e: e.tensor_tensor(lo, src, hi.bitcast(F32), ALU.subtract), high, free))
                load_ready()

            def take(kind, *parts):
                c = len(chunks)
                chunks.append((kind, *parts))
                if known is not None:
                    while len(split) < min(c + LOOK + 1, len(known)):
                        convert(len(split))
                    PE.wait(split[c])
                return c, w_hi[:, c % NSPLIT, :], w_lo[:, c % NSPLIT, :]

            def release(c, token):
                used.append(token)

            RING = 7
            bank_free = [None] * 8
            turn = [0]

            def get_bank():
                b = turn[0] % RING
                turn[0] += 1
                PE.wait(bank_free[b])
                return b

            def mm3(out, a_hi, a_lo, b_hi, b_lo, start, stop):
                PE.issue(lambda e: e.matmul(out, a_lo, b_hi, start=start, stop=False))
                PE.issue(lambda e: e.matmul(out, a_hi, b_lo, start=False, stop=False))
                last = lambda e: e.matmul(out, a_hi, b_hi, start=False, stop=stop)
                return last

            later = []

            def run_later():
                todo, later[:] = list(later), []
                for fn in todo:
                    fn()

            if known is not None:
                load_ready()
            for n in range(4):
                AC.issue(lambda e: e.dma_start(hs[:, 2 * n:2 * n + 2, :], io["xT"][:, 2 * n:2 * n + 2, :])
                         .then_inc(s_xt[n], 16))
            AC.issue(lambda e: e.dma_start(params[:, :], io["params"]).then_inc(s_par, 16))
            AC.issue(lambda e: e.dma_start(consts[:, :], io["consts"]).then_inc(s_par, 16))
            par_in, bd_in, x_in = (s_par, 32), (s_bd, 16), (s_x, 16)
            pad_ready = VE.run(lambda e: e.memset(xrp[:, :, 0:CONV_W - 1], 0.0))
            ones_ready = VE.run(lambda e: e.memset(ones[:, :], 1.0))

            x_split = []
            for k in range(DT):
                a = AC.run(lambda e: e.activation(x_hi[:, k, :], hs[:, k, :], ACT.Copy), (s_xt[k // 2], 16))
                x_split.append(VE.run(lambda e: e.tensor_tensor(
                    x_lo[:, k, :], hs[:, k, :], x_hi[:, k, :].bitcast(F32), ALU.subtract), a))

            def late_loads():
                AC.issue(lambda e: e.dma_start(bd[:, :, :], io["bd"]).then_inc(s_bd, 16))
                AC.issue(lambda e: e.dma_start(x_tok[:, :, :], io["x"]).then_inc(s_x, 16))

            lam = params[:, PCOL["lam"]:PCOL["lam"] + RT]
            L = [lamw[:, i, :] for i in range(8)]
            t = AC.run(lambda e: e.activation(L[0], lam, ACT.Abs), par_in)
            t = AC.run(lambda e: e.activation(L[1], L[0], ACT.Exp, scale=-1.0), t)
            t = VE.run(lambda e: e.tensor_scalar(L[2], L[1], 2.0, None, ALU.add), t)
            t = VE.run(lambda e: e.reciprocal(L[3], L[2]), t)
            t = VE.run(lambda e: e.tensor_tensor(L[2], L[1], L[3], ALU.mult), t)
            t = VE.run(lambda e: e.tensor_tensor(L[3], L[2], L[2], ALU.mult), t)
            t = VE.run(lambda e: e.tensor_scalar(L[4], L[3], 1.0 / 17, 1.0 / 15, ALU.mult, ALU.add), t)
            for n in (13, 11, 9, 7, 5, 3, 1):
                t = VE.run(lambda e: e.tensor_tensor(L[5], L[4], L[3], ALU.mult), t)
                t = VE.run(lambda e, n=n: e.tensor_scalar(L[4], L[5], 1.0 / n, None, ALU.add), t)
            t = VE.run(lambda e: e.tensor_tensor(L[5], L[4], L[2], ALU.mult), t)
            t = VE.run(lambda e: e.tensor_scalar(L[6], lam, -1.0, 0.0, ALU.mult, ALU.max), t, par_in)
            t = VE.run(lambda e: e.tensor_scalar(L[6], L[6], 4.0, None, ALU.mult), t)
            c4_ready = VE.run(lambda e: e.scalar_tensor_tensor(L[7], L[5], 8.0, L[6], ALU.mult, ALU.add), t)
            c4 = L[7]

            def in_tile(j):
                c, hi, lo = take("recurrent", (0, io["rec_in"][j], W))
                b = get_bank()
                for k in range(DT):
                    if j == 0:
                        PE.wait(x_split[k])
                    f = mm3(bank[b][:, :], hi[:, k * P:(k + 1) * P], lo[:, k * P:(k + 1) * P],
                            x_hi[:, k, :], x_lo[:, k, :], k == 0, k == DT - 1)
                    if k < DT - 1:
                        PE.issue(f)
                token = PE.run(f)
                release(c, token)
                return b, token

            xc_ready = [None] * RT
            gates_read = [None] * RT

            def conv(j, b, token):
                copied = AC.run(lambda e: e.activation(xrp[:, j % 2, CONV_W - 1:], bank[b][:, :], ACT.Copy),
                                token, pad_ready, xc_ready[j - 2] if j >= 2 else None)
                bank_free[b] = copied
                t = VE.run(lambda e: e.tensor_scalar(xc[:, j, :], xrp[:, j % 2, 0:T], par("conv_w", j),
                                                     par("conv_b", j), ALU.mult, ALU.add), copied, par_in)
                for k in range(1, CONV_W):
                    t = VE.run(lambda e, k=k: e.scalar_tensor_tensor(
                        xc[:, j, :], xrp[:, j % 2, k:k + T], par("conv_w", k * RT + j), xc[:, j, :],
                        ALU.mult, ALU.add), t)
                xc_ready[j] = t

            h_ready = [None] * RT
            rg_read, ig_read, th_read, av_read, mv_read = ([None] * RT for _ in range(5))

            def recur(j):
                s = j % 2
                old = j - 2 if j >= 2 else None
                past = lambda lst: lst[old] if old is not None else None
                PE.wait(bd_in)
                banks = []
                for m in range(2):
                    b = get_bank()
                    pairs = [n for n, (_, jj) in enumerate(BD_PAIRS) if jj == j]
                    for n in pairs:
                        i = BD_PAIRS[n][0]
                        PE.wait(xc_ready[i])
                        f = lambda e, n=n, i=i, b=b, m=m, pairs=pairs: e.matmul(
                            bank[b][:, :], bd[:, m * len(BD_PAIRS) + n, :], xc[:, i, :],
                            start=n == pairs[0], stop=n == pairs[-1])
                        if n != pairs[-1]:
                            PE.issue(f)
                    banks.append((b, PE.run(f)))
                (b_r, r_done), (b_i, i_done) = banks
                r_ok = AC.run(lambda e: e.activation(rg[:, s, :], bank[b_r][:, :], ACT.Sigmoid,
                                                     bias=par("b_r", j)), r_done, par_in, past(rg_read))
                bank_free[b_r] = r_ok
                i_ok = AC.run(lambda e: e.activation(ig[:, s, :], bank[b_i][:, :], ACT.Sigmoid,
                                                     bias=par("b_i", j)), i_done, past(ig_read))
                bank_free[b_i] = i_ok
                th_ok = AC.run(lambda e: e.activation(th[:, s, :], rg[:, s, :], ACT.Tanh,
                                                      scale=c4[:, j:j + 1]), r_ok, c4_ready, past(th_read))
                rg_read[j] = th_ok
                ix = PO.run(lambda e: e.tensor_tensor(ig[:, s, :], ig[:, s, :], xc[:, j, :], ALU.mult),
                            i_ok, xc_ready[j])
                t = VE.run(lambda e: e.tensor_scalar(av[:, s, :], th[:, s, :], 1.0, None, ALU.add), th_ok)
                t = VE.run(lambda e: e.reciprocal(mv[:, s, :], av[:, s, :]), t, past(mv_read))
                q = VE.run(lambda e: e.tensor_tensor(th[:, s, :], th[:, s, :], mv[:, s, :], ALU.mult), t)
                a_ok = VE.run(lambda e: e.tensor_scalar(av[:, s, :], th[:, s, :], -2.0, 1.0,
                                                        ALU.mult, ALU.add), q)
                t = VE.run(lambda e: e.scalar_tensor_tensor(mv[:, s, :], th[:, s, :], 1.0, th[:, s, :],
                                                            ALU.subtract, ALU.mult), a_ok)
                th_read[j] = t
                root = AC.run(lambda e: e.activation(mv[:, s, :], mv[:, s, :], ACT.Sqrt, scale=-4.0), t)

                def scan():
                    u = VE.run(lambda e: e.tensor_tensor(ig[:, s, :], mv[:, s, :], ig[:, s, :], ALU.mult),
                               root, ix)
                    mv_read[j] = u
                    h_ready[j] = VE.run(lambda e: e.tensor_tensor_scan(
                        hs[:, j, :], av[:, s, :], ig[:, s, :], 0.0, ALU.mult, ALU.add), u)
                    ig_read[j] = av_read[j] = h_ready[j]
                return scan

            pend = []
            for j in range(RT):
                b, token = in_tile(j)
                conv(j, b, token)
                if j == 0:
                    late_loads()
                if j >= 2:
                    pend.append(recur(j - 2))
                    if len(pend) > 1:
                        pend.pop(0)()
            rest = list(range(RT - 2, RT))
            y_ready = [None] * RT
            for j in range(RT):
                b, token = in_tile(RT + j)
                if rest:
                    pend.append(recur(rest.pop(0)))
                if pend:
                    pend.pop(0)()
                g_ok = AC.run(lambda e, j=j, b=b: e.activation(gate[:, j % 2, :], bank[b][:, :],
                                                               ACT.Gelu_apprx_tanh),
                              token, y_ready[j - 2] if j >= 2 else None)
                bank_free[b] = g_ok
                while h_ready[j] is None:
                    pend.pop(0)()
                y_ready[j] = VE.run(lambda e, j=j: e.tensor_tensor(hs[:, j, :], hs[:, j, :], gate[:, j % 2, :],
                                                                   ALU.mult), g_ok)
            x_free = token
            more_free += [token, VE.here(), PO.here(), AC.here()]
            y_split = []
            for j in range(RT):
                a = AC.run(lambda e, j=j: e.activation(x_hi[:, j, :], hs[:, j, :], ACT.Copy), y_ready[j], x_free)
                y_split.append(VE.run(lambda e, j=j: e.tensor_tensor(
                    x_lo[:, j, :], hs[:, j, :], x_hi[:, j, :].bitcast(F32), ALU.subtract), a))

            out_banks = [(get_bank() if n < RING else 7) for n in range(8)]
            for k in range(RT):
                c, hi, lo = take("recurrent", (0, io["rec_out"][k], W))
                PE.wait(y_split[k])
                done = []
                for tt in range(TT):
                    for half in range(2):
                        f = mm3(bank[out_banks[2 * tt + half]][:, :], x_hi[:, k, tt * P:(tt + 1) * P],
                                x_lo[:, k, tt * P:(tt + 1) * P], hi[:, half * T:(half + 1) * T],
                                lo[:, half * T:(half + 1) * T], k == 0, k == RT - 1)
                        done.append(PE.run(f))
                release(c, done[-1])
            rec_done = done[-1]

            def load_gains(which, *free):
                for n in range(2):
                    AC.issue(lambda e: e.dma_start(gb[:, n, :], io["ln"][2 * which + n:2 * which + n + 1, :]
                                                   .partition_broadcast(P)).then_inc(s_gb[2 * which + n], 16), *free)

            def statistics(tt, z_ok):
                x = x_tok[:, tt, :]
                for h in range(2):
                    t = VE.run(lambda e: e.bn_stats(st[:, tt, h * 6:h * 6 + 6], x[:, h * T:(h + 1) * T]), z_ok)
                t = VE.run(lambda e: e.bn_aggr(st[:, tt, 12:14], st[:, tt, 0:12]), t)
                t = VE.run(lambda e: e.tensor_scalar(st[:, tt, 14:15], st[:, tt, 13:14], LN_EPS, None, ALU.add), t)
                return AC.run(lambda e: e.activation(st[:, tt, 15:16], st[:, tt, 14:15], ACT.Sqrt), t)

            def normalise(tt, which, root):
                x = x_tok[:, tt, :]
                r = VE.run(lambda e: e.reciprocal(st[:, tt, 16:17], st[:, tt, 15:16]), root)
                t = VE.run(lambda e: e.scalar_tensor_tensor(x, x, st[:, tt, 12:13], gb[:, 0, :], ALU.subtract, ALU.mult),
                           root, (s_gb[2 * which], 16))
                t = AC.run(lambda e: e.activation(x, x, ACT.Copy, scale=st[:, tt, 16:17]), t, r)
                on = VE if tt == TT - 1 else PO
                return on.run(lambda e: e.tensor_tensor(x, x, gb[:, 1, :], ALU.add), t, (s_gb[2 * which + 1], 16))

            def layer_norm(which, z_of, then):
                roots, oks = [], []
                for tt in range(TT + 1):
                    if tt < TT:
                        roots.append(statistics(tt, z_of(tt)))
                    if tt >= 1:
                        oks.append(normalise(tt - 1, which, roots[tt - 1]))
                        then(tt - 1, oks[-1])
                return oks

            load_gains(0, x_free)

            def first_sum(tt):
                for half in range(2):
                    b = out_banks[2 * tt + half]
                    x = x_tok[:, tt, half * T:(half + 1) * T]
                    t = VE.run(lambda e: e.scalar_tensor_tensor(x, x, ALPHA, bank[b][:, :], ALU.mult, ALU.add),
                               done[2 * tt + half], x_in)
                    bank_free[b] = t
                return t

            x1_ok = layer_norm(0, first_sum, lambda tt, ok: PO.issue(
                lambda e: e.dma_start(x1_dram[tt * P:(tt + 1) * P, :], x_tok[:, tt, :]).then_inc(s_x1, 16), ok))

            def transpose4(src, b, ok):
                PE.wait(ok, par_in)
                for n in range(4):
                    f = lambda e, n=n: e.transpose(bank[b][:, n * P:(n + 1) * P], src(n), ident)
                    if n < 3:
                        PE.issue(f)
                return PE.run(f)

            AC.issue(lambda e: e.dma_start(wr[:, :, :], io["wr"]).then_inc(s_router, 16), x_free)
            AC.issue(lambda e: e.dma_start(br[:, :], io["br"]).then_inc(s_router, 16))
            x1T_ok = []
            for tt in range(TT):
                for half in range(2):
                    b = get_bank()
                    t = transpose4(lambda n, tt=tt, half=half: x_tok[:, tt, (4 * half + n) * P:(4 * half + n + 1) * P],
                                   b, x1_ok[tt])
                    t = AC.run(lambda e, b=b, tt=tt, half=half: e.activation(
                        x1T[:, 4 * half:4 * half + 4, tt * P:(tt + 1) * P],
                        bank[b][:, :].rearrange("p (n q) -> p n q", n=4), ACT.Copy), t)
                    bank_free[b] = t
                x1T_ok.append(t)
            lg_bank = get_bank()
            PE.wait((s_router, 32), ones_ready)
            for tt in range(TT):
                o = bank[lg_bank][:, tt * (NG + NE):(tt + 1) * (NG + NE)]
                PE.wait(x1T_ok[tt])
                for k in range(DT):
                    PE.issue(lambda e, o=o, k=k, tt=tt: e.matmul(o, x1T[:, k, tt * P:(tt + 1) * P], wr[:, k, :],
                                                                 start=k == 0, stop=False))
                t = PE.run(lambda e, o=o: e.matmul(o, ones[0:1, :], br[0:1, :], start=False, stop=True))
            t = VE.run(lambda e: e.tensor_copy(lg[:, :, :], bank[lg_bank][:, 0:TT * (NG + NE)]
                                               .rearrange("p (a n) -> p a n", a=TT)), t)
            bank_free[lg_bank] = lg_ok = t

            S = lambda n: sm[:, n, :]
            Rt = lambda n: rt[:, n, :, :]
            wide = lambda ap: ap.unsqueeze(2).to_broadcast([P, TT, NE])
            V = lambda fn, *w: VE.run(fn, *w)

            def tt_(o, a, b, op, *w):
                return V(lambda e: e.tensor_tensor(o, a, b, op), *w)

            def ts_(o, a, s1, s2, op0, op1=None, *w):
                if op1 is None:
                    return V(lambda e: e.tensor_scalar(o, a, s1, None, op0), *w)
                return V(lambda e: e.tensor_scalar(o, a, s1, s2, op0, op1), *w)

            grank = consts[:, C_GRANK:C_GRANK + TT * NG].rearrange("p (a n) -> p a n", a=TT)
            erank = consts[:, C_ERANK:C_ERANK + TT * NE].rearrange("p (a n) -> p a n", a=TT)
            eidx = consts[:, C_EIDX:C_EIDX + TT * NE].rearrange("p (a n) -> p a n", a=TT)
            gl = lg[:, :, 0:NG]
            el = lg[:, :, NG:NG + NE]
            G = lambda n: rt[:, n, :, 0:NG]
            gwide = lambda ap: ap.unsqueeze(2).to_broadcast([P, TT, NG])

            t = V(lambda e: e.tensor_reduce(S(0), gl, AX_X, ALU.max), t)
            t = tt_(G(0), gl, gwide(S(0)), ALU.is_equal, t)
            t = tt_(G(1), G(0), grank, ALU.mult, t)
            t = V(lambda e: e.tensor_reduce(S(1), G(1), AX_X, ALU.max), t)
            t = tt_(G(2), G(1), gwide(S(1)), ALU.is_equal, t)
            t = ts_(G(5), G(2), 1.0, BIG, ALU.subtract, ALU.mult, t)
            em = Rt(6)
            t = tt_(em.rearrange("p a (g n) -> p a g n", g=NG), el.rearrange("p a (g n) -> p a g n", g=NG),
                    G(5).unsqueeze(3).to_broadcast([P, TT, NG, EPG]), ALU.add, t)

            def largest(vals, value, onehot, scratch, t):
                t = V(lambda e: e.tensor_reduce(value, vals, AX_X, ALU.max), t)
                t = tt_(scratch, vals, wide(value), ALU.is_equal, t)
                t = tt_(scratch, scratch, erank, ALU.mult, t)
                t = V(lambda e: e.tensor_reduce(S(4), scratch, AX_X, ALU.max), t)
                return tt_(onehot, scratch, wide(S(4)), ALU.is_equal, t)

            t = largest(em, S(5), Rt(7), Rt(0), t)
            t = V(lambda e: e.scalar_tensor_tensor(
                rt[:, 9, :, :].rearrange("p a n -> p (a n)"), rt[:, 7, :, :].rearrange("p a n -> p (a n)"),
                -4.0 * BIG, rt[:, 6, :, :].rearrange("p a n -> p (a n)"), ALU.mult, ALU.add), t)
            t = largest(Rt(9), S(6), Rt(8), Rt(0), t)
            sel_ok = tt_(Rt(10), Rt(7), Rt(8), ALU.add, t)

            t2 = tt_(G(3), gl, gwide(S(0)), ALU.subtract)
            t3 = tt_(S(7), S(6), S(5), ALU.subtract, sel_ok)
            e2 = AC.run(lambda e: e.activation(G(4), G(3), ACT.Exp), t2)
            e3 = AC.run(lambda e: e.activation(S(8), S(7), ACT.Exp), t3)

            def gates():
                t2 = V(lambda e: e.tensor_reduce(S(2), G(4), AX_X, ALU.add), e2)
                t2 = V(lambda e: e.reciprocal(S(3), S(2)), t2)
                t3 = ts_(S(9), S(8), 1.0, None, ALU.add, None, e3)
                t3 = V(lambda e: e.reciprocal(S(10), S(9)), t3)
                t3 = tt_(S(11), S(10), S(3), ALU.mult, t3, t2)
                return tt_(S(12), S(11), S(8), ALU.mult, t3)

            rk_bank = get_bank()
            PE.wait(sel_ok)
            for tt in range(TT + 1):
                o = bank[rk_bank][:, tt * NE:(tt + 1) * NE]
                terms = [(ones[:, :], a) for a in range(min(tt, TT))] + ([(upper, tt)] if tt < TT else [])
                for n, (m, a) in enumerate(terms):
                    f = lambda e, o=o, m=m, a=a, n=n, k=len(terms): e.matmul(
                        o, m, rt[:, 10, a, :], start=n == 0, stop=n == k - 1)
                    if not (tt == TT and n == len(terms) - 1):
                        PE.issue(f)
            t = PE.run(f)
            t = V(lambda e: e.tensor_copy(rt[:, 11:13, :, :].rearrange("p k a n -> p (k a n)")[:, 0:(TT + 1) * NE],
                                          bank[rk_bank][:, 0:(TT + 1) * NE]), t)
            bank_free[rk_bank] = t
            counts = rt[:, 12, 0, :]
            C = lambda n: rt[:, 12, n, :]
            D_ = lambda n: rt[:, 13, n, :]
            u = ts_(C(1), counts, float(P), None, ALU.is_gt, None, t)
            for m in (2, 3):
                u = V(lambda e: e.scalar_tensor_tensor(C(1), counts, float(m * P), C(1), ALU.is_gt, ALU.add), u)
            one = V(lambda e: e.memset(D_(0), 1.0))
            u = V(lambda e: e.tensor_tensor_scan(C(3), D_(0), C(1), 0.0, ALU.mult, ALU.add), u, one)
            u = tt_(D_(1), C(3), C(1), ALU.subtract, u)

            pair = rt[:, 0:2, :, :].rearrange("p k a n -> p (k a) n")
            pick = rt[:, 7:9, :, :]
            RANK, EXP, START, BLOCK, MORE = (place[:, n, :] for n in range(5))
            flat = lambda ap: ap.rearrange("p k a n -> p k (a n)")
            both = lambda ap: ap.rearrange("p a n -> p (a n)").unsqueeze(1).to_broadcast([P, 2, TT * NE])
            every = lambda ap: ap.unsqueeze(1).to_broadcast([P, 2 * TT, NE])
            t = tt_(flat(rt[:, 0:2, :, :]), flat(pick), both(Rt(11)), ALU.mult, t)
            t = V(lambda e: e.tensor_reduce(RANK, pair, AX_X, ALU.add), t)
            w1 = tt_(flat(rt[:, 0:2, :, :]), flat(pick), both(eidx), ALU.mult, t)
            w1 = V(lambda e: e.tensor_reduce(EXP, pair, AX_X, ALU.add), w1)
            w1 = tt_(pair, pick.rearrange("p k a n -> p (k a) n"), every(D_(1)), ALU.mult, w1, u)
            w1 = V(lambda e: e.tensor_reduce(START, pair, AX_X, ALU.add), w1)
            t = ts_(BLOCK, RANK, float(P) - 0.5, None, ALU.is_gt, None, t)
            for m in (2, 3):
                t = V(lambda e: e.scalar_tensor_tensor(BLOCK, RANK, float(m * P) - 0.5, BLOCK, ALU.is_gt, ALU.add), t)
            t = V(lambda e: e.scalar_tensor_tensor(RANK, BLOCK, -float(P), RANK, ALU.mult, ALU.add), t)
            t = V(lambda e: e.scalar_tensor_tensor(START, START, float(NE - 1), BLOCK, ALU.add, ALU.add), t, w1)
            t = tt_(START, START, EXP, ALU.subtract, t)
            t = V(lambda e: e.scalar_tensor_tensor(START, BLOCK, 0.5, START, ALU.is_gt, ALU.mult), t)
            t = tt_(EXP, EXP, START, ALU.add, t)
            oneh_ok = []
            for n in range(2 * TT):
                V(lambda e: e.tensor_scalar(oneh[:, n, :], iota, place[:, 0, n:n + 1], None, ALU.is_equal), t)
                oneh_ok.append(V(lambda e: e.tensor_scalar(
                    blkh[:, n, :], iota[:, 0:NBLK], place[:, 1, n:n + 1],
                    consts[:, C_SLOT + n:C_SLOT + n + 1], ALU.is_equal, ALU.mult), t))
            tb_bank = get_bank()
            for n in range(2 * TT):
                PE.wait(oneh_ok[n])
                f = lambda e, n=n: e.matmul(bank[tb_bank][:, 0:NBLK], oneh[:, n, :], blkh[:, n, :],
                                            start=n == 0, stop=n == 2 * TT - 1)
                if n < 2 * TT - 1:
                    PE.issue(f)
            t = PE.run(f)
            Tb = lambda n: tabs[:, n, :]
            t = V(lambda e: e.tensor_scalar(Tb(0), bank[tb_bank][:, 0:NBLK], 1.0, None, ALU.subtract), t)
            bank_free[tb_bank] = t
            t = ts_(Tb(1), Tb(0), 0.0, float(8 * T), ALU.is_lt, ALU.mult, t)
            t = tt_(Tb(2), Tb(0), Tb(1), ALU.add, t)
            t = V(lambda e: e.tensor_copy(sidx[:, :], Tb(2)), t)
            t = ts_(Tb(1), Tb(2), float(T) - 0.5, -float(T), ALU.is_gt, ALU.mult, t)
            t = tt_(Tb(3), Tb(2), Tb(1), ALU.add, t)
            idx_ok = V(lambda e: e.tensor_copy(gidx[:, :], Tb(3)), t)
            xe_clear = PO.run(lambda e: e.memset(xe[:, :, :], 0.0), rec_done)
            gates_ok = gates()
            t = V(lambda e: e.tensor_copy(cnt[:, :], C(3)[:, NE - 1:NE]))
            for j in range(EXTRA):
                t = V(lambda e: e.tensor_scalar(D_(2), C(3), float(j) + 0.5, None, ALU.is_lt), t)
                t = V(lambda e: e.tensor_reduce(sm[:, 30, 0:1], D_(2), AX_X, ALU.add), t)
                t = V(lambda e: e.tensor_scalar(sm[:, 31, 0:1], sm[:, 30, 0:1], float(4 * P),
                                                consts[:, C_ROW4:C_ROW4 + 1], ALU.mult, ALU.add), t)
                for q in range(4):
                    u = V(lambda e: e.tensor_scalar(wix[:, j, q:q + 1], sm[:, 31, 0:1], float(q), None, ALU.add), t)
            cnt_ok = V(lambda e: e.tensor_copy(widx[:, :, :], wix[:, :, :]), u)
            for tt in range(TT):
                PO.run(lambda e: e.tensor_scalar(x_tok[:, tt, :], x_tok[:, tt, :], ALPHA, 1.0, ALU.mult, ALU.mult),
                       (s_x1, 16 * TT), PE.here())
            alpha_ok = PO.here()
            load_gains(1, x1_ok[TT - 1], x1_ok[TT - 2])

            gathers = [0, 0, 0]
            scatters = [0, 0, 0]
            xe_read = {}

            def gather(n):
                s = n % 3
                gathers[s] += 16
                PO.issue(lambda e: e.indirect_dma_start(
                    xe[:, s, :], None, x1_dram, bass.IndirectOffsetOnAxis(ap=gidx[:, n:n + 1], axis=0),
                    bounds_check=T - 1, oob_is_err=False).then_inc(s_gather[s], 16),
                    idx_ok, xe_clear, lg_ok, (s_x1, 16 * TT), xe_read.get(n - 3))

            xeT_ok, xeT_read, hd_ok, hT_ok, sil_read, hd_read, hT_read = {}, {}, {}, {}, {}, {}, {}

            def x_turn(n):
                s = n % 2
                oks = []
                for half in range(2):
                    b = get_bank()
                    t = transpose4(lambda q, half=half: xe[:, n % 3, (4 * half + q) * P:(4 * half + q + 1) * P],
                                   b, (s_gather[n % 3], 16 * (n // 3 + 1)))
                    xe_read[n] = t
                    o = slice(half * T, (half + 1) * T)
                    hi = AC.run(lambda e, o=o, b=b: e.activation(xeT_hi[:, s, o], bank[b][:, :], ACT.Copy),
                                t, xeT_read.get(n - 2))
                    lo = VE.run(lambda e, o=o, b=b: e.tensor_tensor(xeT_lo[:, s, o], bank[b][:, :],
                                                                    xeT_hi[:, s, o].bitcast(F32), ALU.subtract),
                                hi, xeT_read.get(n - 2))
                    bank_free[b] = lo
                xeT_ok[n] = lo

            def up(n):
                s = n % 2
                toks = []
                for m, name in enumerate(("moe1", "moe3")):
                    b = get_bank()
                    for q in range(4):
                        c, hi, lo = take("expert", (0, io[name][n, q], W))
                        PE.wait(xeT_ok.get(n))
                        for kk in range(2):
                            k = 2 * q + kk
                            f = mm3(bank[b][:, :], xeT_hi[:, s, k * P:(k + 1) * P], xeT_lo[:, s, k * P:(k + 1) * P],
                                    hi[:, kk * FE:(kk + 1) * FE], lo[:, kk * FE:(kk + 1) * FE], k == 0, k == DT - 1)
                            if kk == 0:
                                PE.issue(f)
                        t = PE.run(f)
                        release(c, t)
                        if m == 1 and q == 1 and n + 1 < NE:
                            x_turn(n + 1)
                    if m == 0:
                        sil_ok = AC.run(lambda e, b=b: e.activation(sil[:, s, :], bank[b][:, :], ACT.Silu),
                                        t, sil_read.get(n - 2))
                        bank_free[b] = sil_ok
                    else:
                        hd_ok[n] = VE.run(lambda e, b=b: e.tensor_tensor(hd[:, s, :], sil[:, s, :], bank[b][:, :],
                                                                         ALU.mult), t, sil_ok, hd_read.get(n - 2))
                        sil_read[n] = bank_free[b] = hd_ok[n]
                xeT_read[n] = t

            def h_turn(n):
                s = n % 2
                b = get_bank()
                t = transpose4(lambda q: hd[:, s, q * P:(q + 1) * P], b, hd_ok[n])
                hd_read[n] = t
                hi = AC.run(lambda e: e.activation(hT_hi[:, s, :], bank[b][:, :], ACT.Copy), t, hT_read.get(n - 2))
                hT_ok[n] = VE.run(lambda e: e.tensor_tensor(hT_lo[:, s, :], bank[b][:, :],
                                                            hT_hi[:, s, :].bitcast(F32), ALU.subtract), hi)
                bank_free[b] = hT_ok[n]

            def down(n):
                s = n % 2
                bs = [get_bank(), get_bank()]
                for q in range(FET):
                    c, hi, lo = take("expert", (0, io["moe2"][n, q], W))
                    PE.wait(hT_ok[n])
                    toks = []
                    for half in range(2):
                        f = mm3(bank[bs[half]][:, :], hT_hi[:, s, q * P:(q + 1) * P], hT_lo[:, s, q * P:(q + 1) * P],
                                hi[:, half * T:(half + 1) * T], lo[:, half * T:(half + 1) * T], q == 0, q == FET - 1)
                        toks.append(PE.run(f))
                    release(c, toks[-1])
                hT_read[n] = toks[-1]
                y = n % 3
                gone = (s_scatter[y], scatters[y]) if scatters[y] else None
                a = AC.run(lambda e: e.activation(ye[:, y, 0:T], bank[bs[0]][:, :], ACT.Copy), toks[0], gone)
                v = VE.run(lambda e: e.tensor_copy(ye[:, y, T:D], bank[bs[1]][:, :]), toks[1], gone)
                bank_free[bs[0]], bank_free[bs[1]] = a, v
                scatters[y] += 16
                PO.issue(lambda e: e.indirect_dma_start(
                    ys_dram, bass.IndirectOffsetOnAxis(ap=sidx[:, n:n + 1], axis=0), ye[:, y, :], None,
                    bounds_check=2 * T - 1, oob_is_err=False).then_inc(s_scatter[y], 16), a, v)

            gather(0)
            gather(1)
            x_turn(0)
            for n in range(NE + 1):
                if n + 2 < NE:
                    gather(n + 2)
                if n < NE:
                    up(n)
                if n >= 1:
                    down(n - 1)
                if n < NE:
                    h_turn(n)

            outer = [PE.here(), AC.here(), VE.here(), PO.here(), cnt_ok] + [(s_scatter[i], scatters[i]) for i in range(3)]
            saved = [(q, q.done, q.sem, q.seen) for q in (PE, AC, VE, PO)]
            branch = ExitStack()
            for q, o in ((PE, o_pe), (AC, o_act), (VE, o_dve), (PO, o_pool)):
                q.wait(cnt_ok)
                if q.eng is not None:
                    more = q.eng.value_load(cnt[0:1, 0:1], min_val=0, max_val=EXTRA)
                    branch.enter_context(q.eng.If(more != 0))
                q.sem, q.done, q.seen = o, 0, dict(q.seen)
                q.wait(*outer)
            o_w, o_r, o_s = [0], [0], [0]
            w_free = None
            for x in range(EXTRA):
                n = NE + x
                o_r[0] += 16
                PO.issue(lambda e, n=n: e.indirect_dma_start(
                    xe[:, 0, :], None, x1_dram, bass.IndirectOffsetOnAxis(ap=gidx[:, n:n + 1], axis=0),
                    bounds_check=T - 1, oob_is_err=False).then_inc(o_rows, 16), PE.here())
                for half in range(2):
                    t = transpose4(lambda q, half=half: xe[:, 0, (4 * half + q) * P:(4 * half + q + 1) * P],
                                   half, (o_rows, o_r[0]))
                    o = slice(half * T, (half + 1) * T)
                    hi = AC.run(lambda e, o=o, half=half: e.activation(xeT_hi[:, 0, o], bank[half][:, :], ACT.Copy), t)
                    lo = VE.run(lambda e, o=o, half=half: e.tensor_tensor(
                        xeT_lo[:, 0, o], bank[half][:, :], xeT_hi[:, 0, o].bitcast(F32), ALU.subtract), hi)

                def weights(name, x, q):
                    o_w[0] += 16
                    PO.issue(lambda e: e.indirect_dma_start(
                        o_raw[:, :], None, io[name + "_rows"], bass.IndirectOffsetOnAxis(ap=widx[:, x, q:q + 1], axis=0),
                        bounds_check=NE * P * 4 - 1, oob_is_err=False).then_inc(o_weight, 16), VE.here())
                    hi = AC.run(lambda e: e.activation(o_hi[:, :], o_raw[:, :], ACT.Copy), (o_weight, o_w[0]), PE.here())
                    PE.wait(VE.run(lambda e: e.tensor_tensor(o_lo[:, :], o_raw[:, :], o_hi[:, :].bitcast(F32),
                                                             ALU.subtract), hi))

                if x == 0:
                    o_clear = PO.run(lambda e: e.memset(o_raw[:, :], 0.0))
                    VE.wait(o_clear)
                    PO.wait(o_clear)
                PE.wait(lo)
                for m, name in enumerate(("moe1", "moe3")):
                    for q in range(4):
                        weights(name, x, q)
                        for kk in range(2):
                            k = 2 * q + kk
                            t = PE.run(mm3(bank[2 + m][:, :], xeT_hi[:, 0, k * P:(k + 1) * P],
                                           xeT_lo[:, 0, k * P:(k + 1) * P], o_hi[:, kk * FE:(kk + 1) * FE],
                                           o_lo[:, kk * FE:(kk + 1) * FE], k == 0, k == DT - 1))
                t = AC.run(lambda e: e.activation(sil[:, 0, :], bank[2][:, :], ACT.Silu), t)
                t = VE.run(lambda e: e.tensor_tensor(hd[:, 0, :], sil[:, 0, :], bank[3][:, :], ALU.mult), t)
                t = transpose4(lambda q: hd[:, 0, q * P:(q + 1) * P], 4, t)
                t = AC.run(lambda e: e.activation(hT_hi[:, 0, :], bank[4][:, :], ACT.Copy), t)
                t = VE.run(lambda e: e.tensor_tensor(hT_lo[:, 0, :], bank[4][:, :], hT_hi[:, 0, :].bitcast(F32),
                                                     ALU.subtract), t)
                PE.wait(t)
                for q in range(FET):
                    weights("moe2", x, q)
                    for half in range(2):
                        t = PE.run(mm3(bank[5 + half][:, :], hT_hi[:, 0, q * P:(q + 1) * P],
                                       hT_lo[:, 0, q * P:(q + 1) * P], o_hi[:, half * T:(half + 1) * T],
                                       o_lo[:, half * T:(half + 1) * T], q == 0, q == FET - 1))
                t = VE.run(lambda e: e.tensor_copy(ye[:, 0, 0:T], bank[5][:, :]), t,
                           (o_store, o_s[0]) if o_s[0] else None)
                t = VE.run(lambda e: e.tensor_copy(ye[:, 0, T:D], bank[6][:, :]), t)
                o_s[0] += 16
                PO.issue(lambda e, n=n: e.indirect_dma_start(
                    ys_dram, bass.IndirectOffsetOnAxis(ap=sidx[:, n:n + 1], axis=0), ye[:, 0, :], None,
                    bounds_check=2 * T - 1, oob_is_err=False).then_inc(o_store, 16), t)
            ends = [q.here() for q in (PE, AC, VE, PO)] + [(o_store, o_s[0])]
            for q, done_, s_, seen_ in saved:
                q.wait(*ends)
                q.sem, q.done, q.seen = s_, done_, seen_
            branch.close()

            over = PO.run(lambda e: e.memset(sm[:, 29, 0:1], 0.0), *outer)
            for n in range(2 * TT):
                tt, k = n // 2, n % 2
                AC.issue(lambda e: e.dma_start(ysl[:, n, :], ys_dram[k * T + tt * P:k * T + (tt + 1) * P, :])
                         .then_inc(s_ys[tt], 16), over)

            def second_sum(tt):
                x = x_tok[:, tt, :]
                t = alpha_ok
                for k in range(2):
                    t = VE.run(lambda e: e.scalar_tensor_tensor(
                        x, ysl[:, 2 * tt + k, :], sm[:, 11 + k, tt:tt + 1], x, ALU.mult, ALU.add),
                        t, (s_ys[tt], 32), gates_ok)
                return t

            last_tok = layer_norm(1, second_sum, lambda tt, ok: None)

            FREE = {}
            stat = {"bank_free": VE.here()}
            xg_ok = [None] * DT
            rs_state = {}

            def finish(j, x_ok, gain):
                s = j % 2
                if gain is not None:
                    t = VE.run(lambda e: e.tensor_scalar(tmp[:, 4 + s, :], xT[:, j, :], gain, None, ALU.mult),
                               x_ok, FREE.get(("xg", s)))
                    hi = AC.run(lambda e: e.activation(xg_hi[:, j, :], tmp[:, 4 + s, :], ACT.Copy), t)
                    xg_ok[j] = VE.run(lambda e: e.tensor_tensor(xg_lo[:, j, :], tmp[:, 4 + s, :],
                                                                xg_hi[:, j, :].bitcast(F32), ALU.subtract), hi)
                    FREE["xg", s] = xg_ok[j]
                if j == 0:
                    sq = AC.run(lambda e: e.activation(rsq[:, :], xT[:, j, :], ACT.Square), x_ok, PO.here())
                else:
                    sq = AC.run(lambda e: e.activation(tmp[:, 6 + s, :], xT[:, j, :], ACT.Square),
                                x_ok, FREE.get(("sq", s)))
                if j > 0:
                    acc = PO.run(lambda e: e.tensor_tensor(rsq[:, :], rsq[:, :], tmp[:, 6 + s, :], ALU.add),
                                 sq, rs_state["acc"])
                    FREE["sq", s] = acc
                    rs_state["acc"] = acc
                else:
                    rs_state["acc"] = sq
                if j < DT - 1:
                    return

                def add():
                    t = PE.run(lambda e: e.matmul(bank[7][:, :], ones[:, :], rsq[:, :], start=True, stop=True),
                               acc, stat["bank_free"])
                    t = VE.run(lambda e: e.tensor_scalar(rsq[:, :], bank[7][:, :], 1.0 / D, RMS_EPS,
                                                         ALU.mult, ALU.add), t)
                    stat["bank_free"] = t
                    t = AC.run(lambda e: e.activation(rsq[:, :], rsq[:, :], ACT.Sqrt), t)
                    rs_state["ok"] = VE.run(lambda e: e.reciprocal(rsq[:, :], rsq[:, :]), t)
                later.append(add)

            if True:
                for j in range(DT):
                    b = get_bank()
                    for tt in range(TT):
                        PE.wait(last_tok[tt])
                        f = lambda e, b=b, j=j, tt=tt: e.transpose(bank[b][:, tt * P:(tt + 1) * P],
                                                                   x_tok[:, tt, j * P:(j + 1) * P], ident)
                        if tt < TT - 1:
                            PE.issue(f)
                    t = PE.run(f)
                    x_ok = VE.run(lambda e, j=j, b=b: e.tensor_copy(xT[:, j, :], bank[b][:, :]), t, *last_tok)
                    bank_free[b] = x_ok
                    run_later()
                    finish(j, x_ok, par("g_ffn1", j))
            tok_gone = t

            def product(b, tiles, rhs_hi, rhs_lo, oks):
                for n, (a_hi, a_lo, k, start, stop) in enumerate(tiles):
                    PE.wait(oks(k))
                    f = mm3(bank[b][:, :], a_hi, a_lo, rhs_hi(k), rhs_lo(k), start, stop)
                    if n < len(tiles) - 1:
                        PE.issue(f)
                return PE.run(f)

            def from_xg(src):
                c, hi, lo = take("dense", (0, src, W))
                b = get_bank()
                t = product(b, [(hi[:, k * P:(k + 1) * P], lo[:, k * P:(k + 1) * P], k, k == 0, k == DT - 1)
                                for k in range(DT)], lambda k: xg_hi[:, k, :], lambda k: xg_lo[:, k, :],
                            lambda k: xg_ok[k])
                release(c, t)
                run_later()
                return b, t

            def split_to(g, src_ap, ok, *more):
                hi = AC.run(lambda e: e.activation(g_hi[:, g, :], src_ap, ACT.Copy), ok, *more)
                return VE.run(lambda e: e.tensor_tensor(g_lo[:, g, :], src_ap, g_hi[:, g, :].bitcast(F32),
                                                        ALU.subtract), hi, ok, *more)

            def residual(j, b, t, coef, gain):
                x_ok = VE.run(lambda e: e.scalar_tensor_tensor(xT[:, j, :], bank[b][:, :], coef, xT[:, j, :],
                                                               ALU.mult, ALU.add), t)
                bank_free[b] = x_ok
                finish(j, x_ok, gain)

            def swiglu(l, names, gain):
                g_ok = [None] * FFT
                for j in range(FFT):
                    s = j % 2
                    b1, t1 = from_xg(io[names[0]][l, j])
                    b3, t3 = from_xg(io[names[1]][l, j])
                    u = VE.run(lambda e: e.tensor_tensor(tmp[:, s, :], bank[b1][:, :], rsq[:, :], ALU.mult),
                               t1, rs_state["ok"], FREE.get(("u", s)), tok_gone)
                    bank_free[b1] = u
                    u = AC.run(lambda e: e.activation(tmp[:, s, :], tmp[:, s, :], ACT.Silu), u)
                    v = VE.run(lambda e: e.tensor_tensor(tmp[:, 2 + s, :], bank[b3][:, :], rsq[:, :], ALU.mult), t3,
                               FREE.get(("v", s)))
                    bank_free[b3] = v
                    m = PO.run(lambda e: e.tensor_tensor(tmp[:, 2 + s, :], tmp[:, 2 + s, :], tmp[:, s, :], ALU.mult),
                               u, v)
                    FREE["u", s] = m
                    g_ok[j] = split_to(j, tmp[:, 2 + s, :], m)
                    FREE["v", s] = g_ok[j]
                for j in range(DT):
                    b = get_bank()
                    for q in range(3):
                        k0, k1 = 8 * q, min(8 * q + 8, FFT)
                        c, hi, lo = take("dense", (0, io[names[2]][l, j][:, k0 * P:k1 * P], (k1 - k0) * P))
                        t = product(b, [(hi[:, (k - k0) * P:(k - k0 + 1) * P], lo[:, (k - k0) * P:(k - k0 + 1) * P], k,
                                         k == 0, k == FFT - 1) for k in range(k0, k1)],
                                    lambda k: g_hi[:, k, :], lambda k: g_lo[:, k, :], lambda k: g_ok[k])
                        release(c, t)
                    run_later()
                    residual(j, b, t, 0.5, gain(j))

            PAIR_F, PAIR_A, PAIR_M, PAIR_C, PAIR_P = 0, 4, 4, 12, 16

            def mixers(l, gain):
                def column(i):
                    return from_xg(io["w_in"][l, i])

                ok = {}
                for i in range(4):
                    b, t = column(IN_F + i)
                    s = i % 2
                    u = VE.run(lambda e: e.tensor_tensor(tmp[:, s, :], bank[b][:, :], rsq[:, :], ALU.mult),
                               t, rs_state["ok"], FREE.get(("u", s)))
                    bank_free[b] = u
                    ok["u", i] = FREE["u", s] = split_to(PAIR_F + i, tmp[:, s, :], u)

                def conv_branch(i):
                    s = i % 2
                    b, t = column(IN_C + i)
                    cg = VE.run(lambda e: e.tensor_tensor(tmp[:, s, :], bank[b][:, :], rsq[:, :], ALU.mult),
                                t, rs_state["ok"], FREE.get(("u", s)))
                    bank_free[b] = cg
                    b2, t = column(IN_V + i)
                    v = VE.run(lambda e: e.tensor_tensor(tmp[:, 2 + s, :], bank[b2][:, :], rsq[:, :], ALU.mult), t,
                               FREE.get(("v", s)))
                    bank_free[b2] = v
                    z = zc[:, s, :]
                    pad = PO.run(lambda e: e.memset(z, 0.0), FREE.get(("z", s)))
                    t = PO.run(lambda e: e.tensor_tensor(z[:, 1:T + 1], tmp[:, s, :], tmp[:, 2 + s, :], ALU.mult),
                               cg, v, pad)
                    w = lambda k: par("w_conv", (l * 3 + k) * 4 + i)
                    t = VE.run(lambda e: e.tensor_scalar(tmp[:, s, :], z[:, 0:T], w(0), None, ALU.mult), t)
                    for k in (1, 2):
                        t = VE.run(lambda e, k=k: e.scalar_tensor_tensor(tmp[:, s, :], z[:, k:k + T], w(k), tmp[:, s, :],
                                                                         ALU.mult, ALU.add), t)
                    FREE["z", s] = t
                    cv = PO.run(lambda e: e.tensor_tensor(tmp[:, s, :], tmp[:, s, :], rsq[:, :], ALU.mult), t)
                    b3, t = column(IN_B + i)
                    m = VE.run(lambda e: e.tensor_tensor(tmp[:, s, :], tmp[:, s, :], bank[b3][:, :], ALU.mult), t, cv)
                    bank_free[b3] = m
                    ok["c", i] = split_to(PAIR_C + i, tmp[:, s, :], m)
                    FREE["u", s] = FREE["v", s] = ok["c", i]

                def token_spectra():
                    c, hi, lo = take("dense", (0, io["dft_c"], 2 * P))
                    for g in range(4):
                        for tt in range(TT):
                            if tt % 2 == 0:
                                b = get_bank()
                            f = mm3(bank[b][:, (tt % 2) * 256:(tt % 2) * 256 + 256],
                                    g_hi[:, PAIR_F + g, tt * P:(tt + 1) * P], g_lo[:, PAIR_F + g, tt * P:(tt + 1) * P],
                                    hi[:, 0:256], lo[:, 0:256], True, True)
                            PE.wait(ok["u", g])
                            t = PE.run(f)
                            if tt % 2 == 1:
                                pr = PAIR_A + 2 * g + tt // 2
                                hi_t = AC.run(lambda e, pr=pr, b=b: e.activation(g_hi[:, pr, :], bank[b][:, :], ACT.Copy), t)
                                ok["a", g, tt // 2] = VE.run(lambda e, pr=pr, b=b: e.tensor_tensor(
                                    g_lo[:, pr, :], bank[b][:, :], g_hi[:, pr, :].bitcast(F32), ALU.subtract), hi_t)
                                bank_free[b] = ok["a", g, tt // 2]
                    release(c, t)
                    ok["u_read"] = t

                def time_spectra():
                    bs = [get_bank() for _ in range(4)]
                    for n in range(4):
                        c, hi, lo = take("dense", (0, io["dft_s"][n], W))
                        for g in range(4):
                            for kk in range(2):
                                pr = PAIR_A + 2 * g + n % 2
                                PE.wait(ok["a", g, n % 2])
                                o = kk * 256 + (n // 2) * P
                                f = mm3(bank[bs[g]][:, :], g_hi[:, pr, o:o + P], g_lo[:, pr, o:o + P],
                                        hi[:, kk * T:(kk + 1) * T], lo[:, kk * T:(kk + 1) * T],
                                        n == 0 and kk == 0, n == 3 and kk == 1)
                                t = PE.run(f)
                            if n == 3:
                                hi_t = AC.run(lambda e, g=g: e.activation(g_hi[:, PAIR_F + g, :], bank[bs[g]][:, :],
                                                                          ACT.Copy), t, ok["u_read"])
                                ok["f", g] = VE.run(lambda e, g=g: e.tensor_tensor(
                                    g_lo[:, PAIR_F + g, :], bank[bs[g]][:, :], g_hi[:, PAIR_F + g, :].bitcast(F32),
                                    ALU.subtract), hi_t)
                                bank_free[bs[g]] = ok["f", g]
                        release(c, t)
                    ok["a_read"] = t

                conv_branch(0)
                token_spectra()
                conv_branch(1)
                conv_branch(2)
                time_spectra()
                conv_branch(3)

                for i in range(4):
                    s = i % 2
                    w, half = 2 << i, 1 << i
                    b, t = column(IN_P + i)
                    u0 = VE.run(lambda e: e.tensor_tensor(tmp[:, s, :], bank[b][:, :], rsq[:, :], ALU.mult), t,
                                FREE.get(("u", s)))
                    bank_free[b] = u0
                    pad = PO.run(lambda e: e.memset(zc[:, :, :], 0.0), FREE.get(("z", 0)), FREE.get(("z", 1)))
                    t = PO.run(lambda e: e.tensor_copy(zc[:, 0, half:half + T], tmp[:, s, :]), u0, pad)
                    a, n = 0, 1
                    while n < w:
                        width = T + w - 2 * n
                        last = 2 * n == w
                        dst = tmp[:, 2 + s, 0:width] if last else zc[:, 1 - a, 0:width]
                        t = VE.run(lambda e, a=a, n=n, width=width, dst=dst: e.tensor_tensor(
                            dst, zc[:, a, 0:width], zc[:, a, n:n + width], ALU.add), t, FREE.get(("v", s)))
                        a, n = 1 - a, 2 * n
                    FREE["z", 0] = FREE["z", 1] = t
                    t = VE.run(lambda e: e.tensor_scalar(tmp[:, 2 + s, :], tmp[:, 2 + s, :], 1.0 / w, None, ALU.mult), t)
                    for tm in list(range(half)) + list(range(T - half + 1, T)):
                        count = min(tm + half, T) - max(tm - half, 0)
                        if count != w:
                            t = VE.run(lambda e, tm=tm, count=count: e.tensor_scalar(
                                tmp[:, 2 + s, tm:tm + 1], tmp[:, 2 + s, tm:tm + 1], float(w) / count, None, ALU.mult), t)
                    t = VE.run(lambda e: e.tensor_tensor(tmp[:, 2 + s, :], tmp[:, 2 + s, :], tmp[:, s, :], ALU.subtract), t)
                    FREE["u", s] = t
                    ok["p", i] = FREE["v", s] = split_to(PAIR_P + i, tmp[:, 2 + s, :], t)

                for j in range(DT):
                    s = j % 2
                    c, hi, lo = take("dense", (0, io["mix_small"][l, j], 6 * P))
                    g = j // 2
                    outs = []
                    for kind in range(3):
                        b = get_bank()
                        if kind == 0:
                            tiles = [(hi[:, 0:P], lo[:, 0:P], PAIR_F + g, True, True)]
                            oks = lambda k: ok["f", k - PAIR_F]
                        elif kind == 2:
                            tiles = [(hi[:, P:2 * P], lo[:, P:2 * P], PAIR_P + g, True, True)]
                            oks = lambda k: ok["p", k - PAIR_P]
                        else:
                            tiles = [(hi[:, (2 + i) * P:(3 + i) * P], lo[:, (2 + i) * P:(3 + i) * P], PAIR_C + i,
                                      i == 0, i == 3) for i in range(4)]
                            oks = lambda k: ok["c", k - PAIR_C]
                        t = product(b, tiles, lambda k: g_hi[:, k, :], lambda k: g_lo[:, k, :], oks)
                        outs.append((b, t))
                    release(c, t)
                    acc = None
                    for kind in range(3):
                        b, t = column(IN_G + kind * DT + j)
                        q = (3 * j + kind) % 2
                        m = VE.run(lambda e: e.tensor_tensor(tmp[:, q, :], bank[b][:, :], rsq[:, :], ALU.mult), t,
                                   FREE.get(("u", q)))
                        bank_free[b] = m
                        m = AC.run(lambda e: e.activation(tmp[:, q, :], tmp[:, q, :], ACT.Sigmoid), m)
                        by, ty = outs[kind]
                        dst = tmp[:, 2 + s, :] if kind == 0 else tmp[:, q, :]
                        free = FREE.get(("v", s)) if kind == 0 else None
                        if kind == 2:
                            m = VE.run(lambda e: e.scalar_tensor_tensor(dst, bank[by][:, :], par("pool_scale", l * DT + j),
                                                                        tmp[:, q, :], ALU.mult, ALU.mult), m, ty)
                        else:
                            m = VE.run(lambda e: e.tensor_tensor(dst, bank[by][:, :], tmp[:, q, :], ALU.mult), m, ty, free)
                        bank_free[by] = m
                        if kind == 0:
                            acc = m
                        else:
                            acc = PO.run(lambda e: e.tensor_tensor(tmp[:, 2 + s, :], tmp[:, 2 + s, :], tmp[:, q, :],
                                                                   ALU.add), m, acc)
                        FREE["u", q] = acc
                    ok["m", j] = FREE["v", s] = split_to(PAIR_M + j, tmp[:, 2 + s, :], acc, ok["a_read"])
                for j in range(DT):
                    c, hi, lo = take("dense", (0, io["w_o"][l, j], W))
                    b = get_bank()
                    t = product(b, [(hi[:, k * P:(k + 1) * P], lo[:, k * P:(k + 1) * P], k, k == 0, k == DT - 1)
                                    for k in range(DT)], lambda k: g_hi[:, PAIR_M + k, :],
                                lambda k: g_lo[:, PAIR_M + k, :], lambda k: ok["m", k])
                    release(c, t)
                    run_later()
                    residual(j, b, t, 1.0, gain(j))

            for l in range(LAYERS):
                swiglu(l, ("w1_a", "w3_a", "w2_a"), lambda j, l=l: par("g_mix", l * DT + j))
                mixers(l, lambda j, l=l: par("g_ffn2", l * DT + j))
                swiglu(l, ("w1_b", "w3_b", "w2_b"),
                       lambda j, l=l: par("g_ffn1", (l + 1) * DT + j) if l + 1 < LAYERS else None)
            run_later()
            for j in range(DT):
                t = VE.run(lambda e, j=j: e.scalar_tensor_tensor(xT[:, j, :], xT[:, j, :], par("g_final", j),
                                                                 rsq[:, :], ALU.mult, ALU.mult), rs_state["ok"])
                SP.issue(lambda e, j=j: e.dma_start(io["out"][:, j, :], xT[:, j, :]).then_inc(s_out, 16), t)
            SP.wait((s_out, 16 * DT))
            return chunks

        chunks = program(None)
        block = ctx.enter_context(nc.Block())

        @block.sync
        def _(eng):
            program(chunks, "sp", eng)

        @block.scalar
        def _(eng):
            program(chunks, "act", eng)

        @block.vector
        def _(eng):
            program(chunks, "dve", eng)

        @block.gpsimd
        def _(eng):
            program(chunks, "pool", eng)

        @block.tensor
        def _(eng):
            program(chunks, "pe", eng)


POOL_EVERY = 10 ** 9


def dram_views(args):
    io = dict(args)
    for n in ("moe1", "moe3", "moe2"):
        io[n] = args[n].rearrange("(e p c) n -> e c p n", p=P, c=4)
        io[n + "_rows"] = args[n]
    return io


def lay_out(inp):
    import numpy as np

    def tiles(w):
        *lead, K, N = w.shape
        n = len(lead)
        w = w.reshape(*lead, K // P, P, N // P, P)
        w = w.transpose(*range(n), n + 2, n + 1, n, n + 3)
        return np.ascontiguousarray(w).reshape(*lead, N // P, P, K)

    def columns(v):
        return np.ascontiguousarray(v.reshape(-1, P).T)

    f = {k: np.asarray(v) for k, v in inp.items()}
    a = {}
    x = f["x"][0]
    a["x"] = np.ascontiguousarray(x.reshape(TT, P, D).transpose(1, 0, 2))
    a["xT"] = np.ascontiguousarray(x.T.reshape(DT, P, T).transpose(1, 0, 2))
    w_in = tiles(f["rec_w_in"][0])
    a["rec_in"] = np.concatenate([w_in[RT:], w_in[:RT]])
    a["rec_out"] = f["rec_w_out"][0].reshape(RT, P, D)
    bd = np.zeros((2, R, R), np.float32)
    for m, name in enumerate(("rec_w_r", "rec_w_i")):
        for n in range(LRU_BLOCKS):
            s = slice(n * LRU_W, (n + 1) * LRU_W)
            bd[m, s, s] = f[name][0, n]
    a["bd"] = np.stack([bd[m, i * P:(i + 1) * P, j * P:(j + 1) * P] for m in range(2) for i, j in BD_PAIRS], axis=1)
    groups = {"conv_w": f["rec_conv_w"][0], "conv_b": f["rec_conv_b"], "b_r": f["rec_b_r"], "b_i": f["rec_b_i"],
              "lam": f["rec_lambda"], "g_ffn1": f["g_ffn1_2"], "g_mix": f["g_mix_2"], "g_ffn2": f["g_ffn2_2"],
              "pool_scale": f["pool_scale_2"], "g_final": f["g_final_2"], "w_conv": f["w_conv_2"]}
    a["params"] = np.concatenate([columns(groups[n]) for n, _ in PARAM_GROUPS], axis=1)
    a["ln"] = np.stack([f["ln_g"][0, 0], f["ln_b"][0, 0], f["ln_g"][0, 1], f["ln_b"][0, 1]])
    a["wr"] = np.concatenate([f["moe_w_group"][0], f["moe_w_expert"][0]], axis=1) \
        .reshape(DT, P, NG + NE).transpose(1, 0, 2).copy()
    a["br"] = np.concatenate([f["moe_b_group"], f["moe_b_expert"]], axis=1)
    for name, src, kt in (("moe1", "moe_w1", DT), ("moe3", "moe_w3", DT), ("moe2", "moe_w2", FET)):
        w = f[src][0]
        a[name] = np.ascontiguousarray(w.reshape(NE, kt, P, -1).transpose(0, 2, 1, 3)).reshape(NE * P * 4, W)
    for s in ("a", "b"):
        for w in ("w1", "w3", "w2"):
            a[f"{w}_{s}"] = tiles(f[f"{w}_{s}_2"])
    a["w_in"] = tiles(f["w_in_2"])
    a["w_o"] = tiles(f["w_o_2"])
    wf, wp = ([f[n][:, j // 2, :, (j % 2) * P:(j % 2 + 1) * P] for j in range(DT)]
              for n in ("w_fourier_2", "w_pool_2"))
    small = [np.concatenate([wf[j], wp[j], tiles(f["w_conv_out_2"])[:, j]], axis=2) for j in range(DT)]
    a["mix_small"] = np.stack(small, axis=1)

    c = np.zeros((P, NCONST), np.float32)
    c[:, C_IDENT:C_IDENT + P] = np.eye(P)
    c[:, C_UPPER:C_UPPER + P] = np.triu(np.ones((P, P)), 1)
    c[:, C_IOTA:C_IOTA + P] = np.arange(P)
    c[:, C_GRANK:C_GRANK + TT * NG] = np.tile(NG - np.arange(NG), TT)
    c[:, C_ERANK:C_ERANK + TT * NE] = np.tile(NE - np.arange(NE), TT)
    c[:, C_EIDX:C_EIDX + TT * NE] = np.tile(np.arange(NE), TT)
    for k in range(2):
        for tt in range(TT):
            c[:, C_SLOT + k * TT + tt] = k * T + tt * P + np.arange(P) + 1
    c[:, C_ROW4] = 4 * np.arange(P)
    a["consts"] = c
    ang = 2 * np.pi / P * np.outer(np.arange(P), np.arange(P))
    a["dft_c"] = (np.concatenate([np.cos(ang), np.sin(ang)], axis=1) / 256.0).astype(np.float32)
    ang = 2 * np.pi / T * (np.outer(np.arange(T), np.arange(T)) % T)
    full = np.stack([np.cos(ang), -np.sin(ang)]).astype(np.float32)
    a["dft_s"] = full.reshape(2, 2, 2, P, T).transpose(0, 1, 3, 2, 4).reshape(4, P, W).copy()
    return a


def kernel(**inputs):
    import numpy as np
    import concourse.bacc as bacc
    from concourse.bass_utils import run_bass_kernel_spmd

    nc = bacc.Bacc("TRN2", target_bir_lowering=False, num_devices=1)
    arrays, args = {}, {}
    for name, a in lay_out(inputs).items():
        arrays[f"in_{name}"] = a
        args[name] = nc.dram_tensor(f"in_{name}", a.shape, mybir.dt.from_np(a.dtype), kind="ExternalInput").ap()
    args["out"] = nc.dram_tensor("out_0", (P, DT, T), F32, kind="ExternalOutput").ap()
    build(nc, dram_views(args))
    r = run_bass_kernel_spmd(nc, [arrays], core_ids=[0])
    got = r.results[0]["out_0"]
    return got.transpose(2, 1, 0).reshape(1, T, D)
```

```python
from contextlib import ExitStack

import concourse.bass as bass
from concourse import mybir

F32 = mybir.dt.float32
F32R = mybir.dt.float32r
BF16 = mybir.dt.bfloat16
U32 = mybir.dt.uint32
ALU = mybir.AluOpType
ACT = mybir.ActivationFunctionType
AX_X = mybir.AxisListType.X

P = 128
T = 512
D = 1024
TT = T // P
DT = D // P
R = 1280
RT = R // P
LRU_BLOCKS = 16
LRU_W = R // LRU_BLOCKS
CONV_W = 4
NG = 4
EPG = 8
NE = NG * EPG
FE = 512
FET = FE // P
FF = 2816
FFT = FF // P
LAYERS = 2
ALPHA = 2.0 ** 0.25
LN_EPS = 1e-5
RMS_EPS = 1e-6
W = 1024
FIRST = P // 2
NPAIR = NE // 2
EXTRA = 2 * T // (FIRST + 1)
FULL = -(-(T - FIRST) // P)
NBLK = NPAIR + EXTRA
BIG = 1e30

IN_F, IN_B, IN_C, IN_V, IN_P, IN_G = 0, 4, 8, 12, 16, 20
IN_TILES = 44

BD_PAIRS = [(i, j) for j in range(RT) for i in range(RT)
            if any(n * LRU_W < (i + 1) * P and (n + 1) * LRU_W > i * P
                   and n * LRU_W < (j + 1) * P and (n + 1) * LRU_W > j * P for n in range(LRU_BLOCKS))]

PARAM_GROUPS = [("conv_w", CONV_W * RT), ("conv_b", RT), ("b_r", RT), ("b_i", RT), ("lam", RT),
                ("g_ffn1", LAYERS * DT), ("g_mix", LAYERS * DT), ("g_ffn2", LAYERS * DT),
                ("pool_scale", LAYERS * DT), ("g_final", DT), ("w_conv", LAYERS * 3 * 4),
                ("ln_g", 2 * DT), ("ln_b", 2 * DT)]
PCOL = {}
NPAR = 0
for _name, _n in PARAM_GROUPS:
    PCOL[_name] = NPAR
    NPAR += _n

C_IDENT = 0
C_UPPER = C_IDENT + P
C_IOTA = C_UPPER + P
C_GRANK = C_IOTA + P
C_ERANK = C_GRANK + TT * NG
C_EPAIR = C_ERANK + TT * NE
C_EROW = C_EPAIR + TT * NE
C_SLOT = C_EROW + TT * NE
C_ROW4 = C_SLOT + 2 * TT
C_EDGE = C_ROW4 + 1
NCONST = C_EDGE + 32


DFT_CHUNKS = [(0, [(0, T, 0), (1, T // 2 + 2, 0)]), (T + T // 2 + 2, [(2, T // 2 + 2, 0), (3, T // 2 + 2, 0)]),
              (T + 3 * (T // 2 + 2), [(kt, T // 2, T // 2) for kt in range(TT)])]


class Queue:

    def __init__(self, sem, eng=None):
        self.sem = sem
        self.eng = eng
        self.done = 0
        self.seen = {}

    def wait(self, *tokens):
        for token in tokens:
            if token is not None and self.eng is not None:
                sem, value = token
                if self.seen.get(id(sem), 0) < value:
                    self.eng.wait_ge(sem, value)
                    self.seen[id(sem)] = value

    def run(self, fn, *tokens):
        self.wait(*tokens)
        if self.eng is not None:
            fn(self.eng).then_inc(self.sem, 1)
        self.done += 1
        return (self.sem, self.done)

    def issue(self, fn, *tokens):
        self.wait(*tokens)
        if self.eng is not None:
            fn(self.eng)

    def here(self):
        return (self.sem, self.done) if self.done else None


def build(nc, io):
    with ExitStack() as ctx:
        def sb(name, shape, dt=F32, into=None):
            return (into or ctx).enter_context(nc.sbuf_tensor(name, shape, dt))

        def sem(name):
            return ctx.enter_context(nc.semaphore(name))

        s_pe, s_act, s_dve, s_pool = (sem(n) for n in ("s_pe", "s_act", "s_dve", "s_pool"))
        o_pe, o_act, o_dve, o_pool = (sem(n) for n in ("o_pe", "o_act", "o_dve", "o_pool"))
        NRAW, NMORE, NSPLIT = 5, 11, 3
        s_raw = [sem(f"s_raw{i}") for i in range(NRAW + NMORE)]
        s_par, s_x, s_bd, s_router, s_x1, s_out = (
            sem(n) for n in ("s_par", "s_x", "s_bd", "s_router", "s_x1", "s_out"))
        s_xt = [sem(f"s_xt{i}") for i in range(4)]
        s_gb = [sem(f"s_gb{i}") for i in range(4)]
        s_gather = [sem(f"s_gather{i}") for i in range(3)]
        s_scatter = [sem(f"s_scatter{i}") for i in range(3)]
        s_ys = [sem(f"s_ys{i}") for i in range(4)]
        o_weight, o_rows, o_store = sem("o_weight"), sem("o_rows"), sem("o_store")

        bank = [ctx.enter_context(nc.psum_tensor(f"bank{i}", [P, 512], F32)) for i in range(8)]
        raw = sb("raw", [P, NRAW, W])
        w_hi = sb("w_hi", [P, NSPLIT, W], F32R)
        w_lo = sb("w_lo", [P, NSPLIT, W], F32R)
        params = sb("params", [P, NPAR])
        consts = sb("consts", [P, NCONST])
        ones = sb("ones", [P, P])

        with ExitStack() as first:
            x_tok = sb("x_tok", [P, TT, D], into=first)
            with ExitStack() as rec:
                xc = sb("xc", [P, RT, T], into=rec)
                bd = sb("bd", [P, 2 * len(BD_PAIRS), P], into=rec)
                x_hi = sb("x_hi", [P, RT, T], F32R, rec)
                x_lo = sb("x_lo", [P, RT, T], F32R, rec)
                gate = sb("gate", [P, 2, T], into=rec)
                hs = sb("hs", [P, RT, T], into=rec)
                xrp = sb("xrp", [P, 2, T + CONV_W - 1], into=rec)
                rg = sb("rg", [P, 2, T], into=rec)
                ig = sb("ig", [P, 2, T], into=rec)
                th = sb("th", [P, 2, T], into=rec)
                av = sb("av", [P, 2, T], into=rec)
                mv = sb("mv", [P, 2, T], into=rec)
                lamw = sb("lamw", [P, 8, RT], into=rec)
            with ExitStack() as moe:
                raw_more = sb("raw_more", [P, NMORE, W], into=moe)
                gb = sb("gb", [P, 2, D], into=moe)
                st = sb("st", [P, TT, 20], into=moe)
                wr = sb("wr", [P, DT, NG + NE], into=moe)
                br = sb("br", [NG + NE, 1], into=moe)
                lgT = sb("lgT", [NG + NE, T], into=moe)
                lg = sb("lg", [P, TT, NG + NE], into=moe)
                rt = sb("rt", [P, 16, TT, NE], into=moe)
                sm = sb("sm", [P, 32, TT], into=moe)
                chosen = sb("chosen", [P, TT, NE], BF16, moe)
                upper_b = sb("upper_b", [P, P], BF16, moe)
                ones_b = sb("ones_b", [P, P], BF16, moe)
                place = sb("place", [P, 8, 2 * TT], into=moe)
                oneh = sb("oneh", [P, 2 * TT, P], into=moe)
                blkh = sb("blkh", [P, 2 * TT, NBLK], into=moe)
                tabs = sb("tabs", [P, 4, NBLK], into=moe)
                gidx = sb("gidx", [P, NBLK], U32, moe)
                sidx = sb("sidx", [P, NBLK], U32, moe)
                wix = sb("wix", [P, EXTRA, 1], into=moe)
                widx = sb("widx", [P, EXTRA, 4], U32, moe)
                cnt = sb("cnt", [P, 1], U32, moe)
                sil = sb("sil", [P, 2, FE], into=moe)
                hd = sb("hd", [P, 2, FE], into=moe)
                hT_hi = sb("hT_hi", [P, 2, FE], F32R, moe)
                hT_lo = sb("hT_lo", [P, 2, FE], F32R, moe)
                with ExitStack() as experts:
                    with ExitStack() as router:
                        x1T = sb("x1T", [P, DT, T], into=router)
                    with ExitStack() as branch_only:
                        o_raw = sb("o_raw", [P, W], into=branch_only)
                        o_hi = sb("o_hi", [P, W], F32R, branch_only)
                        o_lo = sb("o_lo", [P, W], F32R, branch_only)
                        xe = sb("xe", [P, 3, D], into=branch_only)
                        ye = sb("ye", [P, 3, D], into=branch_only)
                        xeT_hi = sb("xeT_hi", [P, 2, D], F32R, branch_only)
                        xeT_lo = sb("xeT_lo", [P, 2, D], F32R, branch_only)
                with ExitStack() as combine:
                    ysl = sb("ysl", [P, 2 * TT, D], into=combine)
        g_hi = sb("g_hi", [P, FFT, T], F32R)
        g_lo = sb("g_lo", [P, FFT, T], F32R)
        xT = sb("xT", [P, DT, T])
        xg_hi = sb("xg_hi", [P, DT, T], F32R)
        xg_lo = sb("xg_lo", [P, DT, T], F32R)
        tmp = sb("tmp", [P, 8, T])
        rsq = sb("rsq", [P, T])
        zc = sb("zc", [P, 2, T + 16])

        x1_dram = nc.dram_tensor("x1_rows", (T, D), F32, kind="Internal").ap()
        ys_dram = nc.dram_tensor("y_rows", (2 * T, D), F32, kind="Internal").ap()

        ident = consts[:, C_IDENT:C_IDENT + P]
        upper = consts[:, C_UPPER:C_UPPER + P]
        iota = consts[:, C_IOTA:C_IOTA + P]

        def par(name, k=0):
            c = PCOL[name] + k
            return params[:, c:c + 1]

        def program(known, walk=None, eng=None):
            chunks = []
            PE, AC, VE, PO, SP = (Queue(q, eng if walk == n else None) for n, q in
                                  (("pe", s_pe), ("act", s_act), ("dve", s_dve), ("pool", s_pool), ("sp", None)))

            split = []
            used = []
            slots = []
            owner = {}
            landed = [0] * (NRAW + NMORE)
            LOOK = NSPLIT - 1
            more_free = []

            def raw_slot(i, n):
                return raw[:, i, 0:n] if i < NRAW else raw_more[:, i - NRAW, 0:n]

            def load_ready(stop=None):
                while len(slots) < (len(known) if stop is None else stop):
                    c = len(slots)
                    far = known[c][0] == "expert"
                    if far and not more_free:
                        return
                    i = min(range(NRAW + NMORE if far else NRAW), key=lambda i: owner.get(i, -1))
                    if i in owner:
                        if owner[i] >= len(split):
                            return
                        SP.wait(split[owner[i]])
                    elif i >= NRAW:
                        SP.wait(*more_free)
                    owner[i] = c
                    slots.append((i, landed[i] + 16 * (len(known[c]) - 1)))
                    landed[i] = slots[c][1]
                    for col, src, width in known[c][1:]:
                        SP.issue(lambda e: e.dma_start(raw_slot(i, W)[:, col:col + width], src)
                                 .then_inc(s_raw[i], 16))

            def convert(c):
                load_ready()
                i, value = slots[c]
                _, *parts = known[c]
                n = parts[-1][0] + parts[-1][2]
                free = used[c - NSPLIT] if c >= NSPLIT else None
                hi = w_hi[:, c % NSPLIT, 0:n]
                lo = w_lo[:, c % NSPLIT, 0:n]
                src = raw_slot(i, n)
                high = AC.run(lambda e: e.activation(hi, src, ACT.Copy), (s_raw[i], value), free)
                on = PO if known[c][0] == "recurrent" and c % 3 == 2 else VE
                split.append(on.run(lambda e: e.tensor_tensor(lo, src, hi.bitcast(F32), ALU.subtract), high, free))
                load_ready()

            def take(kind, *parts):
                c = len(chunks)
                chunks.append((kind, *parts))
                if known is not None:
                    while len(split) < min(c + LOOK + 1, len(known)):
                        convert(len(split))
                    PE.wait(split[c])
                return c, w_hi[:, c % NSPLIT, :], w_lo[:, c % NSPLIT, :]

            def release(c, token):
                used.append(token)

            RING = 7
            bank_free = [None] * 8
            turn = [0]

            def get_bank():
                b = turn[0] % RING
                turn[0] += 1
                PE.wait(bank_free[b])
                return b

            def mm3(out, a_hi, a_lo, b_hi, b_lo, start, stop):
                PE.issue(lambda e: e.matmul(out, a_lo, b_hi, start=start, stop=False))
                PE.issue(lambda e: e.matmul(out, a_hi, b_lo, start=False, stop=False))
                last = lambda e: e.matmul(out, a_hi, b_hi, start=False, stop=stop)
                return last

            later = []

            def run_later():
                todo, later[:] = list(later), []
                for fn in todo:
                    fn()

            if known is not None:
                load_ready(1)
            for n in range(4):
                SP.issue(lambda e: e.dma_start(hs[:, 2 * n:2 * n + 2, :], io["xT"][:, 2 * n:2 * n + 2, :])
                         .then_inc(s_xt[n], 16))
            if known is not None:
                convert(0)
            AC.issue(lambda e: e.dma_start(params[:, :], io["params"]).then_inc(s_par, 16))
            AC.issue(lambda e: e.dma_start(consts[:, :], io["consts"]).then_inc(s_par, 16))
            par_in, bd_in, x_in = (s_par, 32), (s_bd, 16), (s_x, 16)
            pad_ready = VE.run(lambda e: e.memset(xrp[:, :, 0:CONV_W - 1], 0.0))
            ones_ready = VE.run(lambda e: e.memset(ones[:, :], 1.0))

            x_split = []
            for k in range(DT):
                a = AC.run(lambda e: e.activation(x_hi[:, k, :], hs[:, k, :], ACT.Copy), (s_xt[k // 2], 16))
                x_split.append(VE.run(lambda e: e.tensor_tensor(
                    x_lo[:, k, :], hs[:, k, :], x_hi[:, k, :].bitcast(F32), ALU.subtract), a))

            def late_loads():
                AC.issue(lambda e: e.dma_start(bd[:, :, :], io["bd"]).then_inc(s_bd, 16))
                AC.issue(lambda e: e.dma_start(x_tok[:, :, :], io["x"]).then_inc(s_x, 16))

            lam = params[:, PCOL["lam"]:PCOL["lam"] + RT]
            L = [lamw[:, i, :] for i in range(8)]
            t = AC.run(lambda e: e.activation(L[0], lam, ACT.Abs), par_in)
            t = AC.run(lambda e: e.activation(L[1], L[0], ACT.Exp, scale=-1.0), t)
            t = VE.run(lambda e: e.tensor_scalar(L[2], L[1], 2.0, None, ALU.add), t)
            t = VE.run(lambda e: e.reciprocal(L[3], L[2]), t)
            t = VE.run(lambda e: e.tensor_tensor(L[2], L[1], L[3], ALU.mult), t)
            t = VE.run(lambda e: e.tensor_tensor(L[3], L[2], L[2], ALU.mult), t)
            t = VE.run(lambda e: e.tensor_scalar(L[4], L[3], 1.0 / 17, 1.0 / 15, ALU.mult, ALU.add), t)
            for n in (13, 11, 9, 7, 5, 3, 1):
                t = VE.run(lambda e: e.tensor_tensor(L[5], L[4], L[3], ALU.mult), t)
                t = VE.run(lambda e, n=n: e.tensor_scalar(L[4], L[5], 1.0 / n, None, ALU.add), t)
            t = VE.run(lambda e: e.tensor_tensor(L[5], L[4], L[2], ALU.mult), t)
            t = VE.run(lambda e: e.tensor_scalar(L[6], lam, -1.0, 0.0, ALU.mult, ALU.max), t, par_in)
            t = VE.run(lambda e: e.tensor_scalar(L[6], L[6], 4.0, None, ALU.mult), t)
            c4_ready = VE.run(lambda e: e.scalar_tensor_tensor(L[7], L[5], 8.0, L[6], ALU.mult, ALU.add), t)
            c4 = L[7]

            def in_tile(j):
                c, hi, lo = take("recurrent", (0, io["rec_in"][j], W))
                b = get_bank()
                for k in range(DT):
                    if j == 0:
                        PE.wait(x_split[k])
                    f = mm3(bank[b][:, :], hi[:, k * P:(k + 1) * P], lo[:, k * P:(k + 1) * P],
                            x_hi[:, k, :], x_lo[:, k, :], k == 0, k == DT - 1)
                    if k < DT - 1:
                        PE.issue(f)
                token = PE.run(f)
                release(c, token)
                return b, token

            xc_ready = [None] * RT
            gates_read = [None] * RT

            def conv(j, b, token):
                copied = AC.run(lambda e: e.activation(xrp[:, j % 2, CONV_W - 1:], bank[b][:, :], ACT.Copy),
                                token, pad_ready, xc_ready[j - 2] if j >= 2 else None)
                bank_free[b] = copied
                t = VE.run(lambda e: e.tensor_scalar(xc[:, j, :], xrp[:, j % 2, 0:T], par("conv_w", j),
                                                     par("conv_b", j), ALU.mult, ALU.add), copied, par_in)
                for k in range(1, CONV_W):
                    t = VE.run(lambda e, k=k: e.scalar_tensor_tensor(
                        xc[:, j, :], xrp[:, j % 2, k:k + T], par("conv_w", k * RT + j), xc[:, j, :],
                        ALU.mult, ALU.add), t)
                xc_ready[j] = t

            h_ready = [None] * RT
            rg_read, ig_read, th_read, av_read, mv_read = ([None] * RT for _ in range(5))

            def recur(j):
                s = j % 2
                old = j - 2 if j >= 2 else None
                past = lambda lst: lst[old] if old is not None else None
                PE.wait(bd_in)
                banks = []
                for m in range(2):
                    b = get_bank()
                    pairs = [n for n, (_, jj) in enumerate(BD_PAIRS) if jj == j]
                    for n in pairs:
                        i = BD_PAIRS[n][0]
                        PE.wait(xc_ready[i])
                        f = lambda e, n=n, i=i, b=b, m=m, pairs=pairs: e.matmul(
                            bank[b][:, :], bd[:, m * len(BD_PAIRS) + n, :], xc[:, i, :],
                            start=n == pairs[0], stop=n == pairs[-1])
                        if n != pairs[-1]:
                            PE.issue(f)
                    banks.append((b, PE.run(f)))
                (b_r, r_done), (b_i, i_done) = banks
                r_ok = AC.run(lambda e: e.activation(rg[:, s, :], bank[b_r][:, :], ACT.Sigmoid,
                                                     bias=par("b_r", j)), r_done, par_in, past(rg_read))
                bank_free[b_r] = r_ok
                i_ok = AC.run(lambda e: e.activation(ig[:, s, :], bank[b_i][:, :], ACT.Sigmoid,
                                                     bias=par("b_i", j)), i_done, past(ig_read))
                bank_free[b_i] = i_ok
                th_ok = AC.run(lambda e: e.activation(th[:, s, :], rg[:, s, :], ACT.Tanh,
                                                      scale=c4[:, j:j + 1]), r_ok, c4_ready, past(th_read))
                rg_read[j] = th_ok
                ix = PO.run(lambda e: e.tensor_tensor(ig[:, s, :], ig[:, s, :], xc[:, j, :], ALU.mult),
                            i_ok, xc_ready[j])
                t = VE.run(lambda e: e.tensor_scalar(av[:, s, :], th[:, s, :], 1.0, None, ALU.add), th_ok)
                t = VE.run(lambda e: e.reciprocal(mv[:, s, :], av[:, s, :]), t, past(mv_read))
                q = VE.run(lambda e: e.tensor_tensor(th[:, s, :], th[:, s, :], mv[:, s, :], ALU.mult), t)
                a_ok = VE.run(lambda e: e.tensor_scalar(av[:, s, :], th[:, s, :], -2.0, 1.0,
                                                        ALU.mult, ALU.add), q)
                t = VE.run(lambda e: e.scalar_tensor_tensor(mv[:, s, :], th[:, s, :], 1.0, th[:, s, :],
                                                            ALU.subtract, ALU.mult), a_ok)
                th_read[j] = t
                root = AC.run(lambda e: e.activation(mv[:, s, :], mv[:, s, :], ACT.Sqrt, scale=-4.0), t)

                def scan():
                    u = VE.run(lambda e: e.tensor_tensor(ig[:, s, :], mv[:, s, :], ig[:, s, :], ALU.mult),
                               root, ix)
                    mv_read[j] = u
                    h_ready[j] = VE.run(lambda e: e.tensor_tensor_scan(
                        hs[:, j, :], av[:, s, :], ig[:, s, :], 0.0, ALU.mult, ALU.add), u)
                    ig_read[j] = av_read[j] = h_ready[j]
                return scan

            pend = []
            for j in range(RT):
                b, token = in_tile(j)
                conv(j, b, token)
                if j == 0:
                    late_loads()
                if j >= 2:
                    pend.append(recur(j - 2))
                    if len(pend) > 1:
                        pend.pop(0)()
            rest = list(range(RT - 2, RT))
            y_ready, y_split = [None] * RT, [None] * RT
            y_at = [(DT + j) % RT for j in range(RT)]

            def split_y(j, free=None):
                a = AC.run(lambda e: e.activation(x_hi[:, y_at[j], :], hs[:, j, :], ACT.Copy), y_ready[j], free)
                y_split[j] = VE.run(lambda e: e.tensor_tensor(
                    x_lo[:, y_at[j], :], hs[:, j, :], x_hi[:, y_at[j], :].bitcast(F32), ALU.subtract), a)

            for j in range(RT):
                b, token = in_tile(RT + j)
                if rest:
                    pend.append(recur(rest.pop(0)))
                if pend:
                    pend.pop(0)()
                g_ok = AC.run(lambda e, j=j, b=b: e.activation(gate[:, j % 2, :], bank[b][:, :],
                                                               ACT.Gelu_apprx_tanh),
                              token, y_ready[j - 2] if j >= 2 else None)
                bank_free[b] = g_ok
                while h_ready[j] is None:
                    pend.pop(0)()
                y_ready[j] = VE.run(lambda e, j=j: e.tensor_tensor(hs[:, j, :], hs[:, j, :], gate[:, j % 2, :],
                                                                   ALU.mult), g_ok)
                if j < RT - DT:
                    split_y(j)
            x_free = token
            for j in range(RT - DT, RT):
                split_y(j, x_free)
            more_free += [token, VE.here(), PO.here(), AC.here()]
            out_banks = [(get_bank() if n < RING else 7) for n in range(8)]
            for k in range(RT):
                c, hi, lo = take("recurrent", (0, io["rec_out"][k], W))
                PE.wait(y_split[k])
                done = []
                for tt in range(TT):
                    for half in range(2):
                        f = mm3(bank[out_banks[2 * tt + half]][:, :], x_hi[:, y_at[k], tt * P:(tt + 1) * P],
                                x_lo[:, y_at[k], tt * P:(tt + 1) * P], hi[:, half * T:(half + 1) * T],
                                lo[:, half * T:(half + 1) * T], k == 0, k == RT - 1)
                        done.append(PE.run(f))
                release(c, done[-1])
            rec_done = done[-1]

            for n in range(2):
                AC.issue(lambda e: e.dma_start(gb[:, n, :], io["ln"][n:n + 1, :].partition_broadcast(P))
                         .then_inc(s_gb[n], 16), x_free, *h_ready)
            AC.issue(lambda e: e.dma_start(wr[:, :, :], io["wr"]).then_inc(s_router, 16))
            AC.issue(lambda e: e.dma_start(br[:, :], io["br"]).then_inc(s_router, 16))

            def statistics(tt, z_ok):
                x = x_tok[:, tt, :]
                for h in range(2):
                    t = VE.run(lambda e: e.bn_stats(st[:, tt, h * 6:h * 6 + 6], x[:, h * T:(h + 1) * T]), z_ok)
                t = VE.run(lambda e: e.bn_aggr(st[:, tt, 12:14], st[:, tt, 0:12]), t)
                t = VE.run(lambda e: e.tensor_scalar(st[:, tt, 14:15], st[:, tt, 13:14], LN_EPS, None, ALU.add), t)
                return AC.run(lambda e: e.activation(st[:, tt, 15:16], st[:, tt, 14:15], ACT.Sqrt), t)

            def layer_norm(z_of):
                roots, oks = [], []
                for tt in range(TT + 1):
                    if tt < TT:
                        roots.append(statistics(tt, z_of(tt)))
                    if tt >= 1:
                        x, a = x_tok[:, tt - 1, :], tt - 1
                        r = VE.run(lambda e: e.reciprocal(st[:, a, 16:17], st[:, a, 15:16]), roots[a])
                        oks.append(VE.run(lambda e: e.tensor_scalar(x, x, st[:, a, 12:13], st[:, a, 16:17],
                                                                    ALU.subtract, ALU.mult), r))
                return oks

            def first_sum(tt):
                for half in range(2):
                    b = out_banks[2 * tt + half]
                    x = x_tok[:, tt, half * T:(half + 1) * T]
                    t = VE.run(lambda e: e.scalar_tensor_tensor(x, x, ALPHA, bank[b][:, :], ALU.mult, ALU.add),
                               done[2 * tt + half], x_in)
                    bank_free[b] = t
                return t

            xn_ok = layer_norm(first_sum)

            def transpose4(src, b, ok):
                PE.wait(ok, par_in)
                for n in range(4):
                    f = lambda e, n=n: e.transpose(bank[b][:, n * P:(n + 1) * P], src(n), ident)
                    if n < 3:
                        PE.issue(f)
                return PE.run(f)

            lg_bank = 7
            PE.wait((s_router, 32), bank_free[7])
            for tt in range(TT):
                halves = []
                for half in range(2):
                    b = get_bank()
                    t = transpose4(lambda n: x_tok[:, tt, (4 * half + n) * P:(4 * half + n + 1) * P], b, xn_ok[tt])
                    x_turned = t
                    for n in range(4):
                        k = 4 * half + n
                        o, i = x1T[:, k, tt * P:(tt + 1) * P], bank[b][:, n * P:(n + 1) * P]
                        if half == 0:
                            t = AC.run(lambda e: e.activation(o, i, ACT.Identity, scale=par("ln_g", k),
                                                              bias=par("ln_b", k)), x_turned)
                        else:
                            t = VE.run(lambda e: e.tensor_scalar(o, i, par("ln_g", k), par("ln_b", k),
                                                                 ALU.mult, ALU.add), x_turned)
                    bank_free[b] = t
                    halves.append(t)
                x = x_tok[:, tt, :]
                t = PO.run(lambda e: e.tensor_tensor(x, x, gb[:, 0, :], ALU.mult), x_turned, (s_gb[0], 16))
                t = PO.run(lambda e: e.tensor_tensor(x, x, gb[:, 1, :], ALU.add), t, (s_gb[1], 16))
                PO.issue(lambda e: e.dma_start(x1_dram[tt * P:(tt + 1) * P, :], x).then_inc(s_x1, 16), t)
                PE.wait(*halves)
                for k in range(DT):
                    f = lambda e: e.matmul(bank[lg_bank][0:NG + NE, tt * P:(tt + 1) * P], wr[:, k, :],
                                           x1T[:, k, tt * P:(tt + 1) * P], start=k == 0, stop=k == DT - 1)
                    if k < DT - 1:
                        PE.issue(f)
                x1T_read = PE.run(f)
            VE.run(lambda e: e.memset(ones_b[:, :], 1.0))
            VE.run(lambda e: e.tensor_copy(upper_b[:, :], upper))
            t = VE.run(lambda e: e.tensor_scalar(lgT[:, :], bank[lg_bank][0:NG + NE, :], br[:, :], None, ALU.add),
                       x1T_read)
            bank_free[lg_bank] = t
            b = get_bank()
            PE.wait(t)
            for tt in range(TT):
                f = lambda e: e.transpose(bank[b][:, tt * (NG + NE):(tt + 1) * (NG + NE)],
                                          lgT[:, tt * P:(tt + 1) * P], ident[0:NG + NE, 0:NG + NE])
                if tt < TT - 1:
                    PE.issue(f)
            t = PE.run(f)
            t = VE.run(lambda e: e.tensor_copy(lg[:, :, :], bank[b][:, 0:TT * (NG + NE)]
                                               .rearrange("p (a n) -> p a n", a=TT)), t)
            bank_free[b] = lg_ok = t

            S = lambda n: sm[:, n, :]
            Rt = lambda n: rt[:, n, :, :]
            wide = lambda ap: ap.unsqueeze(2).to_broadcast([P, TT, NE])
            V = lambda fn, *w: VE.run(fn, *w)

            def tt_(o, a, b, op, *w):
                return V(lambda e: e.tensor_tensor(o, a, b, op), *w)

            def ts_(o, a, s1, s2, op0, op1=None, *w):
                if op1 is None:
                    return V(lambda e: e.tensor_scalar(o, a, s1, None, op0), *w)
                return V(lambda e: e.tensor_scalar(o, a, s1, s2, op0, op1), *w)

            grank = consts[:, C_GRANK:C_GRANK + TT * NG].rearrange("p (a n) -> p a n", a=TT)
            erank = consts[:, C_ERANK:C_ERANK + TT * NE].rearrange("p (a n) -> p a n", a=TT)
            epair = consts[:, C_EPAIR:C_EPAIR + TT * NE].rearrange("p (a n) -> p a n", a=TT)
            erow = consts[:, C_EROW:C_EROW + TT * NE].rearrange("p (a n) -> p a n", a=TT)
            gl = lg[:, :, 0:NG]
            el = lg[:, :, NG:NG + NE]
            G = lambda n: rt[:, n, :, 0:NG]
            gwide = lambda ap: ap.unsqueeze(2).to_broadcast([P, TT, NG])

            t = V(lambda e: e.tensor_reduce(S(0), gl, AX_X, ALU.max), t)
            t = tt_(G(0), gl, gwide(S(0)), ALU.is_equal, t)
            t = tt_(G(1), G(0), grank, ALU.mult, t)
            t = V(lambda e: e.tensor_reduce(S(1), G(1), AX_X, ALU.max), t)
            t = tt_(G(2), G(1), gwide(S(1)), ALU.is_equal, t)
            t = ts_(G(5), G(2), 1.0, BIG, ALU.subtract, ALU.mult, t)
            em = Rt(6)
            t = tt_(em.rearrange("p a (g n) -> p a g n", g=NG), el.rearrange("p a (g n) -> p a g n", g=NG),
                    G(5).unsqueeze(3).to_broadcast([P, TT, NG, EPG]), ALU.add, t)

            def largest(vals, value, onehot, scratch, t):
                t = V(lambda e: e.tensor_reduce(value, vals, AX_X, ALU.max), t)
                t = tt_(scratch, vals, wide(value), ALU.is_equal, t)
                t = tt_(scratch, scratch, erank, ALU.mult, t)
                t = V(lambda e: e.tensor_reduce(S(4), scratch, AX_X, ALU.max), t)
                return tt_(onehot, scratch, wide(S(4)), ALU.is_equal, t)

            t = largest(em, S(5), Rt(7), Rt(0), t)
            t = V(lambda e: e.scalar_tensor_tensor(
                rt[:, 9, :, :].rearrange("p a n -> p (a n)"), rt[:, 7, :, :].rearrange("p a n -> p (a n)"),
                -4.0 * BIG, rt[:, 6, :, :].rearrange("p a n -> p (a n)"), ALU.mult, ALU.add), t)
            t = largest(Rt(9), S(6), Rt(8), Rt(0), t)
            sel_ok = tt_(chosen[:, :, :], Rt(7), Rt(8), ALU.add, t)

            t2 = tt_(G(3), gl, gwide(S(0)), ALU.subtract)
            t3 = tt_(S(7), S(6), S(5), ALU.subtract, sel_ok)
            e2 = AC.run(lambda e: e.activation(G(4), G(3), ACT.Exp), t2)
            e3 = AC.run(lambda e: e.activation(S(8), S(7), ACT.Exp), t3)

            def gates():
                t2 = V(lambda e: e.tensor_reduce(S(2), G(4), AX_X, ALU.add), e2)
                t2 = V(lambda e: e.reciprocal(S(3), S(2)), t2)
                t3 = ts_(S(9), S(8), 1.0, None, ALU.add, None, e3)
                t3 = V(lambda e: e.reciprocal(S(10), S(9)), t3)
                t3 = tt_(S(11), S(10), S(3), ALU.mult, t3, t2)
                return tt_(S(12), S(11), S(8), ALU.mult, t3)

            rk_bank = get_bank()
            PE.wait(sel_ok)
            for tt in range(TT + 1):
                o = bank[rk_bank][:, tt * NE:(tt + 1) * NE]
                terms = [(ones_b[:, :], a) for a in range(min(tt, TT))] + ([(upper_b[:, :], tt)] if tt < TT else [])
                for n, (m, a) in enumerate(terms):
                    f = lambda e, o=o, m=m, a=a, n=n, k=len(terms): e.matmul(
                        o, m, chosen[:, a, :], start=n == 0, stop=n == k - 1)
                    if not (tt == TT and n == len(terms) - 1):
                        PE.issue(f)
            t = PE.run(f)
            t = V(lambda e: e.tensor_copy(rt[:, 11:13, :, :].rearrange("p k a n -> p (k a n)")[:, 0:(TT + 1) * NE],
                                          bank[rk_bank][:, 0:(TT + 1) * NE]), t)
            bank_free[rk_bank] = t
            counts = rt[:, 12, 0, :]
            C = lambda n: rt[:, 12, n, :]
            D_ = lambda n: rt[:, 13, n, :]
            u = ts_(C(1), counts, float(FIRST), None, ALU.is_gt, None, t)
            for m in range(1, FULL):
                u = V(lambda e: e.scalar_tensor_tensor(C(1), counts, float(FIRST + m * P), C(1), ALU.is_gt,
                                                       ALU.add), u)
            one = V(lambda e: e.memset(D_(0), 1.0))
            u = V(lambda e: e.tensor_tensor_scan(C(3), D_(0), C(1), 0.0, ALU.mult, ALU.add), u, one)
            u = tt_(D_(1), C(3), C(1), ALU.subtract, u)

            pair = rt[:, 0:2, :, :].rearrange("p k a n -> p (k a) n")
            pick = rt[:, 7:9, :, :]
            RANK, PAIR, START, BLOCK, ROW = (place[:, n, :] for n in range(5))
            flat = lambda ap: ap.rearrange("p k a n -> p k (a n)")
            both = lambda ap: ap.rearrange("p a n -> p (a n)").unsqueeze(1).to_broadcast([P, 2, TT * NE])
            every = lambda ap: ap.unsqueeze(1).to_broadcast([P, 2 * TT, NE])
            t = tt_(flat(rt[:, 0:2, :, :]), flat(pick), both(Rt(11)), ALU.mult, t)
            t = V(lambda e: e.tensor_reduce(RANK, pair, AX_X, ALU.add), t)
            w1 = tt_(flat(rt[:, 0:2, :, :]), flat(pick), both(epair), ALU.mult, t)
            w1 = V(lambda e: e.tensor_reduce(PAIR, pair, AX_X, ALU.add), w1)
            w1 = tt_(flat(rt[:, 0:2, :, :]), flat(pick), both(erow), ALU.mult, w1)
            w1 = V(lambda e: e.tensor_reduce(ROW, pair, AX_X, ALU.add), w1)
            w1 = tt_(pair, pick.rearrange("p k a n -> p (k a) n"), every(D_(1)), ALU.mult, w1, u)
            w1 = V(lambda e: e.tensor_reduce(START, pair, AX_X, ALU.add), w1)
            t = ts_(BLOCK, RANK, float(FIRST) - 0.5, None, ALU.is_gt, None, t)
            for m in range(1, FULL):
                t = V(lambda e: e.scalar_tensor_tensor(BLOCK, RANK, float(FIRST + m * P) - 0.5, BLOCK, ALU.is_gt,
                                                       ALU.add), t)
            t = V(lambda e: e.scalar_tensor_tensor(RANK, BLOCK, -float(P), RANK, ALU.mult, ALU.add), t)
            t = tt_(RANK, RANK, ROW, ALU.add, t, w1)
            t = ts_(ROW, ROW, -1.0, float(FIRST), ALU.mult, ALU.add, t)
            t = V(lambda e: e.scalar_tensor_tensor(ROW, BLOCK, 0.5, ROW, ALU.is_gt, ALU.mult), t)
            t = tt_(RANK, RANK, ROW, ALU.add, t)
            t = V(lambda e: e.scalar_tensor_tensor(START, START, float(NPAIR - 1), BLOCK, ALU.add, ALU.add), t)
            t = tt_(START, START, PAIR, ALU.subtract, t)
            t = V(lambda e: e.scalar_tensor_tensor(START, BLOCK, 0.5, START, ALU.is_gt, ALU.mult), t)
            t = tt_(PAIR, PAIR, START, ALU.add, t)
            oneh_ok = []
            for n in range(2 * TT):
                V(lambda e: e.tensor_scalar(oneh[:, n, :], iota, place[:, 0, n:n + 1], None, ALU.is_equal), t)
                oneh_ok.append(V(lambda e: e.tensor_scalar(
                    blkh[:, n, :], iota[:, 0:NBLK], place[:, 1, n:n + 1],
                    consts[:, C_SLOT + n:C_SLOT + n + 1], ALU.is_equal, ALU.mult), t))
            tb_bank = get_bank()
            for n in range(2 * TT):
                PE.wait(oneh_ok[n])
                f = lambda e, n=n: e.matmul(bank[tb_bank][:, 0:NBLK], oneh[:, n, :], blkh[:, n, :],
                                            start=n == 0, stop=n == 2 * TT - 1)
                if n < 2 * TT - 1:
                    PE.issue(f)
            t = PE.run(f)
            Tb = lambda n: tabs[:, n, :]
            t = V(lambda e: e.tensor_scalar(Tb(0), bank[tb_bank][:, 0:NBLK], 1.0, None, ALU.subtract), t)
            bank_free[tb_bank] = t
            t = ts_(Tb(1), Tb(0), 0.0, float(8 * T), ALU.is_lt, ALU.mult, t)
            t = tt_(Tb(2), Tb(0), Tb(1), ALU.add, t)
            t = V(lambda e: e.tensor_copy(sidx[:, :], Tb(2)), t)
            t = ts_(Tb(1), Tb(2), float(T) - 0.5, -float(T), ALU.is_gt, ALU.mult, t)
            t = tt_(Tb(3), Tb(2), Tb(1), ALU.add, t)
            idx_ok = V(lambda e: e.tensor_copy(gidx[:, :], Tb(3)), t)
            xe_clear = PO.run(lambda e: e.memset(xe[:, :, :], 0.0), x1T_read)
            gates_ok = gates()
            t = V(lambda e: e.tensor_copy(cnt[:, :], C(3)[:, NE - 1:NE]))
            before = rt[:, 5:9, :, :].rearrange("p k a n -> p (k a) n")[:, 0:EXTRA, :]
            t = tt_(before, C(3).unsqueeze(1).to_broadcast([P, EXTRA, NE]),
                    iota[:, 0:EXTRA].unsqueeze(2).to_broadcast([P, EXTRA, NE]), ALU.is_le, t)
            t = V(lambda e: e.tensor_reduce(wix[:, :, 0], before, AX_X, ALU.add), t)
            t = V(lambda e: e.tensor_scalar(wix[:, :, 0], wix[:, :, 0], float(4 * P), consts[:, C_ROW4:C_ROW4 + 1],
                                            ALU.mult, ALU.add), t)
            cnt_ok = tt_(widx[:, :, :], wix[:, :, :].to_broadcast([P, EXTRA, 4]),
                         iota[:, 0:4].unsqueeze(1).to_broadcast([P, EXTRA, 4]), ALU.add, t)
            gathers = [0, 0, 0]
            scatters = [0, 0, 0]
            xe_read = {}

            def gather(n):
                s = n % 3
                gathers[s] += 16
                PO.issue(lambda e: e.indirect_dma_start(
                    xe[:, s, :], None, x1_dram, bass.IndirectOffsetOnAxis(ap=gidx[:, n:n + 1], axis=0),
                    bounds_check=T - 1, oob_is_err=False).then_inc(s_gather[s], 16),
                    idx_ok, xe_clear, lg_ok, (s_x1, 16 * TT), xe_read.get(n - 3))

            xeT_ok, xeT_read, hd_ok, hT_ok, sil_read, hd_read, hT_read = {}, {}, {}, {}, {}, {}, {}

            def x_turn(n):
                s = n % 2
                oks = []
                for half in range(2):
                    b = get_bank()
                    t = transpose4(lambda q, half=half: xe[:, n % 3, (4 * half + q) * P:(4 * half + q + 1) * P],
                                   b, (s_gather[n % 3], 16 * (n // 3 + 1)))
                    xe_read[n] = t
                    o = slice(half * T, (half + 1) * T)
                    hi = AC.run(lambda e, o=o, b=b: e.activation(xeT_hi[:, s, o], bank[b][:, :], ACT.Copy),
                                t, xeT_read.get(n - 2))
                    lo = VE.run(lambda e, o=o, b=b: e.tensor_tensor(xeT_lo[:, s, o], bank[b][:, :],
                                                                    xeT_hi[:, s, o].bitcast(F32), ALU.subtract),
                                hi, xeT_read.get(n - 2))
                    bank_free[b] = lo
                xeT_ok[n] = lo

            def up(n, h):
                s = n % 2
                rows = slice(h * FIRST, (h + 1) * FIRST)
                for m, name in enumerate(("moe1", "moe3")):
                    b = get_bank()
                    for q in range(4):
                        c, hi, lo = take("expert", (0, io[name][2 * n + h, q], W))
                        PE.wait(xeT_ok.get(n))
                        for kk in range(2):
                            k = 2 * q + kk
                            f = mm3(bank[b][:, :], xeT_hi[:, s, k * P:(k + 1) * P], xeT_lo[:, s, k * P:(k + 1) * P],
                                    hi[:, kk * FE:(kk + 1) * FE], lo[:, kk * FE:(kk + 1) * FE], k == 0, k == DT - 1)
                            if kk == 0:
                                PE.issue(f)
                        t = PE.run(f)
                        release(c, t)
                        if h == 1 and m == 1 and q == 1 and n + 1 < NPAIR:
                            x_turn(n + 1)
                    if m == 0:
                        sil_ok = AC.run(lambda e, b=b: e.activation(sil[rows, s, :], bank[b][rows, :], ACT.Silu),
                                        t, sil_read.get((n - 2, h)))
                        bank_free[b] = sil_ok
                    else:
                        hd_ok[n] = VE.run(lambda e, b=b: e.tensor_tensor(hd[rows, s, :], sil[rows, s, :],
                                                                         bank[b][rows, :], ALU.mult),
                                          t, sil_ok, hd_read.get(n - 2))
                        sil_read[n, h] = bank_free[b] = hd_ok[n]
                if h == 1:
                    xeT_read[n] = t

            def h_turn(n):
                s = n % 2
                b = get_bank()
                t = transpose4(lambda q: hd[:, s, q * P:(q + 1) * P], b, hd_ok[n])
                hd_read[n] = t
                hi = AC.run(lambda e: e.activation(hT_hi[:, s, :], bank[b][:, :], ACT.Copy), t, hT_read.get(n - 2))
                hT_ok[n] = VE.run(lambda e: e.tensor_tensor(hT_lo[:, s, :], bank[b][:, :],
                                                            hT_hi[:, s, :].bitcast(F32), ALU.subtract), hi)
                bank_free[b] = hT_ok[n]

            def down(n, h):
                s = n % 2
                rows = slice(h * FIRST, (h + 1) * FIRST)
                bs = [get_bank(), get_bank()]
                for q in range(FET):
                    c, hi, lo = take("expert", (0, io["moe2"][2 * n + h, q], W))
                    PE.wait(hT_ok[n])
                    toks = []
                    for half in range(2):
                        f = mm3(bank[bs[half]][:, :], hT_hi[:, s, q * P:(q + 1) * P], hT_lo[:, s, q * P:(q + 1) * P],
                                hi[:, half * T:(half + 1) * T], lo[:, half * T:(half + 1) * T], q == 0, q == FET - 1)
                        toks.append(PE.run(f))
                    release(c, toks[-1])
                hT_read[n] = toks[-1]
                y = n % 3
                gone = (s_scatter[y], scatters[y]) if scatters[y] else None
                a = AC.run(lambda e: e.activation(ye[rows, y, 0:T], bank[bs[0]][rows, :], ACT.Copy), toks[0], gone)
                v = VE.run(lambda e: e.tensor_copy(ye[rows, y, T:D], bank[bs[1]][rows, :]), toks[1], gone)
                bank_free[bs[0]], bank_free[bs[1]] = a, v
                if h == 0:
                    return
                scatters[y] += 16
                PO.issue(lambda e: e.indirect_dma_start(
                    ys_dram, bass.IndirectOffsetOnAxis(ap=sidx[:, n:n + 1], axis=0), ye[:, y, :], None,
                    bounds_check=2 * T - 1, oob_is_err=False).then_inc(s_scatter[y], 16), a, v)

            gather(0)
            gather(1)
            for tt in range(TT):
                alpha_ok = PO.run(lambda e: e.tensor_scalar(x_tok[:, tt, :], x_tok[:, tt, :], ALPHA, 1.0,
                                                            ALU.mult, ALU.mult), (s_x1, 16 * TT))
            x_turn(0)
            for n in range(NPAIR + 1):
                if n + 2 < NPAIR:
                    gather(n + 2)
                for h in range(2):
                    if n < NPAIR:
                        up(n, h)
                    if n >= 1:
                        down(n - 1, h)
                if n < NPAIR:
                    h_turn(n)

            outer = [PE.here(), AC.here(), VE.here(), PO.here(), cnt_ok] + [(s_scatter[i], scatters[i]) for i in range(3)]
            saved = [(q, q.done, q.sem, q.seen) for q in (PE, AC, VE, PO)]
            branch = ExitStack()
            for q, o in ((PE, o_pe), (AC, o_act), (VE, o_dve), (PO, o_pool)):
                q.wait(cnt_ok)
                if q.eng is not None:
                    more = q.eng.value_load(cnt[0:1, 0:1], min_val=0, max_val=EXTRA)
                    branch.enter_context(q.eng.If(more != 0))
                q.sem, q.done, q.seen = o, 0, dict(q.seen)
                q.wait(*outer)
            o_w, o_r, o_s = [0], [0], [0]
            w_free = None
            for x in range(EXTRA):
                n = NPAIR + x
                o_r[0] += 16
                PO.issue(lambda e, n=n: e.indirect_dma_start(
                    xe[:, 0, :], None, x1_dram, bass.IndirectOffsetOnAxis(ap=gidx[:, n:n + 1], axis=0),
                    bounds_check=T - 1, oob_is_err=False).then_inc(o_rows, 16), PE.here())
                for half in range(2):
                    t = transpose4(lambda q, half=half: xe[:, 0, (4 * half + q) * P:(4 * half + q + 1) * P],
                                   half, (o_rows, o_r[0]))
                    o = slice(half * T, (half + 1) * T)
                    hi = AC.run(lambda e, o=o, half=half: e.activation(xeT_hi[:, 0, o], bank[half][:, :], ACT.Copy), t)
                    lo = VE.run(lambda e, o=o, half=half: e.tensor_tensor(
                        xeT_lo[:, 0, o], bank[half][:, :], xeT_hi[:, 0, o].bitcast(F32), ALU.subtract), hi)

                def weights(name, x, q):
                    o_w[0] += 16
                    PO.issue(lambda e: e.indirect_dma_start(
                        o_raw[:, :], None, io[name + "_rows"], bass.IndirectOffsetOnAxis(ap=widx[:, x, q:q + 1], axis=0),
                        bounds_check=NE * P * 4 - 1, oob_is_err=False).then_inc(o_weight, 16), VE.here())
                    hi = AC.run(lambda e: e.activation(o_hi[:, :], o_raw[:, :], ACT.Copy), (o_weight, o_w[0]), PE.here())
                    PE.wait(VE.run(lambda e: e.tensor_tensor(o_lo[:, :], o_raw[:, :], o_hi[:, :].bitcast(F32),
                                                             ALU.subtract), hi))

                if x == 0:
                    o_clear = PO.run(lambda e: e.memset(o_raw[:, :], 0.0))
                    VE.wait(o_clear)
                    PO.wait(o_clear)
                PE.wait(lo)
                for m, name in enumerate(("moe1", "moe3")):
                    for q in range(4):
                        weights(name, x, q)
                        for kk in range(2):
                            k = 2 * q + kk
                            t = PE.run(mm3(bank[2 + m][:, :], xeT_hi[:, 0, k * P:(k + 1) * P],
                                           xeT_lo[:, 0, k * P:(k + 1) * P], o_hi[:, kk * FE:(kk + 1) * FE],
                                           o_lo[:, kk * FE:(kk + 1) * FE], k == 0, k == DT - 1))
                t = AC.run(lambda e: e.activation(sil[:, 0, :], bank[2][:, :], ACT.Silu), t)
                t = VE.run(lambda e: e.tensor_tensor(hd[:, 0, :], sil[:, 0, :], bank[3][:, :], ALU.mult), t)
                t = transpose4(lambda q: hd[:, 0, q * P:(q + 1) * P], 4, t)
                t = AC.run(lambda e: e.activation(hT_hi[:, 0, :], bank[4][:, :], ACT.Copy), t)
                t = VE.run(lambda e: e.tensor_tensor(hT_lo[:, 0, :], bank[4][:, :], hT_hi[:, 0, :].bitcast(F32),
                                                     ALU.subtract), t)
                PE.wait(t)
                for q in range(FET):
                    weights("moe2", x, q)
                    for half in range(2):
                        t = PE.run(mm3(bank[5 + half][:, :], hT_hi[:, 0, q * P:(q + 1) * P],
                                       hT_lo[:, 0, q * P:(q + 1) * P], o_hi[:, half * T:(half + 1) * T],
                                       o_lo[:, half * T:(half + 1) * T], q == 0, q == FET - 1))
                t = VE.run(lambda e: e.tensor_copy(ye[:, 0, 0:T], bank[5][:, :]), t,
                           (o_store, o_s[0]) if o_s[0] else None)
                t = VE.run(lambda e: e.tensor_copy(ye[:, 0, T:D], bank[6][:, :]), t)
                o_s[0] += 16
                PO.issue(lambda e, n=n: e.indirect_dma_start(
                    ys_dram, bass.IndirectOffsetOnAxis(ap=sidx[:, n:n + 1], axis=0), ye[:, 0, :], None,
                    bounds_check=2 * T - 1, oob_is_err=False).then_inc(o_store, 16), t)
            ends = [q.here() for q in (PE, AC, VE, PO)] + [(o_store, o_s[0])]
            for q, done_, s_, seen_ in saved:
                q.wait(*ends)
                q.sem, q.done, q.seen = s_, done_, seen_
            branch.close()

            over = PO.run(lambda e: e.memset(sm[:, 29, 0:1], 0.0), *outer)
            for n in range(2 * TT):
                tt, k = n // 2, n % 2
                AC.issue(lambda e: e.dma_start(ysl[:, n, :], ys_dram[k * T + tt * P:k * T + (tt + 1) * P, :])
                         .then_inc(s_ys[tt], 16), over)

            def second_sum(tt):
                x, y1, y2 = x_tok[:, tt, :], ysl[:, 2 * tt, :], ysl[:, 2 * tt + 1, :]
                gate1, gate2 = (sm[:, 11 + k, tt:tt + 1] for k in range(2))
                if tt % 2 == 0:
                    t = VE.run(lambda e: e.scalar_tensor_tensor(x, y1, gate1, x, ALU.mult, ALU.add),
                               alpha_ok, (s_ys[tt], 32), gates_ok)
                else:
                    t = AC.run(lambda e: e.activation(y1, y1, ACT.Copy, scale=gate1), (s_ys[tt], 32), gates_ok)
                    t = PO.run(lambda e: e.tensor_tensor(x, x, y1, ALU.add), t)
                return VE.run(lambda e: e.scalar_tensor_tensor(x, y2, gate2, x, ALU.mult, ALU.add), t, (s_ys[tt], 32))

            last_tok = layer_norm(second_sum)

            FREE = {}
            stat = {"bank_free": bank_free[7]}
            xg_ok = [None] * DT
            rs_state = {}

            def finish(j, x_ok, gain):
                s = j % 2
                if gain is not None:
                    t = VE.run(lambda e: e.tensor_scalar(tmp[:, 4 + s, :], xT[:, j, :], gain, None, ALU.mult),
                               x_ok, FREE.get(("xg", s)))
                    hi = AC.run(lambda e: e.activation(xg_hi[:, j, :], xT[:, j, :], ACT.Copy, scale=gain), x_ok)
                    xg_ok[j] = VE.run(lambda e: e.tensor_tensor(xg_lo[:, j, :], tmp[:, 4 + s, :],
                                                                xg_hi[:, j, :].bitcast(F32), ALU.subtract), hi, t)
                    FREE["xg", s] = xg_ok[j]
                if j == 0:
                    sq = AC.run(lambda e: e.activation(rsq[:, :], xT[:, j, :], ACT.Square), x_ok, PO.here())
                else:
                    sq = AC.run(lambda e: e.activation(tmp[:, 6 + s, :], xT[:, j, :], ACT.Square),
                                x_ok, FREE.get(("sq", s)))
                if j > 0:
                    acc = PO.run(lambda e: e.tensor_tensor(rsq[:, :], rsq[:, :], tmp[:, 6 + s, :], ALU.add),
                                 sq, rs_state["acc"])
                    FREE["sq", s] = acc
                    rs_state["acc"] = acc
                else:
                    rs_state["acc"] = sq
                if j < DT - 1:
                    return

                def add():
                    t = PE.run(lambda e: e.matmul(bank[7][:, :], ones[:, :], rsq[:, :], start=True, stop=True),
                               acc, stat["bank_free"])
                    t = VE.run(lambda e: e.tensor_scalar(rsq[:, :], bank[7][:, :], 1.0 / D, RMS_EPS,
                                                         ALU.mult, ALU.add), t)
                    stat["bank_free"] = t
                    t = AC.run(lambda e: e.activation(rsq[:, :], rsq[:, :], ACT.Sqrt), t)
                    rs_state["ok"] = VE.run(lambda e: e.reciprocal(rsq[:, :], rsq[:, :]), t)
                later.append(add)

            for j in range(DT):
                b = get_bank()
                for tt in range(TT):
                    PE.wait(last_tok[tt])
                    f = lambda e: e.transpose(bank[b][:, tt * P:(tt + 1) * P], x_tok[:, tt, j * P:(j + 1) * P], ident)
                    if tt < TT - 1:
                        PE.issue(f)
                t = PE.run(f)
                x_ok = AC.run(lambda e: e.activation(xT[:, j, :], bank[b][:, :], ACT.Identity,
                                                     scale=par("ln_g", DT + j), bias=par("ln_b", DT + j)), t, *last_tok)
                bank_free[b] = x_ok
                run_later()
                finish(j, x_ok, par("g_ffn1", j))
            tok_gone = t

            def product(b, tiles, rhs_hi, rhs_lo, oks):
                for n, (a_hi, a_lo, k, start, stop) in enumerate(tiles):
                    PE.wait(oks(k))
                    f = mm3(bank[b][:, :], a_hi, a_lo, rhs_hi(k), rhs_lo(k), start, stop)
                    if n < len(tiles) - 1:
                        PE.issue(f)
                return PE.run(f)

            def from_xg(src):
                c, hi, lo = take("dense", (0, src, W))
                b = get_bank()
                t = product(b, [(hi[:, k * P:(k + 1) * P], lo[:, k * P:(k + 1) * P], k, k == 0, k == DT - 1)
                                for k in range(DT)], lambda k: xg_hi[:, k, :], lambda k: xg_lo[:, k, :],
                            lambda k: xg_ok[k])
                release(c, t)
                run_later()
                return b, t

            def split_to(g, src_ap, ok, *more):
                hi = AC.run(lambda e: e.activation(g_hi[:, g, :], src_ap, ACT.Copy), ok, *more)
                return VE.run(lambda e: e.tensor_tensor(g_lo[:, g, :], src_ap, g_hi[:, g, :].bitcast(F32),
                                                        ALU.subtract), hi, ok, *more)

            def residual(j, b, t, coef, gain):
                x_ok = VE.run(lambda e: e.scalar_tensor_tensor(xT[:, j, :], bank[b][:, :], coef, xT[:, j, :],
                                                               ALU.mult, ALU.add), t)
                bank_free[b] = x_ok
                finish(j, x_ok, gain)

            def swiglu(l, names, gain):
                g_ok = [None] * FFT
                for j in range(FFT):
                    s = j % 2
                    b1, t1 = from_xg(io[names[0]][l, j])
                    b3, t3 = from_xg(io[names[1]][l, j])
                    u = VE.run(lambda e: e.tensor_tensor(tmp[:, s, :], bank[b1][:, :], rsq[:, :], ALU.mult),
                               t1, rs_state["ok"], FREE.get(("u", s)), tok_gone)
                    bank_free[b1] = u
                    u = AC.run(lambda e: e.activation(tmp[:, s, :], tmp[:, s, :], ACT.Silu), u)
                    v = VE.run(lambda e: e.tensor_tensor(tmp[:, 2 + s, :], bank[b3][:, :], rsq[:, :], ALU.mult), t3,
                               FREE.get(("v", s)))
                    bank_free[b3] = v
                    m = PO.run(lambda e: e.tensor_tensor(tmp[:, 2 + s, :], tmp[:, 2 + s, :], tmp[:, s, :], ALU.mult),
                               u, v)
                    FREE["u", s] = m
                    g_ok[j] = split_to(j, tmp[:, 2 + s, :], m)
                    FREE["v", s] = g_ok[j]
                for j in range(DT):
                    b = get_bank()
                    for q in range(3):
                        k0, k1 = 8 * q, min(8 * q + 8, FFT)
                        c, hi, lo = take("dense", (0, io[names[2]][l, j][:, k0 * P:k1 * P], (k1 - k0) * P))
                        t = product(b, [(hi[:, (k - k0) * P:(k - k0 + 1) * P], lo[:, (k - k0) * P:(k - k0 + 1) * P], k,
                                         k == 0, k == FFT - 1) for k in range(k0, k1)],
                                    lambda k: g_hi[:, k, :], lambda k: g_lo[:, k, :], lambda k: g_ok[k])
                        release(c, t)
                    run_later()
                    residual(j, b, t, 0.5, gain(j))

            PAIR_F, PAIR_A, PAIR_M, PAIR_C, PAIR_P = 0, 4, 4, 12, 16

            def mixers(l, gain):
                def column(i):
                    return from_xg(io["w_in"][l, i])

                ok = {}
                for i in range(4):
                    b, t = column(IN_F + i)
                    s = i % 2
                    u = VE.run(lambda e: e.tensor_tensor(tmp[:, s, :], bank[b][:, :], rsq[:, :], ALU.mult),
                               t, rs_state["ok"], FREE.get(("u", s)))
                    bank_free[b] = u
                    ok["u", i] = FREE["u", s] = split_to(PAIR_F + i, tmp[:, s, :], u)

                def conv_branch(i):
                    s = i % 2
                    b, t = column(IN_C + i)
                    cg = VE.run(lambda e: e.tensor_tensor(tmp[:, s, :], bank[b][:, :], rsq[:, :], ALU.mult),
                                t, rs_state["ok"], FREE.get(("u", s)))
                    bank_free[b] = cg
                    b2, t = column(IN_V + i)
                    v = VE.run(lambda e: e.tensor_tensor(tmp[:, 2 + s, :], bank[b2][:, :], rsq[:, :], ALU.mult), t,
                               FREE.get(("v", s)))
                    bank_free[b2] = v
                    z = zc[:, s, :]
                    PO.run(lambda e: e.memset(z[:, 0:1], 0.0), FREE.get(("z", s)))
                    pad = PO.run(lambda e: e.memset(z[:, T + 1:T + 2], 0.0), FREE.get(("z", s)))
                    t = PO.run(lambda e: e.tensor_tensor(z[:, 1:T + 1], tmp[:, s, :], tmp[:, 2 + s, :], ALU.mult),
                               cg, v, pad)
                    w = lambda k: par("w_conv", (l * 3 + k) * 4 + i)
                    t = VE.run(lambda e: e.tensor_scalar(tmp[:, s, :], z[:, 0:T], w(0), None, ALU.mult), t)
                    for k in (1, 2):
                        t = VE.run(lambda e, k=k: e.scalar_tensor_tensor(tmp[:, s, :], z[:, k:k + T], w(k), tmp[:, s, :],
                                                                         ALU.mult, ALU.add), t)
                    FREE["z", s] = t
                    cv = PO.run(lambda e: e.tensor_tensor(tmp[:, s, :], tmp[:, s, :], rsq[:, :], ALU.mult), t)
                    b3, t = column(IN_B + i)
                    m = VE.run(lambda e: e.tensor_tensor(tmp[:, s, :], tmp[:, s, :], bank[b3][:, :], ALU.mult), t, cv)
                    bank_free[b3] = m
                    ok["c", i] = split_to(PAIR_C + i, tmp[:, s, :], m)
                    FREE["u", s] = FREE["v", s] = ok["c", i]

                def token_spectra():
                    c, hi, lo = take("dense", (0, io["dft_c"], 2 * P))
                    for g in range(4):
                        for tt in range(TT):
                            if tt % 2 == 0:
                                b = get_bank()
                            f = mm3(bank[b][:, (tt % 2) * 256:(tt % 2) * 256 + 256],
                                    g_hi[:, PAIR_F + g, tt * P:(tt + 1) * P], g_lo[:, PAIR_F + g, tt * P:(tt + 1) * P],
                                    hi[:, 0:256], lo[:, 0:256], True, True)
                            PE.wait(ok["u", g])
                            t = PE.run(f)
                            if tt % 2 == 1:
                                pr = PAIR_A + 2 * g + tt // 2
                                hi_t = AC.run(lambda e, pr=pr, b=b: e.activation(g_hi[:, pr, :], bank[b][:, :], ACT.Copy), t)
                                ok["a", g, tt // 2] = VE.run(lambda e, pr=pr, b=b: e.tensor_tensor(
                                    g_lo[:, pr, :], bank[b][:, :], g_hi[:, pr, :].bitcast(F32), ALU.subtract), hi_t)
                                bank_free[b] = ok["a", g, tt // 2]
                    release(c, t)
                    ok["u_read"] = t

                def time_spectra():
                    H = T // 2
                    bs = [get_bank() for _ in range(4)]
                    for n, (col, kts) in enumerate(DFT_CHUNKS):
                        width = sum(w for _, w, _ in kts)
                        c, hi, lo = take("dense", (0, io["dft_s"][:, col:col + width], width))
                        for g in range(4):
                            at = 0
                            for m, (kt, w, base) in enumerate(kts):
                                pr = PAIR_A + 2 * g + kt // 2
                                PE.wait(ok["a", g, kt // 2])
                                o = (kt % 2) * 256 + (P if base else 0)
                                f = mm3(bank[bs[g]][:, base:base + w], g_hi[:, pr, o:o + P], g_lo[:, pr, o:o + P],
                                        hi[:, at:at + w], lo[:, at:at + w], n == 0 and m == 0,
                                        n == len(DFT_CHUNKS) - 1 and m == len(kts) - 1)
                                t = PE.run(f)
                                at += w
                            if n == len(DFT_CHUNKS) - 1:
                                done = t
                                b, q = bs[g], g % 2
                                pq, fo = tmp[:, q, :], tmp[:, 2 + q, :]
                                e0 = AC.run(lambda e: e.activation(pq, bank[b][:, :], ACT.Copy), done, FREE.get(("u", q)))
                                bank_free[b] = e0
                                VE.wait(FREE.get(("v", q)))
                                VE.run(lambda e: e.tensor_copy(fo[:, 0:H + 1:H], pq[:, 0:H + 1:H]), e0)
                                VE.run(lambda e: e.tensor_tensor(fo[:, 1:H], pq[:, 1:H], pq[:, H + 1:T],
                                                                 ALU.subtract), e0)
                                e1 = VE.run(lambda e: e.tensor_tensor(fo[:, T - 1:H:-1], pq[:, 1:H], pq[:, H + 1:T],
                                                                      ALU.add), e0)
                                FREE["u", q] = e1
                                ok["f", g] = FREE["v", q] = split_to(PAIR_F + g, fo, e1, ok["u_read"])
                        release(c, t)
                    ok["a_read"] = t

                def pool_branch(i):
                    s = i % 2
                    w, half = 2 << i, 1 << i
                    z = zc[:, s, :]
                    b, t = column(IN_P + i)
                    u0 = VE.run(lambda e: e.tensor_tensor(tmp[:, s, :], bank[b][:, :], rsq[:, :], ALU.mult), t,
                                FREE.get(("u", s)), rs_state["ok"])
                    bank_free[b] = u0
                    PO.run(lambda e: e.memset(z[:, 0:half], 0.0), FREE.get(("z", s)))
                    pad = PO.run(lambda e: e.memset(z[:, half + T:T + w], 0.0), FREE.get(("z", s)))
                    t = AC.run(lambda e: e.activation(z[:, half:half + T], tmp[:, s, :], ACT.Copy), u0,
                               FREE.get(("z", s)))
                    VE.wait(pad, FREE.get(("v", s)))
                    n = 1
                    while n < w:
                        width = T + w - 2 * n
                        dst = tmp[:, 2 + s, 0:width] if 2 * n == w else z[:, 0:width]
                        t = VE.run(lambda e: e.tensor_tensor(dst, z[:, 0:width], z[:, n:n + width], ALU.add), t)
                        n *= 2
                    FREE["z", s] = t
                    m = tmp[:, 2 + s, :]
                    t = VE.run(lambda e: e.tensor_scalar(m, m, 1.0 / w, None, ALU.mult), t)
                    edge = consts[:, C_EDGE + 2 * half:C_EDGE + 4 * half]
                    t = VE.run(lambda e: e.tensor_tensor(m[:, 0:half], m[:, 0:half], edge[:, 0:half], ALU.mult), t)
                    t = VE.run(lambda e: e.tensor_tensor(m[:, T - half:T], m[:, T - half:T], edge[:, half:2 * half],
                                                         ALU.mult), t)
                    t = VE.run(lambda e: e.tensor_tensor(m, m, tmp[:, s, :], ALU.subtract), t)
                    FREE["u", s] = t
                    ok["p", i] = FREE["v", s] = split_to(PAIR_P + i, m, t)

                conv_branch(0)
                token_spectra()
                pool_branch(0)
                pool_branch(1)
                conv_branch(1)
                conv_branch(2)
                time_spectra()
                pool_branch(2)
                pool_branch(3)
                conv_branch(3)

                for j in range(DT):
                    s = j % 2
                    c, hi, lo = take("dense", (0, io["mix_small"][l, j], 6 * P))
                    g = j // 2
                    outs = []
                    for kind in range(3):
                        b = get_bank()
                        if kind == 0:
                            tiles = [(hi[:, 0:P], lo[:, 0:P], PAIR_F + g, True, True)]
                            oks = lambda k: ok["f", k - PAIR_F]
                        elif kind == 2:
                            tiles = [(hi[:, P:2 * P], lo[:, P:2 * P], PAIR_P + g, True, True)]
                            oks = lambda k: ok["p", k - PAIR_P]
                        else:
                            tiles = [(hi[:, (2 + i) * P:(3 + i) * P], lo[:, (2 + i) * P:(3 + i) * P], PAIR_C + i,
                                      i == 0, i == 3) for i in range(4)]
                            oks = lambda k: ok["c", k - PAIR_C]
                        t = product(b, tiles, lambda k: g_hi[:, k, :], lambda k: g_lo[:, k, :], oks)
                        outs.append((b, t))
                    release(c, t)
                    acc = None
                    for kind in range(3):
                        b, t = column(IN_G + kind * DT + j)
                        q = (3 * j + kind) % 2
                        m = VE.run(lambda e: e.tensor_tensor(tmp[:, q, :], bank[b][:, :], rsq[:, :], ALU.mult), t,
                                   FREE.get(("u", q)))
                        bank_free[b] = m
                        m = AC.run(lambda e: e.activation(tmp[:, q, :], tmp[:, q, :], ACT.Sigmoid), m)
                        by, ty = outs[kind]
                        dst = tmp[:, 2 + s, :] if kind == 0 else tmp[:, q, :]
                        free = FREE.get(("v", s)) if kind == 0 else None
                        if kind == 2:
                            m = VE.run(lambda e: e.scalar_tensor_tensor(dst, bank[by][:, :], par("pool_scale", l * DT + j),
                                                                        tmp[:, q, :], ALU.mult, ALU.mult), m, ty)
                        else:
                            m = VE.run(lambda e: e.tensor_tensor(dst, bank[by][:, :], tmp[:, q, :], ALU.mult), m, ty, free)
                        bank_free[by] = m
                        if kind == 0:
                            acc = m
                        else:
                            acc = PO.run(lambda e: e.tensor_tensor(tmp[:, 2 + s, :], tmp[:, 2 + s, :], tmp[:, q, :],
                                                                   ALU.add), m, acc)
                        FREE["u", q] = acc
                    ok["m", j] = FREE["v", s] = split_to(PAIR_M + j, tmp[:, 2 + s, :], acc, ok["a_read"])
                for j in range(DT):
                    c, hi, lo = take("dense", (0, io["w_o"][l, j], W))
                    b = get_bank()
                    t = product(b, [(hi[:, k * P:(k + 1) * P], lo[:, k * P:(k + 1) * P], k, k == 0, k == DT - 1)
                                    for k in range(DT)], lambda k: g_hi[:, PAIR_M + k, :],
                                lambda k: g_lo[:, PAIR_M + k, :], lambda k: ok["m", k])
                    release(c, t)
                    run_later()
                    residual(j, b, t, 1.0, gain(j))

            for l in range(LAYERS):
                swiglu(l, ("w1_a", "w3_a", "w2_a"), lambda j, l=l: par("g_mix", l * DT + j))
                mixers(l, lambda j, l=l: par("g_ffn2", l * DT + j))
                swiglu(l, ("w1_b", "w3_b", "w2_b"),
                       lambda j, l=l: par("g_ffn1", (l + 1) * DT + j) if l + 1 < LAYERS else None)
            run_later()
            for j in range(DT):
                t = VE.run(lambda e, j=j: e.scalar_tensor_tensor(xT[:, j, :], xT[:, j, :], par("g_final", j),
                                                                 rsq[:, :], ALU.mult, ALU.mult), rs_state["ok"])
                SP.issue(lambda e, j=j: e.dma_start(io["out"][:, j, :], xT[:, j, :]).then_inc(s_out, 16), t)
            SP.wait((s_out, 16 * DT))
            return chunks

        chunks = program(None)
        block = ctx.enter_context(nc.Block())

        @block.sync
        def _(eng):
            program(chunks, "sp", eng)

        @block.scalar
        def _(eng):
            program(chunks, "act", eng)

        @block.vector
        def _(eng):
            program(chunks, "dve", eng)

        @block.gpsimd
        def _(eng):
            program(chunks, "pool", eng)

        @block.tensor
        def _(eng):
            program(chunks, "pe", eng)


POOL_EVERY = 10 ** 9


def dram_views(args):
    io = dict(args)
    for n in ("moe1", "moe3", "moe2"):
        io[n] = args[n].rearrange("(e p c) n -> e c p n", p=P, c=4)
        io[n + "_rows"] = args[n]
    return io


def lay_out(inp):
    import numpy as np

    def tiles(w):
        *lead, K, N = w.shape
        n = len(lead)
        w = w.reshape(*lead, K // P, P, N // P, P)
        w = w.transpose(*range(n), n + 2, n + 1, n, n + 3)
        return np.ascontiguousarray(w).reshape(*lead, N // P, P, K)

    def columns(v):
        return np.ascontiguousarray(v.reshape(-1, P).T)

    f = {k: np.asarray(v) for k, v in inp.items()}
    a = {}
    x = f["x"][0]
    a["x"] = np.ascontiguousarray(x.reshape(TT, P, D).transpose(1, 0, 2))
    a["xT"] = np.ascontiguousarray(x.T.reshape(DT, P, T).transpose(1, 0, 2))
    w_in = tiles(f["rec_w_in"][0])
    a["rec_in"] = np.concatenate([w_in[RT:], w_in[:RT]])
    a["rec_out"] = f["rec_w_out"][0].reshape(RT, P, D)
    bd = np.zeros((2, R, R), np.float32)
    for m, name in enumerate(("rec_w_r", "rec_w_i")):
        for n in range(LRU_BLOCKS):
            s = slice(n * LRU_W, (n + 1) * LRU_W)
            bd[m, s, s] = f[name][0, n]
    a["bd"] = np.stack([bd[m, i * P:(i + 1) * P, j * P:(j + 1) * P] for m in range(2) for i, j in BD_PAIRS], axis=1)
    groups = {"conv_w": f["rec_conv_w"][0], "conv_b": f["rec_conv_b"], "b_r": f["rec_b_r"], "b_i": f["rec_b_i"],
              "lam": f["rec_lambda"], "g_ffn1": f["g_ffn1_2"], "g_mix": f["g_mix_2"], "g_ffn2": f["g_ffn2_2"],
              "pool_scale": f["pool_scale_2"], "g_final": f["g_final_2"], "w_conv": f["w_conv_2"],
              "ln_g": f["ln_g"], "ln_b": f["ln_b"]}
    a["params"] = np.concatenate([columns(groups[n]) for n, _ in PARAM_GROUPS], axis=1)
    a["ln"] = np.stack([f["ln_g"][0, 0], f["ln_b"][0, 0]])
    a["wr"] = np.concatenate([f["moe_w_group"][0], f["moe_w_expert"][0]], axis=1) \
        .reshape(DT, P, NG + NE).transpose(1, 0, 2).copy()
    a["br"] = np.concatenate([f["moe_b_group"], f["moe_b_expert"]], axis=1).reshape(NG + NE, 1)
    for name, src, kt in (("moe1", "moe_w1", DT), ("moe3", "moe_w3", DT), ("moe2", "moe_w2", FET)):
        w = f[src][0]
        a[name] = np.ascontiguousarray(w.reshape(NE, kt, P, -1).transpose(0, 2, 1, 3)).reshape(NE * P * 4, W)
    for s in ("a", "b"):
        for w in ("w1", "w3", "w2"):
            a[f"{w}_{s}"] = tiles(f[f"{w}_{s}_2"])
    a["w_in"] = tiles(f["w_in_2"])
    a["w_o"] = tiles(f["w_o_2"])
    wf, wp = ([f[n][:, j // 2, :, (j % 2) * P:(j % 2 + 1) * P] for j in range(DT)]
              for n in ("w_fourier_2", "w_pool_2"))
    small = [np.concatenate([wf[j], wp[j], tiles(f["w_conv_out_2"])[:, j]], axis=2) for j in range(DT)]
    a["mix_small"] = np.stack(small, axis=1)

    c = np.zeros((P, NCONST), np.float32)
    c[:, C_IDENT:C_IDENT + P] = np.eye(P)
    c[:, C_UPPER:C_UPPER + P] = np.triu(np.ones((P, P)), 1)
    c[:, C_IOTA:C_IOTA + P] = np.arange(P)
    c[:, C_GRANK:C_GRANK + TT * NG] = np.tile(NG - np.arange(NG), TT)
    c[:, C_ERANK:C_ERANK + TT * NE] = np.tile(NE - np.arange(NE), TT)
    c[:, C_EPAIR:C_EPAIR + TT * NE] = np.tile(np.arange(NE) // 2, TT)
    c[:, C_EROW:C_EROW + TT * NE] = np.tile(FIRST * (np.arange(NE) % 2), TT)
    for k in range(2):
        for tt in range(TT):
            c[:, C_SLOT + k * TT + tt] = k * T + tt * P + np.arange(P) + 1
    c[:, C_ROW4] = 4 * np.arange(P)
    for half in (1, 2, 4, 8):
        times = np.concatenate([np.arange(half), np.arange(T - half, T)])
        terms = np.minimum(times + half, T) - np.maximum(times - half, 0)
        c[:, C_EDGE + 2 * half:C_EDGE + 4 * half] = 2 * half / terms
    a["consts"] = c
    ang = 2 * np.pi / P * np.outer(np.arange(P), np.arange(P))
    a["dft_c"] = (np.concatenate([np.cos(ang), np.sin(ang)], axis=1) / 256.0).astype(np.float32)
    ang = 2 * np.pi / T * (np.outer(np.arange(T), np.arange(T)) % T)
    cos, sin = np.cos(ang[:, :T // 2 + 1]), np.sin(ang[:, :T // 2])
    parts = []
    for _, kts in DFT_CHUNKS:
        for kt, w, base in kts:
            part = np.zeros((P, w))
            src = sin if base else cos
            part[:, :src.shape[1]] = src[kt * P:(kt + 1) * P]
            parts.append(part)
    a["dft_s"] = np.concatenate(parts, axis=1).astype(np.float32)
    return a


def kernel(**inputs):
    import numpy as np
    import concourse.bacc as bacc
    from concourse.bass_utils import run_bass_kernel_spmd

    nc = bacc.Bacc("TRN2", target_bir_lowering=False, num_devices=1)
    arrays, args = {}, {}
    for name, a in lay_out(inputs).items():
        arrays[f"in_{name}"] = a
        args[name] = nc.dram_tensor(f"in_{name}", a.shape, mybir.dt.from_np(a.dtype), kind="ExternalInput").ap()
    args["out"] = nc.dram_tensor("out_0", (P, DT, T), F32, kind="ExternalOutput").ap()
    build(nc, dram_views(args))
    r = run_bass_kernel_spmd(nc, [arrays], core_ids=[0])
    got = r.results[0]["out_0"]
    return got.transpose(2, 1, 0).reshape(1, T, D)
```
